# Optimizing a Trainium2 kernel written in Bass

```python
import jax, jax.numpy as jnp
from jax import lax
import numpy as np

D_MODEL = 1024
BATCH = 1
SEQ = 512
DEPTH = 2
DEC_BATCH = 8
DEC_SEQ = 4
PAST_LEN = 4096
PAGE_SIZE = 128

N_MIXERS = 2
N_GDN = (DEPTH + 1) // 2
N_RWKV = DEPTH // 2
GDN_HEADS = 8
GDN_HEAD_DIM = 128
GDN_QK = GDN_HEADS * GDN_HEAD_DIM
GDN_V = GDN_HEADS * GDN_HEAD_DIM
GDN_CONV_DIM = 2 * GDN_QK + GDN_V
GDN_IN = GDN_CONV_DIM + GDN_V + 2 * GDN_HEADS
GDN_CONV = 4
GDN_CHUNK = 64
RWKV_HEAD = 64
RWKV_HEADS = D_MODEL // RWKV_HEAD
D_DECAY_LORA = 64
D_AAA_LORA = 64
D_MV_LORA = 32
D_GATE_LORA = 128
D_FF = 2816
N_NORMS = 6
NORM_EPS = 1e-6
L2_EPS = 1e-6
GN_EPS = 64e-5

kernel_name = 'hybrid_gdn_rwkv7_macaron_step'

def rms_norm(x, g):
    xf = x.astype(jnp.float32)
    y = xf * lax.rsqrt(jnp.mean(xf * xf, axis=-1, keepdims=True) + NORM_EPS)
    return (y * g.astype(jnp.float32)).astype(x.dtype)

def l2_normalize(x):
    xf = x.astype(jnp.float32)
    return xf * lax.rsqrt(jnp.sum(xf * xf, axis=-1, keepdims=True) + L2_EPS)

def swiglu(x, w_in, w_out):
    gate, up = jnp.split(x @ w_in, 2, axis=-1)
    return (jax.nn.silu(gate) * up) @ w_out

def causal_dwconv(x_ext, w):
    return lax.conv_general_dilated(
        x_ext, w[:, None, :].astype(x_ext.dtype), window_strides=(1,), padding='VALID',
        dimension_numbers=('NWC', 'WIO', 'NWC'), feature_group_count=x_ext.shape[-1])

def chunk_gated_delta(q, k, v, g, beta, s0):
    B, T, H, dk = q.shape
    dv = v.shape[-1]
    C = min(GDN_CHUNK, T)
    pad = (-T) % C
    n = (T + pad) // C

    def prep(t):
        t = jnp.moveaxis(t.astype(jnp.float32), 1, 2)
        t = jnp.pad(t, [(0, 0), (0, 0), (0, pad)] + [(0, 0)] * (t.ndim - 3))
        return t.reshape(B, H, n, C, *t.shape[3:])

    q = prep(l2_normalize(q) * dk ** -0.5)
    k = prep(l2_normalize(k))
    v = prep(v)
    beta = prep(beta)
    g = jnp.cumsum(prep(g), axis=-1)
    idx = jnp.arange(C)
    incl = idx[:, None] >= idx[None, :]
    strict = idx[:, None] > idx[None, :]
    decay = jnp.exp(jnp.where(incl, g[..., :, None] - g[..., None, :], -jnp.inf))
    kb = k * beta[..., None]
    a_mat = jnp.where(strict, jnp.einsum('bhncd,bhnsd->bhncs', kb, k) * decay, 0.0) + jnp.eye(C, dtype=jnp.float32)
    rhs = jnp.concatenate([v * beta[..., None], kb * jnp.exp(g)[..., None]], axis=-1)
    sol = lax.linalg.triangular_solve(a_mat, rhs, left_side=True, lower=True, unit_diagonal=True)
    u, w = sol[..., :dv], sol[..., dv:]
    attn = jnp.where(incl, jnp.einsum('bhncd,bhnsd->bhncs', q, k) * decay, 0.0)
    q_dec = q * jnp.exp(g)[..., None]
    k_dec = k * jnp.exp(g[..., -1:] - g)[..., None]
    g_tot = jnp.exp(g[..., -1])
    xs = tuple(jnp.moveaxis(t, 2, 0) for t in (u, w, q_dec, k_dec, attn, g_tot))

    def step(S, inp):
        u_c, w_c, q_c, k_c, attn_c, gt = inp
        v_new = u_c - jnp.einsum('bhcd,bhde->bhce', w_c, S)
        o = jnp.einsum('bhcd,bhde->bhce', q_c, S) + jnp.einsum('bhcs,bhse->bhce', attn_c, v_new)
        S = S * gt[..., None, None] + jnp.einsum('bhcd,bhce->bhde', k_c, v_new)
        return S, o

    S, o = lax.scan(step, s0.astype(jnp.float32), xs)
    o = jnp.moveaxis(o, 0, 2).reshape(B, H, n * C, dv)[:, :, :T]
    return jnp.moveaxis(o, 1, 2), S

def gdn_mixer(x, conv_buf, s0, w_in, conv_w, a_log, dt_bias, o_norm, w_out):
    B, T, _ = x.shape
    proj = x @ w_in
    qkv, z, b, a = jnp.split(proj, [GDN_CONV_DIM, GDN_CONV_DIM + GDN_V, GDN_CONV_DIM + GDN_V + GDN_HEADS], axis=-1)
    qkv_ext = jnp.concatenate([conv_buf.astype(qkv.dtype), qkv], axis=1)
    new_buf = qkv_ext[:, T:]
    qkv = jax.nn.silu(causal_dwconv(qkv_ext, conv_w))
    q, k, v = jnp.split(qkv, [GDN_QK, 2 * GDN_QK], axis=-1)
    shp = (B, T, GDN_HEADS, GDN_HEAD_DIM)
    beta = jax.nn.sigmoid(b.astype(jnp.float32))
    g = -jnp.exp(a_log.astype(jnp.float32)) * jax.nn.softplus(a.astype(jnp.float32) + dt_bias.astype(jnp.float32))
    o, s = chunk_gated_delta(q.reshape(shp), k.reshape(shp), v.reshape(shp), g, beta, s0)
    o = rms_norm(o, o_norm) * jax.nn.silu(z.reshape(shp).astype(jnp.float32))
    y = o.reshape(B, T, GDN_V).astype(x.dtype) @ w_out
    return y, new_buf, s.astype(s0.dtype)

def rwkv7_recurrence(r, decay, k, v, a, b, s0):
    xs = tuple(jnp.moveaxis(t.astype(jnp.float32), 1, 0) for t in (r, decay, k, v, a, b))

    def step(S, inp):
        r_t, w_t, k_t, v_t, a_t, b_t = inp
        sa = jnp.einsum('bhij,bhj->bhi', S, a_t)
        S = S * w_t[:, :, None, :] + sa[..., None] * b_t[:, :, None, :] + v_t[..., None] * k_t[:, :, None, :]
        return S, jnp.einsum('bhij,bhj->bhi', S, r_t)

    S, y = lax.scan(step, s0.astype(jnp.float32), xs)
    return jnp.moveaxis(y, 0, 1), S

def rwkv_mixer(x, shift_prev, s0, v_first, lerp, w_rkv, w0, w1, w2, a0, a1, a2, vres,
               g1, g2, k_k, k_a, r_k, ln_w, ln_b, w_o):
    B, T, D = x.shape
    x_prev = jnp.concatenate([shift_prev[:, None].astype(x.dtype), x[:, :-1]], axis=1)
    xs = x[:, :, None] + (x_prev - x)[:, :, None] * lerp
    rkv = jnp.einsum('btsd,sde->btse', xs[:, :, :3], w_rkv)
    r, k, v = rkv[:, :, 0], rkv[:, :, 1], rkv[:, :, 2]
    xv, xw, xa, xg = xs[:, :, 2], xs[:, :, 3], xs[:, :, 4], xs[:, :, 5]
    logw = -jax.nn.softplus(-(w0 + jnp.tanh(xw @ w1) @ w2).astype(jnp.float32)) - 0.5
    if v_first is None:
        v_first = v
    else:
        v0, v1, v2 = vres
        v = v + (v_first - v) * jax.nn.sigmoid(v0 + (xv @ v1) @ v2)
    a = jax.nn.sigmoid((a0 + (xa @ a1) @ a2).astype(jnp.float32))
    g = jax.nn.sigmoid(xg @ g1) @ g2

    def heads(t):
        return t.reshape(B, T, RWKV_HEADS, RWKV_HEAD)

    kk = l2_normalize(heads(k * k_k))
    k = k * (1.0 + (a - 1.0) * k_a)
    y, s = rwkv7_recurrence(heads(r), jnp.exp(-jnp.exp(heads(logw))), heads(k), heads(v), -kk, kk * heads(a), s0)
    mu = jnp.mean(y, axis=-1, keepdims=True)
    yc = y - mu
    y = yc * lax.rsqrt(jnp.mean(yc * yc, axis=-1, keepdims=True) + GN_EPS)
    y = y.reshape(B, T, D) * ln_w + ln_b
    bonus = jnp.sum(heads(r).astype(jnp.float32) * heads(k).astype(jnp.float32) * r_k.astype(jnp.float32),
                    axis=-1, keepdims=True) * heads(v).astype(jnp.float32)
    y = y + bonus.reshape(B, T, D)
    out = (y * g.astype(jnp.float32)).astype(x.dtype) @ w_o
    return out, x[:, -1], s.astype(s0.dtype), v_first

def trunk(h, gdn_s, gdn_buf, rw_s, rw_shift, p):
    out_gdn_s, out_gdn_buf, out_rw_s, out_rw_shift = [], [], [], []
    v_first = None
    for i in range(DEPTH):
        ng = p['norm_g'][i]
        h = h + 0.5 * rms_norm(swiglu(rms_norm(h, ng[0]), p['ffn_w_in'][i, 0], p['ffn_w_out'][i, 0]), ng[1])
        u = rms_norm(h, ng[2])
        j = i // N_MIXERS
        if i % N_MIXERS == 0:
            out, buf, s = gdn_mixer(u, gdn_buf[j], gdn_s[j], p['gdn_w_in'][j], p['gdn_conv_w'][j],
                                    p['gdn_a_log'][j], p['gdn_dt_bias'][j], p['gdn_o_norm'][j], p['gdn_w_out'][j])
            out_gdn_s.append(s)
            out_gdn_buf.append(buf)
        else:
            vres = None if j == 0 else (p['rwkv_v0'][j - 1], p['rwkv_v1'][j - 1], p['rwkv_v2'][j - 1])
            out, shift, s, v_first = rwkv_mixer(
                u, rw_shift[j], rw_s[j], v_first, p['rwkv_lerp'][j], p['rwkv_w_rkv'][j],
                p['rwkv_w0'][j], p['rwkv_w1'][j], p['rwkv_w2'][j], p['rwkv_a0'][j], p['rwkv_a1'][j], p['rwkv_a2'][j],
                vres, p['rwkv_g1'][j], p['rwkv_g2'][j], p['rwkv_k_k'][j], p['rwkv_k_a'][j], p['rwkv_r_k'][j],
                p['rwkv_ln_w'][j], p['rwkv_ln_b'][j], p['rwkv_w_o'][j])
            out_rw_s.append(s)
            out_rw_shift.append(shift)
        h = h + rms_norm(out, ng[3])
        h = h + 0.5 * rms_norm(swiglu(rms_norm(h, ng[4]), p['ffn_w_in'][i, 1], p['ffn_w_out'][i, 1]), ng[5])
    return h, jnp.stack(out_gdn_s), jnp.stack(out_gdn_buf), jnp.stack(out_rw_s), jnp.stack(out_rw_shift)

def setup_inputs(seed: int = 0) -> dict:
    key = jax.random.key(seed)
    ks = iter(jax.random.split(key, 48))

    def nrm(shape, scale, shift=0.0):
        return shift + scale * jax.random.normal(next(ks), shape, jnp.float32)

    D = D_MODEL
    nv = N_RWKV - 1
    return {
        'x_prompt': nrm((BATCH, SEQ, D), 1.0),
        'x_sample': nrm((DEC_BATCH, DEC_SEQ, D), 1.0),
        'state_gdn': nrm((N_GDN, DEC_BATCH, GDN_HEADS, GDN_HEAD_DIM, GDN_HEAD_DIM), 0.3),
        'state_gdn_conv': nrm((N_GDN, DEC_BATCH, GDN_CONV - 1, GDN_CONV_DIM), 1.0),
        'state_rwkv': nrm((N_RWKV, DEC_BATCH, RWKV_HEADS, RWKV_HEAD, RWKV_HEAD), 0.3),
        'state_rwkv_shift': nrm((N_RWKV, DEC_BATCH, D), 1.0),
        'norm_g': nrm((DEPTH, N_NORMS, D), 0.05, 1.0),
        'ffn_w_in': nrm((DEPTH, 2, D, 2 * D_FF), D ** -0.5),
        'ffn_w_out': nrm((DEPTH, 2, D_FF, D), D_FF ** -0.5),
        'gdn_w_in': nrm((N_GDN, D, GDN_IN), D ** -0.5),
        'gdn_conv_w': nrm((N_GDN, GDN_CONV, GDN_CONV_DIM), 0.5),
        'gdn_a_log': jnp.log(jax.random.uniform(next(ks), (N_GDN, GDN_HEADS), jnp.float32, 1.0, 16.0)),
        'gdn_dt_bias': nrm((N_GDN, GDN_HEADS), 0.1),
        'gdn_o_norm': nrm((N_GDN, GDN_HEAD_DIM), 0.05, 1.0),
        'gdn_w_out': nrm((N_GDN, GDN_V, D), GDN_V ** -0.5),
        'rwkv_lerp': jax.random.uniform(next(ks), (N_RWKV, 6, D), jnp.float32),
        'rwkv_w_rkv': nrm((N_RWKV, 3, D, D), D ** -0.5),
        'rwkv_w0': nrm((N_RWKV, D), 0.5, -1.5),
        'rwkv_w1': nrm((N_RWKV, D, D_DECAY_LORA), D ** -0.5),
        'rwkv_w2': nrm((N_RWKV, D_DECAY_LORA, D), 0.5 * D_DECAY_LORA ** -0.5),
        'rwkv_a0': nrm((N_RWKV, D), 0.1),
        'rwkv_a1': nrm((N_RWKV, D, D_AAA_LORA), D ** -0.5),
        'rwkv_a2': nrm((N_RWKV, D_AAA_LORA, D), 0.5 * D_AAA_LORA ** -0.5),
        'rwkv_v0': nrm((nv, D), 0.1),
        'rwkv_v1': nrm((nv, D, D_MV_LORA), D ** -0.5),
        'rwkv_v2': nrm((nv, D_MV_LORA, D), 0.5 * D_MV_LORA ** -0.5),
        'rwkv_g1': nrm((N_RWKV, D, D_GATE_LORA), D ** -0.5),
        'rwkv_g2': nrm((N_RWKV, D_GATE_LORA, D), D_GATE_LORA ** -0.5),
        'rwkv_k_k': nrm((N_RWKV, D), 0.05, 0.85),
        'rwkv_k_a': nrm((N_RWKV, D), 0.05, 1.0),
        'rwkv_r_k': nrm((N_RWKV, RWKV_HEADS, RWKV_HEAD), 0.1),
        'rwkv_ln_w': nrm((N_RWKV, D), 0.05, 1.0),
        'rwkv_ln_b': nrm((N_RWKV, D), 0.01),
        'rwkv_w_o': nrm((N_RWKV, D, D), D ** -0.5),
    }

def reference(x_prompt, x_sample, state_gdn, state_gdn_conv, state_rwkv, state_rwkv_shift,
              norm_g, ffn_w_in, ffn_w_out, gdn_w_in, gdn_conv_w, gdn_a_log, gdn_dt_bias, gdn_o_norm, gdn_w_out,
              rwkv_lerp, rwkv_w_rkv, rwkv_w0, rwkv_w1, rwkv_w2, rwkv_a0, rwkv_a1, rwkv_a2,
              rwkv_v0, rwkv_v1, rwkv_v2, rwkv_g1, rwkv_g2, rwkv_k_k, rwkv_k_a, rwkv_r_k,
              rwkv_ln_w, rwkv_ln_b, rwkv_w_o):
    p = dict(norm_g=norm_g, ffn_w_in=ffn_w_in, ffn_w_out=ffn_w_out,
             gdn_w_in=gdn_w_in, gdn_conv_w=gdn_conv_w, gdn_a_log=gdn_a_log, gdn_dt_bias=gdn_dt_bias,
             gdn_o_norm=gdn_o_norm, gdn_w_out=gdn_w_out,
             rwkv_lerp=rwkv_lerp, rwkv_w_rkv=rwkv_w_rkv, rwkv_w0=rwkv_w0, rwkv_w1=rwkv_w1, rwkv_w2=rwkv_w2,
             rwkv_a0=rwkv_a0, rwkv_a1=rwkv_a1, rwkv_a2=rwkv_a2, rwkv_v0=rwkv_v0, rwkv_v1=rwkv_v1, rwkv_v2=rwkv_v2,
             rwkv_g1=rwkv_g1, rwkv_g2=rwkv_g2, rwkv_k_k=rwkv_k_k, rwkv_k_a=rwkv_k_a, rwkv_r_k=rwkv_r_k,
             rwkv_ln_w=rwkv_ln_w, rwkv_ln_b=rwkv_ln_b, rwkv_w_o=rwkv_w_o)
    dt = x_prompt.dtype
    zero_gdn = jnp.zeros((N_GDN, BATCH, GDN_HEADS, GDN_HEAD_DIM, GDN_HEAD_DIM), dt)
    zero_conv = jnp.zeros((N_GDN, BATCH, GDN_CONV - 1, GDN_CONV_DIM), dt)
    zero_rwkv = jnp.zeros((N_RWKV, BATCH, RWKV_HEADS, RWKV_HEAD, RWKV_HEAD), dt)
    zero_shift = jnp.zeros((N_RWKV, BATCH, D_MODEL), dt)
    y_prompt, gdn_s_p, gdn_c_p, rw_s_p, rw_sh_p = trunk(x_prompt, zero_gdn, zero_conv, zero_rwkv, zero_shift, p)
    y_sample, gdn_s_s, gdn_c_s, rw_s_s, rw_sh_s = trunk(x_sample, state_gdn, state_gdn_conv, state_rwkv, state_rwkv_shift, p)
    return (y_prompt, y_sample, gdn_s_p, gdn_c_p, rw_s_p, rw_sh_p, gdn_s_s, gdn_c_s, rw_s_s, rw_sh_s)


_drawn_inputs = setup_inputs


def setup_inputs(seed=0):
    import zlib

    import numpy as np

    out = dict(_drawn_inputs(seed))
    spreads = {}
    factors = {'rwkv_k_k': 3.622, 'rwkv_ln_b': 8.0}
    for name, (base, spread) in spreads.items():
        noise = np.random.default_rng([zlib.crc32(name.encode()), seed]).standard_normal(out[name].shape)
        drawn = base * np.exp(spread * noise) if base else spread * noise
        out[name] = __import__('jax').numpy.asarray(drawn.astype(out[name].dtype))
    for name, factor in factors.items():
        out[name] = (out[name] * factor).astype(out[name].dtype)
    return out
```

```python
from contextlib import ExitStack

import numpy as np
import concourse.bass as bass
from concourse import mybir

F32 = mybir.dt.float32
F32R = mybir.dt.float32r
BF16 = mybir.dt.bfloat16
ALU = mybir.AluOpType
ACT = mybir.ActivationFunctionType
ds = bass.ds

P = 128
D = 1024
NM = D // P
TP = 512
NB, TS = 8, 4
NS = NB * TS
T = TP + NS
HALF = T // 2
DFF = 2816
NF = DFF // P
KTO = NF // 2
HG = 8
NCH = TP // P
NQKV = 3 * HG
EXT = TP + 3 + NB * (TS + 3)
EPS = 1e-6
GN_EPS = 64e-5
LEVELS = 7

V_NORM = 0
V_CONV = V_NORM + 12 * NM
V_ONORM = V_CONV + NQKV * 4
V_LERP = V_ONORM + 1
V_W0 = V_LERP + 6 * NM
V_A0 = V_W0 + NM
V_KK = V_A0 + NM
V_KA = V_KK + NM
V_RK = V_KA + NM
V_LNW = V_RK + NM
V_LNB = V_LNW + NM
V_ALOG = V_LNB + NM
V_DT = V_ALOG + HG
NVEC = V_DT + HG

PRODUCTS = [
    ("ffn0_in", 2 * NF, NM), ("ffn0_out", 2 * NM, KTO),
    ("gdn_in", 4 * HG, NM), ("gdn_out", NM, NM),
    ("ffn1_in", 2 * NF, NM), ("ffn1_out", 2 * NM, KTO),
    ("ffn2_in", 2 * NF, NM), ("ffn2_out", 2 * NM, KTO),
    ("r", NM, NM), ("k", NM, NM), ("v", NM, NM), ("lora", 3, NM), ("wo", NM, NM),
    ("ffn3_in", 2 * NF, NM), ("ffn3_out", 2 * NM, KTO),
]
BASE, COUNT, KT, SRC = {}, {}, {}, {}
_n, _n8, _n11 = 0, 0, 0
for _name, _units, _kt in PRODUCTS:
    BASE[_name], COUNT[_name], KT[_name] = _n, _units, _kt
    _n += _units
    if _kt == KTO:
        SRC[_name] = _n11
        _n11 += _units
    else:
        SRC[_name] = _n8
        _n8 += _units
N8, N11 = _n8, _n11
SETS = {n: i for i, n in enumerate(
    ["ffn0_in", "gdn_in", "gdn_out", "ffn1_in", "ffn2_in", "x0", "x1", "x2", "x3", "x4", "x5", "wo", "ffn3_in"])}


def masks():
    i = np.arange(P)
    t, s = i[:, None], i[None, :]
    m = {}
    m["ones"] = np.ones((P, P))
    m["ident"] = np.eye(P)
    m["headones"] = (t // 64 == s // 64)
    m["cum128"] = (t <= s)
    m["cum4"] = (t <= s) & (t // 4 == s // 4)
    m["blk4"] = (t // 4 == s // 4)
    lev = [((t >> l) == (s >> l)) & (((t >> (l - 1)) & 1) == 1) & (((s >> (l - 1)) & 1) == 0)
           for l in range(1, LEVELS + 1)]
    lo = {"incl128": (t <= s), "incl64": (t <= s) & (t // 64 == s // 64), "strict64": (t < s) & (t // 64 == s // 64),
          "incl4": (t <= s) & (t // 4 == s // 4), "strict4": (t < s) & (t // 4 == s // 4)}
    f = np.concatenate([np.asarray(v, np.float32) for v in m.values()], 1)
    g = np.concatenate([np.asarray(v, np.float32) for v in lev + list(lo.values())], 1)
    seq = (t // 4 == np.arange(NB)[None, :]).astype(np.float32)
    return f, list(m), g, list(lo), seq


RESET = np.ones((P, T), np.float32)
RESET[:, 0:TP:64] = 0
RESET[:, TP:T:TS] = 0
MF, MF_NAMES, MG, MG_NAMES, MSEQ = masks()


def trunk_kernel(nc, a):
    es = ExitStack()
    with es:
        cursor = [(nc.sbuf_base + 63) // 64 * 64]
        es.enter_context(nc.sbuf_tensor("fence", [P, (nc.sbuf_usable_end - cursor[0] - 128) // 4], F32))
        end = nc.sbuf_usable_end

        def place(name, shape, dt=F32, at=None):
            n = int(np.prod(shape[1:])) * (2 if dt == BF16 else 4)
            n = (n + 31) // 32 * 32
            where = cursor[0] if at is None else at[0]
            assert where + n <= end, (name, where + n, end)
            t = nc.alloc_sbuf_tensor_at(name, list(shape), dt, offset=where)
            if at is None:
                cursor[0] += n
            else:
                at[0] += n
            return t

        vec = place("vec", [P, NVEC])
        mf = place("mf", [P, MF.shape[1]])
        mg = place("mg", [P, MG.shape[1]], BF16)
        mseq = place("mseq", [P, NB])
        eps, gneps = place("eps", [P, 1]), place("gneps", [P, 1])
        M = {n: mf[:, i * P:(i + 1) * P] for i, n in enumerate(MF_NAMES)}
        level_mask = [mg[:, l * P:(l + 1) * P] for l in range(LEVELS)]
        MB = {n: mg[:, (LEVELS + i) * P:(LEVELS + i + 1) * P] for i, n in enumerate(MG_NAMES)}
        h = place("h", [P, 2 * NM, HALF])
        raw = [place(f"raw{i}", [P, KTO * P]) for i in range(4)]
        ECE = place("ECE", [P, NM, 16], F32)
        small_at = cursor[0] - NM * 16 * 4
        tb_at = cursor[0]
        tb = [place(f"tb{i}", [P, 2, HALF]) for i in range(4)]
        rs = place("rs", [P, 2, HALF])
        region = cursor[0]
        at = [region]
        mg_f = place("mg_f", [P, MG.shape[1]], F32, [region + 57344 + 65536])
        whi = [place(f"whi{i}", [P, KTO * P], F32R, at) for i in range(2)]
        wlo = [place(f"wlo{i}", [P, KTO * P], F32R, at) for i in range(2)]
        xh = place("xh", [P, 2 * NM, HALF], F32R, at)
        x_at = at[0] - 2 * NM * HALF * 4
        xl = place("xl", [P, 2 * NM, HALF], F32R, at)
        y = place("y", [P, 2 * NM, HALF], F32, [x_at])
        after_x = at[0]
        mh = place("mh", [P, 2 * NF, HALF], F32R, at)
        ml = place("ml", [P, 2 * NF, HALF], F32R, at)
        ps = es.enter_context(nc.psum_tensor("ps", [P, 8, 512], F32))

        def pair(j):
            return ps[:, 2 * j:2 * j + 2, 0:HALF]

        def v(col):
            return vec[:, col:col + 1]

        def sem(name):
            return es.enter_context(nc.semaphore(name))

        const_in = sem("const_in")
        raw_in = [sem(f"raw_in{i}") for i in range(4)]
        w_hi, w_lo = sem("w_hi"), sem("w_lo")
        acc = sem("acc")
        x_hi, x_lo = sem("x_hi"), sem("x_lo")
        x_f32 = sem("x_f32")
        silu_done, mult_done = sem("silu_done"), sem("mult_done")
        mid_hi, mid_lo = sem("mid_hi"), sem("mid_lo")
        sq_ready, sq_added = sem("sq_ready"), sem("sq_added")
        nrm_mm, rt_ready, rs_ready = sem("nrm_mm"), sem("rt_ready"), sem("rs_ready")
        h_upd, h_tmp = sem("h_upd"), sem("h_tmp")
        cleared = sem("cleared")
        out_done = sem("out_done")

        def above_zero(count):
            return not isinstance(count, int) or count > 0

        def groups(eng, name, body, peel_first=False, peel_last=False):
            n = COUNT[name] // 4
            lo, hi = (1 if peel_first else 0), (n - 1 if peel_last else n)
            if peel_first:
                body(0, n == 1)
            if hi > lo:
                with eng.Fori(lo, hi) as i:
                    body(i * 4, False)
            if peel_last and not (peel_first and n == 1):
                body(4 * (n - 1), True)

        def load_units(sp, name, part=None):
            base, kt = BASE[name], KT[name]
            src = a["w11"] if kt == KTO else a["w8"]

            def one(u, j):
                n = base + u + j
                slot = (base + j) % 4
                if above_zero(n - 3):
                    sp.wait_ge(w_lo, n - 3)
                sp.dma_start(raw[slot][:, 0:kt * P],
                             src[ds(SRC[name] + u + j, 1)].rearrange("o p c -> (o p) c")).then_inc(raw_in[slot], 16)

            def body(u, last):
                for j in range(4):
                    one(u, j)
            if name == "lora":
                for j in range(3):
                    one(0, j)
            elif part is not None:
                body(4 * part, False)
            else:
                groups(sp, name, body, peel_first=(base == 0))

        def split_hi(act, name, u, j):
            base, kt = BASE[name], KT[name]
            n = base + u + j
            slot = (base + j) % 4
            two = (base + j) % 2
            turn = (base + j) // 4 + 1
            cnt = 16 * turn + u * 4
            act.wait_ge(raw_in[slot], cnt)
            if above_zero(2 * (n - 1)):
                act.wait_ge(acc, 2 * (n - 1))
            act.activation(whi[two][:, 0:kt * P], raw[slot][:, 0:kt * P], ACT.Copy).then_inc(w_hi, 1)

        def split_lo(pool, name, u, j):
            base, kt = BASE[name], KT[name]
            n = base + u + j
            slot = (base + j) % 4
            two = (base + j) % 2
            pool.wait_ge(w_hi, n + 1)
            pool.tensor_tensor(wlo[two][:, 0:kt * P], raw[slot][:, 0:kt * P],
                               whi[two][:, 0:kt * P].bitcast(F32), ALU.subtract).then_inc(w_lo, 1)

        def pool_units(pool, name):
            def body(u, last):
                for j in range(4):
                    split_lo(pool, name, u, j)
            groups(pool, name, body)

        def unit_mm(pe, name, u, j, out, hi, lo, k0=0, start=True, stop=True, ready=None):
            base, kt = BASE[name], KT[name]
            n = base + u + j
            two = (base + j) % 2
            pe.wait_ge(w_lo, n + 1)
            for half in range(2):
                for k in range(kt):
                    if ready is not None and half == 0:
                        pe.wait_ge(x_lo, ready + k + 1)
                    wh = whi[two][:, k * P:(k + 1) * P]
                    wl = wlo[two][:, k * P:(k + 1) * P]
                    r = 2 * (k0 + k) + half
                    o = out[:, half, :]
                    pe.matmul(o, wh, hi[:, r, :], start=(start and k == 0), stop=False)
                    pe.matmul(o, wh, lo[:, r, :], start=False, stop=False)
                    mm = pe.matmul(o, wl, hi[:, r, :], start=False, stop=(stop and k == kt - 1))
                mm.then_inc(acc, 1)

        def norm_pe(pe, q):
            pe.wait_ge(sq_added, 8 * (q + 1))
            for half in range(2):
                mm = pe.matmul(pair(3)[:, half, :], M["ones"], tb[2][:, half, :], start=True, stop=True)
            mm.then_inc(nrm_mm, 1)

        def norm_act(act, q):
            act.wait_ge(nrm_mm, q + 1)
            act.activation(rs[:, :, :], pair(3), ACT.Sqrt, bias=eps[:, 0:1], scale=1.0 / D).then_inc(rt_ready, 1)

        def norm_dve(dve, q):
            dve.wait_ge(rt_ready, q + 1)
            dve.reciprocal(rs[:, :, :], rs[:, :, :]).then_inc(rs_ready, 1)
            dve.wait_ge(rs_ready, q + 1)

        def add_square(dve, q, m):
            dve.wait_ge(sq_ready, 8 * q + m + 1)
            if not isinstance(m, int) or m:
                dve.wait_ge(sq_added, 8 * q + m)
            par = m % 2 if isinstance(m, int) else None
            dve.tensor_tensor(tb[2][:, :, :], tb[2][:, :, :], tb[par][:, :, :], ALU.add).then_inc(sq_added, 1)

        def square_h(act, q):
            for m in range(NM):
                if 8 * (q // 2 - 1) + m + 1 > 0:
                    act.wait_ge(h_upd, 8 * (q // 2 - 1) + m + 1)
                if 8 * q + m - 1 > 0:
                    act.wait_ge(sq_added, 8 * q + m - 1)
                act.activation(tb[m % 2][:, :, :], h[:, 2 * m:2 * m + 2, :], ACT.Square).then_inc(sq_ready, 1)

        def clear_squares(dve, q):
            if q > 0:
                dve.wait_ge(nrm_mm, q)
            dve.memset(tb[2][:, :, :], 0.0).then_inc(cleared, 1)
            dve.wait_ge(cleared, q + 1)

        def pre_norm_dve(dve, q, sett, squares=True, keep=None):
            if squares:
                for m in range(NM):
                    add_square(dve, q, m)
            norm_dve(dve, q)
            for m in range(NM):
                xs = tb[m % 2][:, :, :]
                if 8 * sett + m - 1 > 0:
                    dve.wait_ge(x_hi, 8 * sett + m - 1)
                dve.scalar_tensor_tensor(xs, h[:, 2 * m:2 * m + 2, :], v(V_NORM + q * NM + m), rs[:, :, :],
                                         ALU.mult, ALU.mult).then_inc(x_f32, 1)
                dve.wait_ge(x_hi, 8 * sett + m + 1)
                dve.tensor_tensor(xl[:, 2 * m:2 * m + 2, :], xs, xh[:, 2 * m:2 * m + 2, :].bitcast(F32),
                                  ALU.subtract).then_inc(x_lo, 1)

        def pre_norm_act(act, q, sett, xf_base):
            norm_act(act, q)
            for m in range(NM):
                act.wait_ge(x_f32, xf_base + m + 1)
                act.activation(xh[:, 2 * m:2 * m + 2, :], tb[m % 2][:, :, :], ACT.Copy).then_inc(x_hi, 1)

        def post_norm_dve(dve, q, step, last=False, y=y):
            norm_dve(dve, q)
            base = 8 * (q // 2)
            if not last:
                clear_squares(dve, q + 1)
            for m in range(NM):
                if base + m > 0:
                    dve.wait_ge(h_upd, base + m)
                dve.scalar_tensor_tensor(tb[3][:, :, :], y[:, 2 * m:2 * m + 2, :], v(V_NORM + q * NM + m),
                                         rs[:, :, :], ALU.mult, ALU.mult).then_inc(h_tmp, 1)
                dve.wait_ge(h_tmp, tmp_base(q) + m + 1)
                dve.scalar_tensor_tensor(h[:, 2 * m:2 * m + 2, :], tb[3][:, :, :], step,
                                         h[:, 2 * m:2 * m + 2, :], ALU.mult, ALU.add).then_inc(h_upd, 1)
                if not last and m:
                    add_square(dve, q + 1, m - 1)
            if not last:
                add_square(dve, q + 1, NM - 1)

        def tmp_base(q):
            return (q // 2) * 8

        def ffn_pe(pe, f):
            name = f"ffn{f}_in"
            nb = NF * f

            def body(u, last):
                first = isinstance(u, int) and u == 0
                for j in range(4):
                    jj = u // 2 + j // 2 if isinstance(u, int) else (i_half(u) + j // 2)
                    if not first:
                        pe.wait_ge(mult_done if j % 2 else silu_done, nb + jj - 1)
                    unit_mm(pe, name, u, j, pair(j), xh, xl, ready=8 * SETS[name] if first and j == 0 else None)
            n = COUNT[name] // 4
            body(0, False)
            with pe.Fori(1, n) as i:
                pe_i[0] = i
                body(i * 4, False)
            name = f"ffn{f}_out"
            q = FFN_NORM[f] + 1

            def out_body(i, first):
                for j in range(4):
                    m2 = j // 2
                    if j % 2 == 0 and not first:
                        pe.wait_ge(sq_ready, 8 * q + 2 * i + m2 - 1)
                    if first and j == 0:
                        pe.wait_ge(mid_lo, nb + KTO)
                    if first and j == 1:
                        pe.wait_ge(mid_lo, nb + NF)
                    unit_mm(pe, name, i * 4, j, pair(m2), mh, ml, k0=KTO * (j % 2), start=(j % 2 == 0), stop=(j % 2 == 1))
            out_body(0, True)
            with pe.Fori(1, 4) as i:
                out_body(i, False)

        pe_i = [None]

        def i_half(u):
            return pe_i[0] * 2

        FFN_NORM = [0, 4, 6, 10]

        def ffn_act(act, f):
            name = f"ffn{f}_in"
            nb, base = NF * f, BASE[name]

            def body(i, last):
                for j in range(4):
                    n = base + 4 * i + j
                    jj = 2 * i + j // 2
                    if not (last and j >= 2):
                        split_hi(act, name, 4 * i, j + 2)
                    if j % 2 == 0:
                        act.wait_ge(acc, 2 * (n + 1))
                        if above_zero(nb + jj - 1):
                            act.wait_ge(mult_done, nb + jj - 1)
                        act.activation(tb[j // 2][:, :, :], pair(j), ACT.Silu).then_inc(silu_done, 1)
                    else:
                        act.wait_ge(mult_done, nb + jj + 1)
                        act.activation(mh[:, ds(2 * jj, 2), :], tb[2 + j // 2][:, :, :], ACT.Copy).then_inc(mid_hi, 1)
            n = COUNT[name] // 4
            body(0, False)
            with act.Fori(1, n - 1) as i:
                body(i, False)
            body(n - 1, True)
            out_act(act, f"ffn{f}_out", 2, FFN_NORM[f] + 1)

        def out_act(act, name, per_tile, q, y=y):
            base = BASE[name]
            for j in range(2):
                split_hi(act, name, 0, j)

            def body(i, last):
                for j in range(4):
                    n = base + 4 * i + j
                    if not (last and j >= 2):
                        split_hi(act, name, 4 * i, j + 2)
                    if j % per_tile == per_tile - 1:
                        mt = j // per_tile
                        m = (4 // per_tile) * i + mt
                        act.wait_ge(acc, 2 * (n + 1))
                        act.activation(y[:, ds(2 * m, 2), :], pair(mt), ACT.Copy)
                        if not isinstance(i, int) or i or mt >= 2:
                            act.wait_ge(sq_added, 8 * q + m - 1)
                        act.activation(tb[mt % 2][:, :, :], pair(mt), ACT.Square).then_inc(sq_ready, 1)
            n = COUNT[name] // 4
            with act.Fori(0, n - 1) as i:
                body(i, False)
            body(n - 1, True)

        def out_dve(dve, name, per_tile, q):
            clear_squares(dve, q)

            def body(i, last):
                for mt in range(4 // per_tile):
                    m = (4 // per_tile) * i + mt
                    dve.wait_ge(sq_ready, 8 * q + m + 1)
                    dve.wait_ge(sq_added, 8 * q + m)
                    dve.tensor_tensor(tb[2][:, :, :], tb[2][:, :, :], tb[mt % 2][:, :, :], ALU.add).then_inc(sq_added, 1)
            with dve.Fori(0, COUNT[name] // 4) as i:
                body(i, False)

        def ffn_dve(dve, f):
            name = f"ffn{f}_in"
            nb, base = NF * f, BASE[name]
            with dve.Fori(0, NF // 2) as i:
                for two in range(2):
                    jj = 2 * i + two
                    n = base + 4 * i + 2 * two + 1
                    dve.wait_ge(acc, 2 * (n + 1))
                    dve.wait_ge(silu_done, nb + jj + 1)
                    dve.tensor_tensor(tb[2 + two][:, :, :], tb[two][:, :, :], pair(2 * two + 1), ALU.mult).then_inc(mult_done, 1)
                    dve.wait_ge(mid_hi, nb + jj + 1)
                    dve.tensor_tensor(ml[:, ds(2 * jj, 2), :], tb[2 + two][:, :, :],
                                      mh[:, ds(2 * jj, 2), :].bitcast(F32), ALU.subtract).then_inc(mid_lo, 1)
            out_dve(dve, f"ffn{f}_out", 2, FFN_NORM[f] + 1)


        def out_pe(pe, name, q, ready):
            def body(i, first):
                for j in range(4):
                    if not first:
                        pe.wait_ge(sq_ready, 8 * q + 4 * i + j - 3)
                    unit_mm(pe, name, i * 4, j, pair(j), xh, xl, ready=ready if first and j == 0 else None)
            body(0, True)
            body(1, False)

        def whole(t):
            return t[:, :, :].rearrange("p (m a) b -> p m (a b)", a=2)

        def over(ap, n):
            return ap.unsqueeze(2).broadcast_to([ap.shape[0], ap.shape[1], n])

        def over_heads(ap, n):
            return ap.unsqueeze(1).broadcast_to([ap.shape[0], n, ap.shape[1]])

        def banks(b, n, parts, nt):
            return ps[:, b:b + n, :].rearrange("p a (c t) -> p (a c) t", t=P)[0:parts, :, 0:nt]

        INV = ("zl", "tmm", "tcp", "fmm", "gmm", "fup", "gup")

        def inv_at(I, it, l, a):
            L = I["L"]
            full = min(it, I["calls"]) if isinstance(it, int) else it
            small = it - full if isinstance(it, int) else 0
            return (I["past"][0] + full * (2 * L) + 4 * small + 2 * (l - 1) + a,
                    I["past"][1] + full * (2 * L - 2) + 2 * small + 2 * (l - 2) + a,
                    I["past"][2] + full * (2 * L - 4) + 2 * (l - 2) + a,
                    I["past"][3] + full * (2 * L - 2) + 2 * small + 2 * (l - 1) + a)

        def grp(b, a, nt):
            return b[0:nt, 4 * a:4 * a + 4, 0:nt]

        def bank(b, nt):
            return ps[0:nt, b, :].rearrange("p (c t) -> p c t", t=P)[:, :, 0:nt]

        def inv_pool(pool, I, B, it, levels, nt, first=1):
            for l in range(first, levels + 1):
                for a in range(2):
                    if l > 1:
                        pool.wait_ge(I["tmm"], inv_at(I, it, l - 1, a)[0] + 1)
                    if l == 2:
                        pool.wait_ge(I["gup"], inv_at(I, it, 1, a)[3] + 1)
                    pool.tensor_tensor(grp(B["ZL"], a, nt), grp(B["Z"], a, nt),
                                       over_heads(level_mask[l - 1][0:nt, 0:nt], 4), ALU.mult).then_inc(I["zl"], 1)

        def inv_pe(pe, I, B, it, levels, nt):
            for l in range(1, levels + 1):
                for a in range(2):
                    n, c, g, gu = inv_at(I, it, l, a)
                    pe.wait_ge(I["zl"], n + 1)
                    if l > 1:
                        pe.wait_ge(I["fup"], n - 2 + 1)
                        if l > 2:
                            pe.wait_ge(I["tcp"], c - 2 + 1)
                    for i in range(4):
                        r = M["ident"][0:nt, 0:nt] if l == 1 else B["F"][0:nt, 4 * a + i, 0:nt]
                        mm = pe.matmul(bank(a, nt)[:, i, :], B["ZL"][0:nt, 4 * a + i, 0:nt], r, start=True, stop=True)
                    mm.then_inc(I["tmm"], 1)
                if l == 1:
                    continue
                for a in range(2):
                    n, c, g, gu = inv_at(I, it, l, a)
                    pe.wait_ge(I["tcp"], c + 1)
                    pe.wait_ge(I["gup"], gu - 2 + 1)
                    for i in range(4):
                        mm = pe.matmul(bank(2 + 2 * a, nt)[:, i, :], B["G"][0:nt, 4 * a + i, 0:nt],
                                       B["T"][0:nt, 4 * a + i, 0:nt], start=True, stop=True)
                    mm.then_inc(I["fmm"], 1)
                    if l < levels:
                        for i in range(4):
                            mm = pe.matmul(bank(3 + 2 * a, nt)[:, i, :], B["T"][0:nt, 4 * a + i, 0:nt],
                                           B["G"][0:nt, 4 * a + i, 0:nt], start=True, stop=True)
                        mm.then_inc(I["gmm"], 1)

        def inv_act(act, I, B, it, levels, nt):
            for l in range(2, levels + 1):
                for a in range(2):
                    n, c, g, gu = inv_at(I, it, l, a)
                    act.wait_ge(I["tmm"], n + 1)
                    if l > 2:
                        act.wait_ge(I["gmm"], g - 2 + 1)
                    act.activation(grp(B["T"], a, nt), bank(a, nt), ACT.Copy).then_inc(I["tcp"], 1)

        def inv_dve(dve, I, B, it, levels, nt):
            ident = over_heads(M["ident"][0:nt, 0:nt], 4)
            for a in range(2):
                n, c, g, gu = inv_at(I, it, 1, a)
                dve.wait_ge(I["tmm"], n + 1)
                dve.tensor_tensor(grp(B["F"], a, nt), ident, bank(a, nt), ALU.subtract).then_inc(I["fup"], 1)
                dve.tensor_tensor(grp(B["G"], a, nt), ident, grp(B["ZL"], a, nt), ALU.subtract).then_inc(I["gup"], 1)
            for l in range(2, levels + 1):
                for a in range(2):
                    n, c, g, gu = inv_at(I, it, l, a)
                    dve.wait_ge(I["fmm"], c + 1)
                    dve.wait_ge(I["fup"], n - 2 + 1)
                    dve.tensor_tensor(grp(B["F"], a, nt), grp(B["F"], a, nt), bank(2 + 2 * a, nt), ALU.subtract).then_inc(I["fup"], 1)
                    if l < levels:
                        dve.wait_ge(I["gmm"], g + 1)
                        dve.wait_ge(I["gup"], gu - 2 + 1)
                        dve.tensor_tensor(grp(B["G"], a, nt), grp(B["G"], a, nt), bank(3 + 2 * a, nt), ALU.subtract).then_inc(I["gup"], 1)

        at = [after_x]
        qkv = place("qkv", [P, 2 * NQKV, HALF], F32, at)
        zg = place("zg", [P, 2 * HG, HALF], F32, at)
        tail = at[0]
        ext = [place(f"ext{i}", [P, 576], F32, at) for i in range(2)]
        cb = [place(f"cb{i}", [P, 576], F32, at) for i in range(2)]
        hist = place("hist", [P, NQKV, NB * 3], F32, at)
        cnew = place("cnew", [P, NQKV, 3 + NB * 3], F32, at)
        at = [region]
        KV = place("KV", [P, 2, HG, P], F32, at)
        B = dict(**{n: place("g" + n, [P, HG, P], F32, at)
                               for n in ("E", "AT", "Z", "ZL", "T", "F", "G", "BV", "BK", "KD", "U", "EG")})
        assert at[0] <= after_x
        at = [tail]
        ot = place("ot", [P, 2 * HG, HALF], F32, at)
        Sst = place("Sst", [P, HG, P], F32, at)
        SG = place("SG", [P, HG, P], F32, at)
        gs = {n: place("gs_" + n, [P, 5, HG], F32, at) for n in ("beta", "g", "gc", "bE", "egd", "tmp", "tmp2")}
        at = [small_at]
        ba = place("ba", [P, 5, 2 * HG], F32, at)
        gst = place("gst", [P, HG], F32, at)
        wqs = [tb[i][:, 0, 0:2 * NS].rearrange("p (x t) -> p x t", x=2) for i in range(2)]
        wb_at = [tail + T * HG * 4]
        wba = place("wba", [P, NM, 2 * HG], F32, wb_at)
        wbh = place("wbh", [P, NM, 2 * HG], F32R, wb_at)
        wbl = place("wbl", [P, NM, 2 * HG], F32R, wb_at)
        y2 = place("y2", [P, 2 * NM, HALF], F32, [after_x])
        counted = {
            NCH + 1: ("kst", "vst", "gst_r", "gcb_mm", "kk_mm", "vt_mm", "kt_mm", "e_sub", "e_min", "e_max", "eg_exp", "dt_exp",
                      "dn_exp", "z_mul", "at_mul", "bv_up", "bk_up", "kd_up", "z_beta", "at_mask", "qd_up", "wt_mm", "u_mm",
                      "wt_cp", "u_cp"),
            NCH: ("ws_mm", "vn_up", "o_mm", "kv_mm", "sg_up"),
            HG: ("wq_mm", "wq_cp", "wtr_mm", "vns_up", "oa_mm", "oa_up", "vm_up", "kvs_mm", "sgs_up", "sts_up",
                 "on_sq", "on_mm", "on_rt", "on_rs", "on_n", "on_f32", "z_ready"),
            NQKV: ("ext_ready", "conv_done", "qkv_ready"),
        }
        others = ("hist_in", "cv", "l2_sq", "l2_mm", "l2_rt", "l2_rs", "l2_done", "wb_in", "wb_hi", "wb_lo", "ba_mm",
                  "gdn_act", "gdn_dve", "gdn_pe", "o_cp", "s_up", "st_in0", "st_in1", "st_out0", "st_out1", "cn_out", "sp_out")
        S = {n: sem(n) for n in sum(counted.values(), ()) + others}
        GI = dict(L=LEVELS, calls=NCH, past=(0, 0, 0, 0), **{n: sem("inv_" + n) for n in INV})

        def conv_window(t, lo, n):
            return t[:, TP + 3:EXT].rearrange("p (b t) -> p b t", b=NB)[:, :, lo:lo + n]

        def gdn_in_act(act):
            base = BASE["gdn_in"]

            def silu_out(idx, e):
                act.wait_ge(S["cv"], 5 * (idx + 1))
                act.activation(whole(qkv)[:, ds(idx, 1), 0:TP].rearrange("p o t -> p (o t)"), cb[e][:, 0:TP], ACT.Silu)
                act.activation(whole(qkv)[:, ds(idx, 1), TP:T].rearrange("p o (b t) -> p (o b) t", b=NB),
                               conv_window(cb[e], 0, TS), ACT.Silu).then_inc(S["qkv_ready"], 1)

            def body(i, first):
                for j in range(4):
                    idx = 4 * i + j
                    e = j % 2
                    split_hi(act, "gdn_in", 4 * i, j + 2)
                    act.wait_ge(acc, 2 * (base + idx + 1))
                    if above_zero(idx - 1):
                        act.wait_ge(S["conv_done"], idx - 1)
                    act.activation(ext[e][:, 3:3 + HALF], pair(j)[:, 0, :], ACT.Copy)
                    act.activation(ext[e][:, 3 + HALF:3 + TP], pair(j)[:, 1, 0:TP - HALF], ACT.Copy)
                    act.activation(conv_window(ext[e], 3, TS),
                                   pair(j)[:, 1, TP - HALF:HALF].rearrange("p (b t) -> p b t", b=NB),
                                   ACT.Copy).then_inc(S["ext_ready"], 1)
                    if not (first and j == 0):
                        silu_out(idx - 1, 1 - e)
            body(0, True)
            with act.Fori(1, NQKV // 4) as i:
                body(i, False)
            silu_out(NQKV - 1, 1)
            for i in range(2):
                for j in range(4):
                    idx = NQKV + 4 * i + j
                    if 4 * i + j < 6:
                        split_hi(act, "gdn_in", idx - j, j + 2)
                    act.wait_ge(acc, 2 * (base + idx + 1))
                    m = 4 * i + j
                    act.activation(zg[:, 2 * m:2 * m + 2, :], pair(j), ACT.Silu).then_inc(S["z_ready"], 1)

        def gdn_in_dve(dve):
            for e in range(2):
                dve.memset(ext[e][:, 0:3], 0.0)
            dve.wait_ge(S["hist_in"], 16)

            def body(i, first):
                for j in range(4):
                    idx = 4 * i + j
                    e = j % 2

                    def col(tap):
                        return vec[:, ds(V_CONV + 4 * idx + tap, 1)]
                    dve.wait_ge(S["ext_ready"], idx + 1)
                    dve.tensor_copy(conv_window(ext[e], 0, 3),
                                    hist[:, ds(idx, 1), :].rearrange("p o (b t) -> p (o b) t", b=NB)).then_inc(S["cv"], 1)
                    dve.wait_ge(S["cv"], 5 * idx + 1)
                    if above_zero(idx - 1):
                        dve.wait_ge(S["qkv_ready"], idx - 1)
                    n = EXT - 3
                    dve.tensor_scalar(cb[e][:, 0:n], ext[e][:, 0:n], col(0), None, ALU.mult).then_inc(S["cv"], 1)
                    for tap in range(1, 4):
                        dve.wait_ge(S["cv"], 5 * idx + 1 + tap)
                        dve.scalar_tensor_tensor(cb[e][:, 0:n], ext[e][:, tap:tap + n], col(tap), cb[e][:, 0:n],
                                                 ALU.mult, ALU.add).then_inc(S["cv"], 1)
                    cn = cnew[:, ds(idx, 1), :]
                    dve.tensor_copy(cn[:, :, 0:3].rearrange("p o t -> p (o t)"), ext[e][:, TP:TP + 3])
                    dve.tensor_copy(cn[:, :, 3:3 + NB * 3].rearrange("p o (b t) -> p (o b) t", b=NB),
                                    conv_window(ext[e], TS, 3)).then_inc(S["conv_done"], 1)
            body(0, True)
            with dve.Fori(1, NQKV // 4) as i:
                body(i, False)

        def gdn_in_pe(pe):
            ready = 8 * SETS["gdn_in"]

            def body(i, first):
                for j in range(4):
                    if not first:
                        pe.wait_ge(S["ext_ready"], 4 * i + j - 3)
                    unit_mm(pe, "gdn_in", i * 4, j, pair(j), xh, xl, ready=ready if first and j == 0 else None)
            body(0, True)
            with pe.Fori(1, NQKV // 4) as i:
                body(i, False)
            for i in range(2):
                for j in range(4):
                    if i == 0:
                        pe.wait_ge(S["ext_ready"], NQKV - 3 + j)
                    else:
                        pe.wait_ge(S["z_ready"], j + 1)
                    unit_mm(pe, "gdn_in", NQKV + i * 4, j, pair(j), xh, xl)

        def l2_act(act):
            for t in range(2 * HG):
                act.wait_ge(S["qkv_ready"], t + 1)
                if t - 1 > 0:
                    act.wait_ge(S["l2_mm"], t - 1)
                act.activation(tb[t % 2][:, :, :], qkv[:, 2 * t:2 * t + 2, :], ACT.Square).then_inc(S["l2_sq"], 1)
                if t:
                    l2_root(act, t - 1)
            l2_root(act, 2 * HG - 1)

        def l2_root(act, t):
            act.wait_ge(S["l2_mm"], t + 1)
            if t - 1 > 0:
                act.wait_ge(S["l2_done"], t - 1)
            act.activation(tb[2 + t % 2][:, :, :], pair(t % 2), ACT.Sqrt, bias=eps[:, 0:1]).then_inc(S["l2_rt"], 1)

        def l2_pe(pe):
            pe.wait_ge(S["z_ready"], HG)
            for t in range(2 * HG):
                pe.wait_ge(S["l2_sq"], t + 1)
                if t - 1 > 0:
                    pe.wait_ge(S["l2_rt"], t - 1)
                for half in range(2):
                    mm = pe.matmul(pair(t % 2)[:, half, :], M["ones"], tb[t % 2][:, half, :], start=True, stop=True)
                mm.then_inc(S["l2_mm"], 1)

        def l2_dve(dve):
            for t in range(2 * HG):
                dve.wait_ge(S["l2_rt"], t + 1)
                r = tb[2 + t % 2][:, :, :]
                dve.reciprocal(r, r).then_inc(S["l2_rs"], 1)
                dve.wait_ge(S["l2_rs"], t + 1)
                q = qkv[:, 2 * t:2 * t + 2, :]
                dve.scalar_tensor_tensor(q, q, P ** -0.5 if t < HG else 1.0, r, ALU.mult, ALU.mult).then_inc(S["l2_done"], 1)

        PIECES = [(P, slice(0, NCH), list(range(NCH))), (NS, slice(NCH, NCH + 1), [NCH])]

        def ba_pe_first(pe):
            xt_h, xt_l = whole(xh), whole(xl)
            pe.wait_ge(S["wb_lo"], 1)
            pe.wait_ge(S["z_ready"], HG)
            for it in range(NCH + 1):
                lo = it * P if it < NCH else T - P
                o = ps[:, 6, 16 * it:16 * it + 16]
                for k in range(NM):
                    pe.matmul(o, xt_h[:, k, lo:lo + P], wbh[:, k, :], start=(k == 0), stop=False)
                    pe.matmul(o, xt_l[:, k, lo:lo + P], wbh[:, k, :], start=False, stop=False)
                    mm = pe.matmul(o, xt_h[:, k, lo:lo + P], wbl[:, k, :], start=False, stop=(k == NM - 1))
            mm.then_inc(S["ba_mm"], 1)

        def ba_pe_second(pe):
            pe.wait_ge(S["gdn_dve"], 7)
            for nt, sl, its in PIECES:
                cum, blk = (M["cum128"], M["ones"]) if nt == P else (M["cum4"], M["blk4"])
                for it in its:
                    pe.matmul(ps[0:nt, 7, 8 * it:8 * it + 8], cum[0:nt, 0:nt], gs["g"][0:nt, it, :], start=True, stop=True)
                    mm = pe.matmul(ps[0:nt, 7, 64 + 8 * it:72 + 8 * it], blk[0:nt, 0:nt], gs["g"][0:nt, it, :],
                                   start=True, stop=True)
            mm.then_inc(S["gdn_pe"], 1)

        def ba_act(act):
            act.wait_ge(S["wb_in"], 16)
            act.activation(wbh[:, :, :], wba[:, :, :], ACT.Copy).then_inc(S["wb_hi"], 1)

        def ba_act2(act):
            act.wait_ge(S["gdn_dve"], 3)
            act.activation(gs["beta"][:, :, :], ba[:, :, 0:HG], ACT.Sigmoid).then_inc(S["gdn_act"], 1)
            act.activation(gs["tmp2"][:, :, :], gs["tmp"][:, :, :], ACT.Abs).then_inc(S["gdn_act"], 1)
            act.wait_ge(S["gdn_act"], 2)
            act.activation(gs["tmp2"][:, :, :], gs["tmp2"][:, :, :], ACT.Exp, scale=-1.0).then_inc(S["gdn_act"], 1)
            act.wait_ge(S["gdn_act"], 3)
            act.activation(gs["tmp2"][:, :, :], gs["tmp2"][:, :, :], ACT.Ln, bias=1.0).then_inc(S["gdn_act"], 1)
            act.activation(gs["gc"][:, 0, :], vec[:, V_ALOG:V_ALOG + HG], ACT.Exp).then_inc(S["gdn_act"], 1)
            act.wait_ge(S["gdn_dve"], 9)
            act.activation(gs["bE"][:, :, :], gs["gc"][:, :, :], ACT.Exp)
            act.activation(gs["egd"][:, :, :], gs["egd"][:, :, :], ACT.Exp).then_inc(S["gdn_act"], 1)

        def ba_dve(dve):
            dve.wait_ge(S["wb_hi"], 1)
            dve.tensor_tensor(wbl[:, :, :], wba[:, :, :], wbh[:, :, :].bitcast(F32), ALU.subtract).then_inc(S["wb_lo"], 1)

        def ba_dve2(dve):
            d = S["gdn_dve"]
            dve.memset(ba[:, :, :], 0.0).then_inc(d, 1)
            dve.wait_ge(S["ba_mm"], 1)
            dve.wait_ge(d, 1)
            p6 = ps[:, 6, 0:16 * (NCH + 1)].rearrange("p (i c) -> p i c", c=16)
            dve.tensor_copy(ba[:, 0:NCH, :], p6[:, 0:NCH, :])
            dve.tensor_copy(ba[0:NS, NCH, :], p6[P - NS:P, NCH, :]).then_inc(d, 1)
            dve.wait_ge(d, 2)
            dt = vec[:, V_DT:V_DT + HG].unsqueeze(1).broadcast_to([P, NCH + 1, HG])
            dve.tensor_tensor(gs["tmp"][:, :, :], ba[:, :, HG:2 * HG], dt, ALU.add).then_inc(d, 1)
            dve.wait_ge(S["gdn_act"], 5)
            dve.wait_ge(d, 3)
            dve.tensor_scalar(gs["tmp"][:, :, :], gs["tmp"][:, :, :], 0.0, None, ALU.max).then_inc(d, 1)
            dve.wait_ge(d, 4)
            dve.tensor_tensor(gs["g"][:, :, :], gs["tmp"][:, :, :], gs["tmp2"][:, :, :], ALU.add).then_inc(d, 1)
            dve.wait_ge(d, 5)
            ea = gs["gc"][:, 0, :].unsqueeze(1).broadcast_to([P, NCH + 1, HG])
            dve.tensor_tensor(gs["g"][:, :, :], gs["g"][:, :, :], ea, ALU.mult).then_inc(d, 1)
            dve.wait_ge(d, 6)
            dve.tensor_scalar(gs["g"][:, :, :], gs["g"][:, :, :], -1.0, None, ALU.mult).then_inc(d, 1)
            dve.wait_ge(S["gdn_pe"], 1)
            dve.memset(gs["gc"][:, :, :], 0.0)
            dve.memset(gs["egd"][:, :, :], 0.0).then_inc(d, 1)
            dve.wait_ge(d, 8)
            for n, (nt, sl, its) in enumerate(PIECES):
                c = ps[0:nt, 7, 0:40].rearrange("p (i c) -> p i c", c=HG)[:, sl, :]
                dve.tensor_copy(gs["gc"][0:nt, sl, :], c)
                i = dve.tensor_copy(gs["egd"][0:nt, sl, :], ps[0:nt, 7, 64:104].rearrange("p (i c) -> p i c", c=HG)[:, sl, :])
            i.then_inc(S["l2_rs"], 1)
            dve.wait_ge(S["l2_rs"], 2 * HG + 1)
            dve.tensor_tensor(gs["egd"][:, :, :], gs["egd"][:, :, :], gs["gc"][:, :, :], ALU.subtract).then_inc(d, 1)
            dve.memset(Sst[:, :, :], 0.0).then_inc(S["s_up"], 1)
            dve.memset(SG[:, :, :], 0.0).then_inc(S["o_cp"], 1)
            dve.wait_ge(S["gdn_act"], 6)
            dve.tensor_tensor(gs["bE"][:, :, :], gs["bE"][:, :, :], gs["beta"][:, :, :], ALU.mult).then_inc(d, 1)

        def tok(t, it, nt, lo, hi):
            if nt == P:
                return whole(t)[:, lo:hi, ds(it * P, P)]
            return whole(t)[:, lo:hi, TP:T]

        def sc(n, it, nt):
            return gs[n][0:nt, ds(it, 1), :].rearrange("p o h -> p (o h)")

        def chunk_act(act, it, nt):
            act.wait_ge(S["l2_done"], 2 * HG)
            act.wait_ge(S["s_up"], it + 1)
            act.wait_ge(S["o_cp"], it + 1)
            act.activation(KV[:, 0, :, 0:nt], tok(qkv, it, nt, HG, 2 * HG), ACT.Copy).then_inc(S["kst"], 1)
            act.wait_ge(S["e_sub"], it + 1)
            act.activation(B["EG"][:, :, 0:nt], banks(0, 2, P, nt), ACT.Exp).then_inc(S["eg_exp"], 1)
            act.wait_ge(S["e_min"], it + 1)
            act.activation(B["AT"][0:nt, :, 0:nt], B["AT"][0:nt, :, 0:nt], ACT.Exp).then_inc(S["dt_exp"], 1)
            act.wait_ge(S["e_max"], it + 1)
            act.activation(B["E"][0:nt, :, 0:nt], B["E"][0:nt, :, 0:nt], ACT.Exp, scale=-1.0).then_inc(S["dn_exp"], 1)
            inv_act(act, GI, B, it, LEVELS if nt == P else 2, nt)
            act.wait_ge(S["wt_mm"], it + 1)
            act.activation(KV[:, 0, :, 0:nt], banks(6, 2, P, nt), ACT.Copy).then_inc(S["wt_cp"], 1)
            act.wait_ge(S["u_mm"], it + 1)
            act.activation(B["U"][0:nt, :, :], banks(0, 2, nt, P), ACT.Copy).then_inc(S["u_cp"], 1)
            if nt == P:
                act.wait_ge(S["o_mm"], it + 1)
                act.activation(tok(ot, it, nt, 0, HG), banks(4, 2, P, P), ACT.Copy).then_inc(S["o_cp"], 1)

        def chunk_pool(pool, it, nt):
            pool.wait_ge(S["l2_done"], 2 * HG)
            pool.wait_ge(S["gdn_dve"], 10)
            pool.wait_ge(S["s_up"], it + 1)
            pool.wait_ge(S["o_cp"], it + 1)
            pool.tensor_copy(gst[0:nt, :], sc("g", it, nt)).then_inc(S["gst_r"], 1)
            pool.tensor_copy(KV[:, 1, :, 0:nt], tok(qkv, it, nt, 2 * HG, 3 * HG)).then_inc(S["vst"], 1)
            pool.wait_ge(S["z_mul"], it + 1)
            pool.tensor_tensor(B["Z"][0:nt, :, 0:nt], B["Z"][0:nt, :, 0:nt], over(sc("beta", it, nt), nt), ALU.mult).then_inc(S["z_beta"], 1)
            pool.wait_ge(S["z_beta"], it + 1)
            inv_pool(pool, GI, B, it, 1, nt)
            pool.wait_ge(S["at_mul"], it + 1)
            pool.tensor_tensor(B["AT"][0:nt, :, 0:nt], B["AT"][0:nt, :, 0:nt],
                               over_heads(MB["incl128" if nt == P else "incl4"][0:nt, 0:nt], HG), ALU.mult).then_inc(S["at_mask"], 1)
            pool.wait_ge(S["vt_mm"], it + 1)
            pool.wait_ge(S["eg_exp"], it + 1)
            pool.tensor_tensor(KV[:, 1, :, 0:nt], tok(qkv, it, nt, 0, HG), B["EG"][:, :, 0:nt], ALU.mult).then_inc(S["qd_up"], 1)
            inv_pool(pool, GI, B, it, LEVELS if nt == P else 2, nt, first=2)
            if nt == P:
                pool.tensor_tensor(SG[:, :, :], Sst[:, :, :], B["EG"][:, :, P - 1:P].broadcast_to([P, HG, P]),
                                   ALU.mult).then_inc(S["sg_up"], 1)

        KQ = ps[:, 2:6, :].rearrange("p b (h x t) -> p (b h) x t", h=2, x=2)

        def chunk_dve(dve, it, nt):
            dve.wait_ge(S["gcb_mm"], it + 1)
            dve.wait_ge(S["s_up"], it + 1)
            dve.wait_ge(S["o_cp"], it + 1)
            e, at_ = B["E"][0:nt, :, 0:nt], B["AT"][0:nt, :, 0:nt]
            dve.tensor_tensor(e, banks(0, 2, nt, nt), over(sc("gc", it, nt), nt), ALU.subtract).then_inc(S["e_sub"], 1)
            dve.wait_ge(S["e_sub"], it + 1)
            dve.tensor_scalar(at_, e, 0.0, None, ALU.min).then_inc(S["e_min"], 1)
            dve.wait_ge(S["e_min"], it + 1)
            dve.tensor_scalar(e, e, 0.0, None, ALU.max).then_inc(S["e_max"], 1)
            dve.wait_ge(S["kk_mm"], it + 1)
            dve.wait_ge(S["dn_exp"], it + 1)
            dve.tensor_tensor(B["Z"][0:nt, :, 0:nt], KQ[0:nt, :, 1, 0:nt], e, ALU.mult).then_inc(S["z_mul"], 1)
            dve.tensor_tensor(at_, KQ[0:nt, :, 0, 0:nt], at_, ALU.mult).then_inc(S["at_mul"], 1)
            dve.wait_ge(S["vt_mm"], it + 1)
            dve.tensor_tensor(B["BV"][0:nt, :, :], banks(6, 2, nt, P), over(sc("beta", it, nt), P), ALU.mult).then_inc(S["bv_up"], 1)
            dve.wait_ge(S["kt_mm"], it + 1)
            dve.tensor_tensor(B["BK"][0:nt, :, :], banks(0, 2, nt, P), over(sc("bE", it, nt), P), ALU.mult).then_inc(S["bk_up"], 1)
            dve.tensor_tensor(B["KD"][0:nt, :, :], banks(0, 2, nt, P), over(sc("egd", it, nt), P), ALU.mult).then_inc(S["kd_up"], 1)
            inv_dve(dve, GI, B, it, LEVELS if nt == P else 2, nt)
            if nt == P:
                dve.wait_ge(S["ws_mm"], it + 1)
                dve.wait_ge(S["u_cp"], it + 1)
                dve.tensor_tensor(B["U"][:, :, :], B["U"][:, :, :], banks(2, 2, P, P), ALU.subtract).then_inc(S["vn_up"], 1)
                dve.wait_ge(S["o_mm"], it + 1)
                dve.wait_ge(S["sg_up"], it + 1)
                dve.tensor_tensor(Sst[:, :, :], banks(6, 2, P, P), SG[:, :, :], ALU.add).then_inc(S["s_up"], 1)

        def chunk_pe(pe, it, nt):
            pe.wait_ge(S["gst_r"], it + 1)
            pe.wait_ge(S["s_up"], it + 1)
            pe.wait_ge(S["o_cp"], it + 1)
            cum = M["cum128" if nt == P else "cum4"]
            for hh in range(HG):
                mm = pe.matmul(ps[:, hh // 4, (hh % 4) * P:(hh % 4) * P + nt],
                               gst[0:nt, hh:hh + 1].broadcast_to([nt, P]), cum[0:nt, 0:nt], start=True, stop=True)
            mm.then_inc(S["gcb_mm"], 1)
            pe.wait_ge(S["kst"], it + 1)
            for hh in range(HG):
                rhs = tok(qkv, it, nt, 0, 2 * HG).rearrange("p (x h) t -> p x h t", x=2)[:, :, hh, :]
                mm = pe.matmul(KQ[0:nt, hh, :, 0:nt], KV[:, 0, hh, 0:nt], rhs, start=True, stop=True)
            mm.then_inc(S["kk_mm"], 1)
            pe.wait_ge(S["vst"], it + 1)
            for hh in range(HG):
                mm = pe.transpose(ps[0:nt, 6 + hh // 4, (hh % 4) * P:(hh % 4 + 1) * P], KV[:, 1, hh, 0:nt], M["ident"])
            mm.then_inc(S["vt_mm"], 1)
            pe.wait_ge(S["eg_exp"], it + 1)
            for hh in range(HG):
                mm = pe.transpose(ps[0:nt, hh // 4, (hh % 4) * P:(hh % 4 + 1) * P], KV[:, 0, hh, 0:nt], M["ident"])
            mm.then_inc(S["kt_mm"], 1)
            pe.wait_ge(S["kd_up"], it + 1)
            pe.wait_ge(S["at_mul"], it + 1)
            levels = LEVELS if nt == P else 2
            inv_pe(pe, GI, B, it, levels, nt)
            for a in range(2):
                pe.wait_ge(GI["fup"], inv_at(GI, it, levels, a)[0] + 1)
            for hh in range(HG):
                mm = pe.matmul(ps[:, 6 + hh // 4, (hh % 4) * P:(hh % 4) * P + nt], B["BK"][0:nt, hh, :],
                               B["F"][0:nt, hh, 0:nt], start=True, stop=True)
            mm.then_inc(S["wt_mm"], 1)
            for hh in range(HG):
                mm = pe.matmul(ps[0:nt, hh // 4, (hh % 4) * P:(hh % 4 + 1) * P], B["F"][0:nt, hh, 0:nt],
                               B["BV"][0:nt, hh, :], start=True, stop=True)
            mm.then_inc(S["u_mm"], 1)
            pe.wait_ge(S["wt_cp"], it + 1)
            pe.wait_ge(S["qd_up"], it + 1)
            pe.wait_ge(S["at_mask"], it + 1)
            if nt == P:
                for hh in range(HG):
                    mm = pe.matmul(ps[:, 2 + hh // 4, (hh % 4) * P:(hh % 4 + 1) * P], KV[:, 0, hh, :], Sst[:, hh, :],
                                   start=True, stop=True)
                mm.then_inc(S["ws_mm"], 1)
                pe.wait_ge(S["vn_up"], it + 1)
                for hh in range(HG):
                    mm = pe.matmul(ps[:, 6 + hh // 4, (hh % 4) * P:(hh % 4 + 1) * P], B["KD"][:, hh, :], B["U"][:, hh, :],
                                   start=True, stop=True)
                mm.then_inc(S["kv_mm"], 1)
                for hh in range(HG):
                    o = ps[:, 4 + hh // 4, (hh % 4) * P:(hh % 4 + 1) * P]
                    pe.matmul(o, Sst[:, hh, :], KV[:, 1, hh, :], start=True, stop=False)
                    mm = pe.matmul(o, B["U"][:, hh, :], B["AT"][:, hh, :], start=False, stop=True)
                mm.then_inc(S["o_mm"], 1)

        STB = [Sst, SG]

        def seqs(e):
            return ps[:, 6:8, :].rearrange("p a (b t) -> p (a b) t", t=P)

        def sstep_sp(sp):
            sin, sout = [S["st_in0"], S["st_in1"]], [S["st_out0"], S["st_out1"]]
            sp.wait_ge(S["s_up"], NCH + 1)
            sp.dma_start(a["gdn_s_p"], Sst[:, :, :]).then_inc(S["sp_out"], 16)
            sp.wait_ge(S["sp_out"], 16)
            for hh in range(2):
                sp.dma_start(STB[hh][:, :, :], a["state_gdn"][hh]).then_inc(sin[hh], 16)
            for hh in range(HG):
                sp.wait_ge(S["sts_up"], hh + 1)
                sp.dma_start(a["gdn_s_s"][hh], STB[hh % 2][:, :, :]).then_inc(sout[hh % 2], 16)
                if hh + 2 < HG:
                    sp.wait_ge(sout[hh % 2], 16 * (hh // 2 + 1))
                    sp.dma_start(STB[hh % 2][:, :, :], a["state_gdn"][hh + 2]).then_inc(sin[hh % 2], 16)

        def st_arrived(eng, hh):
            eng.wait_ge([S["st_in0"], S["st_in1"]][hh % 2], 16 * (hh // 2 + 1))

        def sstep_pe(pe):
            for hh in range(HG):
                st_arrived(pe, hh)
                pe.wait_ge(S["u_cp"], NCH + 1)
                if hh > 0:
                    pe.wait_ge(S["oa_up"], hh)
                wq = ps[:, hh % 2, 0:2 * NS].rearrange("p (x t) -> p x t", x=2)
                for b in range(NB):
                    mm = pe.matmul(wq[:, :, TS * b:TS * b + TS], STB[hh % 2][:, b, :], KV[:, :, hh, TS * b:TS * b + TS],
                                   start=True, stop=True)
                mm.then_inc(S["wq_mm"], 1)
                pe.wait_ge(S["wq_cp"], hh + 1)
                pe.transpose(ps[0:NS, 2 + hh % 2, 0:P], wqs[hh % 2][:, 0, :], M["ident"]).then_inc(S["wtr_mm"], 1)
                pe.wait_ge(S["vns_up"], hh + 1)
                pe.matmul(ps[:, 4 + hh % 2, 0:NS], B["U"][0:NS, hh, :], B["AT"][0:NS, hh, 0:NS], start=True, stop=True).then_inc(S["oa_mm"], 1)
                pe.wait_ge(S["vm_up"], hh + 1)
                if hh > 0:
                    pe.wait_ge(S["sts_up"], hh)
                for g in range(2):
                    mm = pe.matmul(ps[:, 6 + g, :], B["KD"][0:NS, hh, :],
                                   B["E"][0:NS, 4 * g:4 * g + 4, :].rearrange("p b t -> p (b t)"), start=True, stop=True)
                mm.then_inc(S["kvs_mm"], 1)

        def sstep_act(act):
            for hh in range(HG):
                act.wait_ge(S["wq_mm"], hh + 1)
                if hh - 1 > 0:
                    act.wait_ge(S["oa_up"], hh - 1)
                act.activation(wqs[hh % 2][:, :, :], ps[:, hh % 2, 0:2 * NS].rearrange("p (x t) -> p x t", x=2),
                               ACT.Copy).then_inc(S["wq_cp"], 1)

        def sstep_dve(dve):
            for hh in range(HG):
                dve.wait_ge(S["wtr_mm"], hh + 1)
                dve.wait_ge(S["u_cp"], NCH + 1)
                dve.tensor_tensor(B["U"][0:NS, hh, :], B["U"][0:NS, hh, :], ps[0:NS, 2 + hh % 2, 0:P], ALU.subtract).then_inc(S["vns_up"], 1)
                dve.wait_ge(S["oa_mm"], hh + 1)
                dve.tensor_tensor(whole(ot)[:, hh, TP:T], wqs[hh % 2][:, 1, :], ps[:, 4 + hh % 2, 0:NS], ALU.add).then_inc(S["oa_up"], 1)
                dve.wait_ge(S["kvs_mm"], hh + 1)
                dve.wait_ge(S["sgs_up"], hh + 1)
                dve.tensor_tensor(STB[hh % 2][:, :, :], seqs(0), B["Z"][:, :, :], ALU.add).then_inc(S["sts_up"], 1)

        def sstep_pool(pool):
            for hh in range(HG):
                pool.wait_ge(S["vns_up"], hh + 1)
                if hh > 0:
                    pool.wait_ge(S["kvs_mm"], hh)
                pool.tensor_tensor(B["E"][0:NS, :, :], B["U"][0:NS, hh, :].unsqueeze(1).broadcast_to([NS, NB, P]),
                                   over(mseq[0:NS, :], P), ALU.mult).then_inc(S["vm_up"], 1)
                st_arrived(pool, hh)
                if hh > 0:
                    pool.wait_ge(S["sts_up"], hh)
                gt = B["EG"][:, hh, 0:NS].rearrange("p (b t) -> p b t", t=TS)[:, :, TS - 1]
                pool.tensor_tensor(B["Z"][:, :, :], STB[hh % 2][:, :, :], over(gt, P), ALU.mult).then_inc(S["sgs_up"], 1)

        def onorm_act(act):
            for t in range(HG):
                if t == 0:
                    act.wait_ge(S["oa_up"], HG)
                if t - 1 > 0:
                    act.wait_ge(S["on_mm"], t - 1)
                act.activation(tb[t % 2][:, :, :], ot[:, 2 * t:2 * t + 2, :], ACT.Square).then_inc(S["on_sq"], 1)
                if t:
                    onorm_root(act, t - 1)
            onorm_root(act, HG - 1)
            act.wait_ge(S["sts_up"], HG)
            for t in range(HG):
                act.wait_ge(S["on_f32"], t + 1)
                act.activation(xh[:, 2 * t:2 * t + 2, :], ot[:, 2 * t:2 * t + 2, :], ACT.Copy).then_inc(x_hi, 1)

        def onorm_root(act, t):
            act.wait_ge(S["on_mm"], t + 1)
            if t - 1 > 0:
                act.wait_ge(S["on_n"], t - 1)
            act.activation(tb[2 + t % 2][:, :, :], pair(t % 2), ACT.Sqrt, bias=eps[:, 0:1], scale=1.0 / P).then_inc(S["on_rt"], 1)

        def onorm_pe(pe):
            for t in range(HG):
                pe.wait_ge(S["on_sq"], t + 1)
                if t - 1 > 0:
                    pe.wait_ge(S["on_rt"], t - 1)
                for half in range(2):
                    mm = pe.matmul(pair(t % 2)[:, half, :], M["ones"], tb[t % 2][:, half, :], start=True, stop=True)
                mm.then_inc(S["on_mm"], 1)

        def onorm_dve(dve):
            for t in range(HG):
                dve.wait_ge(S["on_rt"], t + 1)
                r = tb[2 + t % 2][:, :, :]
                o = ot[:, 2 * t:2 * t + 2, :]
                dve.reciprocal(r, r).then_inc(S["on_rs"], 1)
                dve.wait_ge(S["on_rs"], t + 1)
                dve.scalar_tensor_tensor(o, o, v(V_ONORM), r, ALU.mult, ALU.mult).then_inc(S["on_n"], 1)
                dve.wait_ge(S["on_n"], t + 1)
                dve.tensor_tensor(o, o, zg[:, 2 * t:2 * t + 2, :], ALU.mult).then_inc(S["on_f32"], 1)
            for t in range(HG):
                dve.wait_ge(x_hi, 8 * SETS["gdn_out"] + t + 1)
                dve.tensor_tensor(xl[:, 2 * t:2 * t + 2, :], ot[:, 2 * t:2 * t + 2, :],
                                  xh[:, 2 * t:2 * t + 2, :].bitcast(F32), ALU.subtract).then_inc(x_lo, 1)

        def gdn_pe(pe):
            norm_pe(pe, 2)
            gdn_in_pe(pe)
            ba_pe_first(pe)
            l2_pe(pe)
            ba_pe_second(pe)
            with pe.Fori(0, NCH) as it:
                chunk_pe(pe, it, P)
            chunk_pe(pe, NCH, NS)
            sstep_pe(pe)
            onorm_pe(pe)
            out_pe(pe, "gdn_out", 3, 8 * SETS["gdn_out"])
            norm_pe(pe, 3)

        def gdn_act(act):
            for j in range(2):
                split_hi(act, "gdn_in", 0, j)
            pre_norm_act(act, 2, SETS["gdn_in"], 8)
            gdn_in_act(act)
            ba_act(act)
            l2_act(act)
            ba_act2(act)
            with act.Fori(0, NCH) as it:
                chunk_act(act, it, P)
            chunk_act(act, NCH, NS)
            sstep_act(act)
            onorm_act(act)
            out_act(act, "gdn_out", 1, 3, y=y2)
            norm_act(act, 3)
            square_h(act, 4)

        def gdn_dve(dve):
            pre_norm_dve(dve, 2, SETS["gdn_in"], squares=False)
            gdn_in_dve(dve)
            ba_dve(dve)
            l2_dve(dve)
            ba_dve2(dve)
            with dve.Fori(0, NCH) as it:
                chunk_dve(dve, it, P)
            chunk_dve(dve, NCH, NS)
            sstep_dve(dve)
            onorm_dve(dve)
            out_dve(dve, "gdn_out", 1, 3)
            post_norm_dve(dve, 3, 1.0, y=y2)

        def gdn_pool(pool):
            pool_units(pool, "gdn_in")
            with pool.Fori(0, NCH) as it:
                chunk_pool(pool, it, P)
            chunk_pool(pool, NCH, NS)
            sstep_pool(pool)
            pool_units(pool, "gdn_out")

        def gdn_sp(sp):
            sp.wait_ge(mid_lo, NF)
            sp.wait_ge(acc, 2 * BASE["gdn_in"])
            sp.dma_start(hist[:, :, :], a["conv_hist"]).then_inc(S["hist_in"], 16)
            load_units(sp, "gdn_in")
            sp.wait_ge(S["conv_done"], NQKV)
            sp.dma_start(a["conv_new"], cnew[:, :, :]).then_inc(S["cn_out"], 16)
            sp.wait_ge(S["cn_out"], 16)
            sp.dma_start(wba[:, :, :], a["wba"]).then_inc(S["wb_in"], 16)
            load_units(sp, "gdn_out", part=0)
            sstep_sp(sp)
            load_units(sp, "gdn_out", part=1)

        at = [after_x]
        xn = place("xn", [P, 2 * NM, HALF], F32, at)
        dd = place("dd", [P, 2 * NM, HALF], F32, at)
        r_, k_, v_ = (place(n, [P, 2 * NM, HALF], F32, at) for n in ("rr", "rk", "rv"))
        wa2_at = at[0]
        wa2 = place("wa2", [P, D], F32, at)
        lt1 = place("lt1", [P, 2, HALF], F32, at)
        lg = place("lg", [P, 2, HALF], F32, at)
        at = [region]
        RA, RB, BO = (place(n, [P, 2 * NM, HALF], F32, at) for n in ("RA", "RB", "BO"))
        gap = at[0]
        at = [after_x]
        tmp = [[place(f"pt{e}{i}", [P, 2, HALF], F32, at) for i in range(4)] for e in range(2)]
        reset = place("reset", [P, T], F32, at)
        shin = place("shin", [P, NM, NB], F32, [after_x + 2 * NM * HALF * 4 * 2])
        shout = place("shout", [P, NM, 1 + NB], F32, [after_x + 2 * NM * HALF * 4 * 2 + 512])
        at = [after_x]
        Q = dict(**{n: place("r" + n, [P, 8, P], F32, at) for n in ("Z", "ZL", "T", "F", "G", "L2", "L3", "L4")})
        Vt = place("Vt", [P, 4, P], F32, at)
        assert at[0] <= after_x + 2 * 2 * NM * HALF * 4
        Uu = place("Uu", [P, 4, P], F32, [after_x])
        WT = place("WT", [P, 4, P], F32, [after_x + 4096])
        GV = place("GV", [P, 4, P], F32, [after_x + 2 * 4096])
        VMa = place("VMa", [P, NB, P], F32, [after_x + 3 * 4096])
        SO = [place(f"SO{i}", [P, NB, 64], F32, [after_x + 4 * 4096 + 2048 * i]) for i in range(2)]
        VMb = place("VMb", [P, NB, P], F32, [after_x + 5 * 4096])
        at = [gap]
        Att = place("Att", [P, 4, P], F32, at)
        Btt = place("Btt", [P, 4, P], F32, at)
        assert at[0] <= after_x
        at = [wa2_at]
        Ktt = place("Ktt", [P, 4, P], F32, at)
        RS = place("RS", [P, NM, P], F32, at)
        assert at[0] <= wa2_at + 4096 + 2176
        at = [tb_at]
        Ast, Bst, Kst, Vst, Rst = (place(n, [P, 4, P], F32, at) for n in ("Ast", "Bst", "Kst", "Vst", "Rst"))
        assert at[0] <= region
        SB1 = place("SB1", [P, NB, P], F32, [tb_at])
        wqr = [place(f"wqr{i}", [P, 2, NS], F32, [tb_at + 4096 + 256 * i]) for i in range(2)]
        g2w = place("g2w", [P, D], F32, [after_x + 3 * 2 * NM * HALF * 4])
        gdn_last = {}
        spare = [(n, last) for last, names in counted.items() for n in names]

        def take_over(old, last):
            gdn_last[id(old)] = last
            return old

        def past(s, count):
            return count + gdn_last.get(id(s), 0)
        steps = (
            "sh_in", "w2_in", "rm_in", "dd_up", "sh_cp", "sh_out", "mix", "r_cp", "lora_cp", "sg_mm", "sg_cp",
            "kq_sq", "kq_mm", "kq_rt", "kq_rs", "kk_up", "d0", "scan", "cprev", "ex", "a_up", "ka", "b1", "b2", "kp",
            "rkk", "bo_mm", "bo_up", "r_up", "k_up", "ece", "ast", "bst", "rst", "kst", "vst", "l1_mm", "l3_mm", "l2_mm",
            "l4_mm", "z_cp", "l3_up", "l2_up", "l4_up", "vt_mm", "at_mm", "bt_mm", "kt_mm", "vt_cp", "at_cp",
            "bt_cp", "kt_cp", "gv_mm", "gv_cp", "u_mm", "u_cp", "wt_mm", "wt_cp", "sa_mm", "sa_up", "ds_mm", "y_mm",
            "s_add", "s_up", "y_cp", "s_out", "si0", "si1", "so0", "so1", "sb_clr", "wq_mm", "wq_cp", "wtr_mm",
            "sas_up", "ys_mm", "ys_up", "vm_up", "dss_mm", "ss_add", "ss_up", "g2_in", "mu_mm", "yc", "ysq",
            "var_mm", "gn_rt", "gn_rs", "gn1", "gn2", "gn3", "g_mm")
        own = len(steps) - len(spare)
        R = dict(**{n: sem("r_" + n) for n in steps[:own]},
                            **{n: take_over(S[old], last) for n, (old, last) in zip(steps[own:], spare)})
        after = inv_at(GI, NCH + 1, 1, 0), inv_at(GI, NCH + 1, 2, 0)
        RI = dict(L=LEVELS - 1, calls=2 * NCH, past=(after[0][0], after[1][1], after[1][2], after[0][3]),
                   zl=GI["zl"], tmm=GI["tmm"], fup=GI["fup"], tcp=GI["tcp"], fmm=GI["fmm"], gmm=GI["gmm"], gup=GI["gup"])


        def wh(t, m):
            return t[:, 2 * m:2 * m + 2, :]

        def mix_dve(dve, i):
            for m in range(NM):
                c = 8 * i + m
                dve.wait_ge(x_hi, 8 * SETS[f"x{i}"] + m - 1)
                x = tb[m % 2][:, :, :]
                dve.scalar_tensor_tensor(x, wh(dd, m), v(V_LERP + i * NM + m), wh(xn, m), ALU.mult, ALU.add).then_inc(R["mix"], 1)
                dve.wait_ge(x_hi, 8 * SETS[f"x{i}"] + m + 1)
                dve.tensor_tensor(wh(xl, m), x, wh(xh, m).bitcast(F32), ALU.subtract).then_inc(x_lo, 1)

        def mix_act(act, i):
            for m in range(NM):
                act.wait_ge(R["mix"], past(R["mix"], 8 * i + m + 1))
                act.activation(wh(xh, m), tb[m % 2][:, :, :], ACT.Copy).then_inc(x_hi, 1)

        def rkv_act(act, i, name, dst):
            for j in range(2):
                split_hi(act, name, 0, j)
            act.wait_ge(acc, 2 * BASE[name])
            mix_act(act, i)
            for u in (0, 4):
                for j in range(4):
                    if u + j + 2 < NM:
                        split_hi(act, name, u, j + 2)
                    act.wait_ge(acc, 2 * (BASE[name] + u + j + 1))
                    act.activation(wh(dst, u + j), pair(j), ACT.Copy).then_inc(R["r_cp"], 1)

        def rkv_pe(pe, i, name):
            for u in (0, 4):
                for j in range(4):
                    if 8 * i + u + j - 3 > 0:
                        pe.wait_ge(R["r_cp"], past(R["r_cp"], 8 * i + u + j - 3))
                    unit_mm(pe, name, u, j, pair(j), xh, xl, ready=8 * SETS[f"x{i}"] if u + j == 0 else None)

        def shift_dve(dve):
            norm_dve(dve, 8)
            for m in range(NM):
                dve.scalar_tensor_tensor(wh(xn, m), wh(h, m), v(V_NORM + 8 * NM + m), rs[:, :, :],
                                         ALU.mult, ALU.mult).then_inc(x_f32, 1)
            dve.wait_ge(x_f32, 40)
            dve.wait_ge(R["sh_in"], past(R["sh_in"], 16))
            x, d = whole(xn), whole(dd)
            xs = x[:, :, TP:T].rearrange("p m (b t) -> p m b t", b=NB)
            dsn = d[:, :, TP:T].rearrange("p m (b t) -> p m b t", b=NB)
            dve.tensor_tensor(d[:, :, 1:TP], x[:, :, 0:TP - 1], x[:, :, 1:TP], ALU.subtract)
            dve.tensor_scalar(d[:, :, 0:1], x[:, :, 0:1], -1.0, None, ALU.mult)
            dve.tensor_tensor(dsn[:, :, :, 1:TS], xs[:, :, :, 0:TS - 1], xs[:, :, :, 1:TS], ALU.subtract)
            dve.tensor_tensor(dsn[:, :, :, 0], shin[:, :, :], xs[:, :, :, 0], ALU.subtract).then_inc(R["dd_up"], 1)
            dve.tensor_copy(shout[:, :, 0:1], x[:, :, TP - 1:TP])
            dve.tensor_copy(shout[:, :, 1:1 + NB], xs[:, :, :, TS - 1]).then_inc(R["sh_cp"], 1)
            dve.wait_ge(R["dd_up"], past(R["dd_up"], 1))

        def lora_act(act):
            for j in range(2):
                split_hi(act, "lora", 0, j)
            for j in range(3):
                n = BASE["lora"] + j
                act.wait_ge(acc, 2 * n)
                mix_act(act, 3 + j)
                if j == 0:
                    split_hi(act, "lora", 0, 2)
                act.wait_ge(acc, 2 * (n + 1))
                if j == 0:
                    act.activation(lt1[0:64, :, :], ps[0:64, 0:2, 0:HALF], ACT.Tanh).then_inc(R["lora_cp"], 1)
                elif j == 1:
                    act.activation(lt1[64:P, :, :], ps[64:P, 2:4, 0:HALF], ACT.Copy).then_inc(R["lora_cp"], 1)
                else:
                    act.activation(lg[:, :, :], pair(2), ACT.Sigmoid).then_inc(R["lora_cp"], 1)

        def lora_pe(pe):
            for j in range(3):
                pe.wait_ge(R["r_cp"], past(R["r_cp"], 24))
                unit_mm(pe, "lora", 0, j, pair(j), xh, xl, ready=8 * SETS[f"x{3 + j}"])

        def lora_pool(pool):
            for j in range(3):
                split_lo(pool, "lora", 0, j)

        def prep_pe(pe):
            pe.wait_ge(R["w2_in"], past(R["w2_in"], 16))
            pe.wait_ge(R["lora_cp"], past(R["lora_cp"], 3))
            for m in range(NM):
                if 2 * (m - 1) > 0:
                    pe.wait_ge(R["sg_cp"], past(R["sg_cp"], 2 * (m - 1)))
                for par in range(2):
                    lo = 64 * par
                    for half in range(2):
                        mm = pe.matmul(pair(2 * (m % 2) + par)[:, half, :], wa2[lo:lo + 64, m * P:(m + 1) * P],
                                       lt1[lo:lo + 64, half, :], start=True, stop=True)
                    mm.then_inc(R["sg_mm"], 1)
            for m in range(NM):
                pe.wait_ge(R["kq_sq"], past(R["kq_sq"], m + 1))
                if m - 1 > 0:
                    pe.wait_ge(R["kq_rt"], past(R["kq_rt"], m - 1))
                if m < 2:
                    pe.wait_ge(R["sg_cp"], past(R["sg_cp"], 2 * NM))
                for half in range(2):
                    mm = pe.matmul(pair(m % 2)[:, half, :], M["headones"], tb[m % 2][:, half, :], start=True, stop=True)
                mm.then_inc(R["kq_mm"], 1)
            for m in range(NM):
                pe.wait_ge(R["rkk"], past(R["rkk"], m + 1))
                if m - 1 > 0:
                    pe.wait_ge(R["bo_up"], past(R["bo_up"], m - 1))
                for half in range(2):
                    mm = pe.matmul(pair(2 + m % 2)[:, half, :], M["headones"], tmp[m % 2][3][:, half, :], start=True, stop=True)
                mm.then_inc(R["bo_mm"], 1)

        def prep_act(act):
            for m in range(NM):
                for par, (dst, bias) in enumerate(((RA, V_W0), (RB, V_A0))):
                    act.wait_ge(R["sg_mm"], past(R["sg_mm"], 2 * m + par + 1))
                    act.activation(wh(dst, m), pair(2 * (m % 2) + par), ACT.Sigmoid, bias=v(bias + m)).then_inc(R["sg_cp"], 1)
            for m in range(NM):
                if m - 1 > 0:
                    act.wait_ge(R["kq_mm"], past(R["kq_mm"], m - 1))
                act.activation(tb[m % 2][:, :, :], wh(k_, m), ACT.Square, scale=v(V_KK + m)).then_inc(R["kq_sq"], 1)
                if m:
                    kroot(act, m - 1)
            kroot(act, NM - 1)
            for m in range(NM):
                u0, u2, u3, u6 = (t[:, :, :] for t in tmp[m % 2])
                act.wait_ge(R["cprev"], past(R["cprev"], m + 1))
                if m - 1 > 0:
                    act.wait_ge(R["k_up"], past(R["k_up"], m - 1))
                if m - 1 > 0:
                    act.wait_ge(R["b2"], past(R["b2"], m - 1))
                act.activation(u3, u2, ACT.Exp, scale=-1.0)
                act.activation(u0, u0, ACT.Exp).then_inc(R["ex"], 1)
                act.wait_ge(R["ex"], past(R["ex"], 2 * m + 1))
                act.activation(u2, u2, ACT.Exp).then_inc(R["ex"], 1)

        def kroot(act, m):
            act.wait_ge(R["kq_mm"], past(R["kq_mm"], m + 1))
            if m - 1 > 0:
                act.wait_ge(R["kk_up"], past(R["kk_up"], m - 1))
            act.activation(tb[2 + m % 2][:, :, :], pair(m % 2), ACT.Sqrt, bias=eps[:, 0:1]).then_inc(R["kq_rt"], 1)

        def prep_dve(dve):
            for m in range(NM):
                dve.wait_ge(R["kq_rt"], past(R["kq_rt"], m + 1))
                q = tb[2 + m % 2][:, :, :]
                dve.reciprocal(q, q).then_inc(R["kq_rs"], 1)
                dve.wait_ge(R["kq_rs"], past(R["kq_rs"], m + 1))
                dve.scalar_tensor_tensor(wh(BO, m), wh(k_, m), v(V_KK + m), q, ALU.mult, ALU.mult).then_inc(R["kk_up"], 1)
            dve.wait_ge(R["kk_up"], past(R["kk_up"], NM))
            dve.wait_ge(R["rm_in"], past(R["rm_in"], 16))
            for m in range(NM):
                t0, t2, t3, t6 = tmp[m % 2]
                u0, u2, u3, u6 = (t[:, :, :] for t in tmp[m % 2])
                if m - 1 > 0:
                    dve.wait_ge(R["a_up"], past(R["a_up"], m - 1))
                if m - 1 > 0:
                    dve.wait_ge(R["ece"], past(R["ece"], m - 1))
                if m - 1 > 0:
                    dve.wait_ge(R["r_up"], past(R["r_up"], m - 1))
                dve.tensor_scalar(u0, wh(RA, m), -float(np.exp(-0.5)), None, ALU.mult).then_inc(R["d0"], 1)
                dve.wait_ge(R["d0"], past(R["d0"], m + 1))
                flat = lambda t: t[:, :, :].rearrange("p a b -> p (a b)")
                dve.tensor_tensor_scan(flat(t2), reset[:, :], flat(t0), 0.0, ALU.mult, ALU.add).then_inc(R["scan"], 1)
                dve.wait_ge(R["scan"], past(R["scan"], m + 1))
                dve.tensor_tensor(u0, u2, u0, ALU.subtract).then_inc(R["cprev"], 1)
                if m - 1 > 0:
                    dve.wait_ge(R["bo_mm"], past(R["bo_mm"], m - 1))
                dve.tensor_scalar(u6, wh(RB, m), -1.0, v(V_KA + m), ALU.add, ALU.mult).then_inc(R["ka"], 1)
                dve.wait_ge(R["ka"], past(R["ka"], m + 1))
                dve.scalar_tensor_tensor(wh(k_, m), u6, 1.0, wh(k_, m), ALU.add, ALU.mult).then_inc(R["kp"], 1)
                dve.wait_ge(R["kp"], past(R["kp"], m + 1))
                dve.scalar_tensor_tensor(u6, wh(r_, m), v(V_RK + m), wh(k_, m), ALU.mult, ALU.mult).then_inc(R["rkk"], 1)
                dve.wait_ge(R["ex"], past(R["ex"], 2 * m + 1))
                dve.scalar_tensor_tensor(wh(RA, m), wh(BO, m), -1.0, u0, ALU.mult, ALU.mult).then_inc(R["a_up"], 1)
                dve.wait_ge(R["bo_mm"], past(R["bo_mm"], m + 1))
                dve.wait_ge(R["b1"], past(R["b1"], m + 1))
                dve.wait_ge(R["a_up"], past(R["a_up"], m + 1))
                dve.tensor_tensor(wh(BO, m), wh(v_, m), pair(2 + m % 2), ALU.mult).then_inc(R["bo_up"], 1)

        def prep_pool(pool):
            for m in range(NM):
                u0, u2, u3, u6 = (t[:, :, :] for t in tmp[m % 2])
                pool.wait_ge(R["ka"], past(R["ka"], m + 1))
                pool.tensor_tensor(wh(RB, m), wh(BO, m), wh(RB, m), ALU.mult).then_inc(R["b1"], 1)
                pool.wait_ge(R["ex"], past(R["ex"], 2 * m + 1))
                pool.wait_ge(R["b1"], past(R["b1"], m + 1))
                pool.tensor_tensor(wh(RB, m), wh(RB, m), u3, ALU.mult).then_inc(R["b2"], 1)
                pool.wait_ge(R["rkk"], past(R["rkk"], m + 1))
                pool.tensor_tensor(wh(k_, m), wh(k_, m), u3, ALU.mult).then_inc(R["k_up"], 1)
                pool.wait_ge(R["ex"], past(R["ex"], 2 * m + 2))
                pool.tensor_tensor(wh(r_, m), wh(r_, m), u2, ALU.mult).then_inc(R["r_up"], 1)
                flat = tmp[m % 2][1][:, :, :].rearrange("p a b -> p (a b)")
                pool.tensor_copy(ECE[:, m, 0:8], flat[:, 0:TP].rearrange("p (c t) -> p c t", t=64)[:, :, 63])
                pool.tensor_copy(ECE[:, m, 8:16], flat[:, TP:T].rearrange("p (c t) -> p c t", t=TS)[:, :, TS - 1]).then_inc(R["ece"], 1)

        def rt(t, c, g, nt):
            if nt == P:
                return whole(t)[:, 4 * g:4 * g + 4, ds(c * P, P)]
            return whole(t)[:, 4 * g:4 * g + 4, TP:T]

        def start_waits(e, n, smp):
            e.wait_ge(R["s_up"], past(R["s_up"], 2 * n + 1 if smp is None else 17))
            e.wait_ge(R["y_cp"], past(R["y_cp"], n + 1 if smp is None else 9))
            if smp:
                e.wait_ge(R["ss_up"], past(R["ss_up"], 4 * smp))
                e.wait_ge(R["so0"], past(R["so0"], 32 * smp))
                e.wait_ge(R["so1"], past(R["so1"], 32 * smp))
                e.wait_ge(R["vm_up"], past(R["vm_up"], 4 * smp))
                e.wait_ge(R["ys_up"], past(R["ys_up"], 4 * smp))

        def rstep_pool(pool, n, c, g, nt, smp=None):
            start_waits(pool, n, smp)
            pool.tensor_copy(Ast[:, :, 0:nt], rt(RA, c, g, nt)).then_inc(R["ast"], 1)
            pool.tensor_copy(Bst[:, :, 0:nt], rt(RB, c, g, nt)).then_inc(R["bst"], 1)
            pool.tensor_copy(Rst[:, :, 0:nt], rt(r_, c, g, nt)).then_inc(R["rst"], 1)
            pool.tensor_copy(Vst[:, :, 0:nt], rt(v_, c, g, nt)).then_inc(R["vst"], 1)
            pool.wait_ge(R["z_cp"], past(R["z_cp"], n + 1))
            inv_pool(pool, RI, Q, n, LEVELS - 1 if nt == P else 2, nt)

        def rstep_act(act, n, c, g, nt, smp=None):
            start_waits(act, n, smp)
            act.activation(Kst[:, :, 0:nt], rt(k_, c, g, nt), ACT.Copy).then_inc(R["kst"], 1)
            act.wait_ge(R["l1_mm"], past(R["l1_mm"], n + 1))
            act.activation(Q["Z"][0:nt, :, 0:nt], banks(0, 2, nt, nt), ACT.Copy, scale=-1.0).then_inc(R["z_cp"], 1)
            for mm, cp, dst, b in ((R["vt_mm"], R["vt_cp"], Vt, 0), (R["at_mm"], R["at_cp"], Att, 1), (R["bt_mm"], R["bt_cp"], Btt, 2),
                                   (R["kt_mm"], R["kt_cp"], Ktt, 3)):
                act.wait_ge(mm, past(mm, n + 1))
                act.activation(dst[0:nt, :, :], banks(b, 1, nt, P), ACT.Copy).then_inc(cp, 1)
            inv_act(act, RI, Q, n, LEVELS - 1 if nt == P else 2, nt)
            act.wait_ge(R["gv_mm"], past(R["gv_mm"], n + 1))
            act.activation(GV[0:nt, :, :], banks(6, 1, nt, P), ACT.Copy).then_inc(R["gv_cp"], 1)
            act.wait_ge(R["wt_mm"], past(R["wt_mm"], n + 1))
            act.activation(WT[:, :, 0:nt], banks(7, 1, P, nt), ACT.Copy).then_inc(R["wt_cp"], 1)
            act.wait_ge(R["u_mm"], past(R["u_mm"], n + 1))
            act.activation(Uu[0:nt, :, :], banks(0, 1, nt, P), ACT.Copy).then_inc(R["u_cp"], 1)
            if nt == P:
                act.wait_ge(R["y_mm"], past(R["y_mm"], 2 * n + 2))
                act.activation(rt(RA, c, g, nt), banks(6, 1, P, P), ACT.Copy).then_inc(R["y_cp"], 1)

        def rstep_dve(dve, n, c, g, nt, smp=None):
            start_waits(dve, n, smp)
            cs = "64" if nt == P else "4"
            for mm, up, dst, b, mask in ((R["l3_mm"], R["l3_up"], Q["L3"], 2, "incl"), (R["l2_mm"], R["l2_up"], Q["L2"], 4, "strict"),
                                         (R["l4_mm"], R["l4_up"], Q["L4"], 6, "incl")):
                dve.wait_ge(mm, past(mm, n + 1))
                dve.tensor_tensor(dst[0:nt, :, 0:nt], banks(b, 2, nt, nt), over_heads(MB[mask + cs][0:nt, 0:nt], 8),
                                  ALU.mult).then_inc(up, 1)
            inv_dve(dve, RI, Q, n, LEVELS - 1 if nt == P else 2, nt)
            if nt != P:
                return
            for cc in range(2):
                pp = slice(64 * cc, 64 * cc + 64)
                if cc == 0:
                    dve.wait_ge(R["u_cp"], past(R["u_cp"], n + 1))
                dve.wait_ge(R["sa_mm"], past(R["sa_mm"], 2 * n + cc + 1))
                dve.tensor_tensor(Uu[pp, :, :], Uu[pp, :, :], banks(5, 1, P, P)[pp], ALU.add).then_inc(R["sa_up"], 1)
                dve.wait_ge(R["ds_mm"], past(R["ds_mm"], 2 * n + cc + 1))
                dve.wait_ge(R["y_mm"], past(R["y_mm"], 2 * n + cc + 1))
                d = banks(4, 1, P, P)
                for par in range(2):
                    hp = slice(64 * par, 64 * par + 64)
                    i = dve.tensor_tensor(RS[hp, 4 * g:4 * g + 4, hp], RS[hp, 4 * g:4 * g + 4, hp], d[hp, :, hp], ALU.add)
                i.then_inc(R["s_add"], 1)
                dve.wait_ge(R["s_add"], past(R["s_add"], 2 * n + cc + 1))
                e = ECE[:, 4 * g:4 * g + 4, ds(2 * c + cc, 1)].broadcast_to([P, 4, P])
                dve.tensor_tensor(RS[:, 4 * g:4 * g + 4, :], RS[:, 4 * g:4 * g + 4, :], e, ALU.mult).then_inc(R["s_up"], 1)

        def rstep_pe(pe, n, c, g, nt, smp=None):
            start_waits(pe, n, smp)

            def heads():
                for tl in range(4):
                    for par in range(2):
                        yield par * 4 + tl, tl, slice(64 * par, 64 * par + 64)

            def prod(ready, st, rhs, b, done):
                for s_ in ready:
                    pe.wait_ge(s_, past(s_, n + 1))
                for s, tl, pr in heads():
                    mm = pe.matmul(ps[0:nt, b + s // 4, (s % 4) * P:(s % 4) * P + nt], st[pr, tl, 0:nt], rhs[pr, tl, 0:nt],
                                   start=True, stop=True)
                mm.then_inc(done, 1)
            prod((R["ast"], R["bst"]), Ast, Bst, 0, R["l1_mm"])
            prod((R["rst"],), Bst, Rst, 2, R["l3_mm"])
            prod((R["kst"],), Kst, Ast, 4, R["l2_mm"])
            prod((), Kst, Rst, 6, R["l4_mm"])
            for st, b, wait, done in ((Vst, 0, R["z_cp"], R["vt_mm"]), (Ast, 1, R["z_cp"], R["at_mm"]), (Bst, 2, R["l3_up"], R["bt_mm"]),
                                      (Kst, 3, R["l3_up"], R["kt_mm"])):
                pe.wait_ge(wait, past(wait, n + 1))
                if st is Vst:
                    pe.wait_ge(R["vst"], past(R["vst"], n + 1))
                for tl in range(4):
                    mm = pe.transpose(ps[0:nt, b, tl * P:(tl + 1) * P], st[:, tl, 0:nt], M["ident"])
                mm.then_inc(done, 1)
            for cp in (R["vt_cp"], R["at_cp"], R["bt_cp"], R["kt_cp"]):
                pe.wait_ge(cp, past(cp, n + 1))
            pe.wait_ge(R["l2_up"], past(R["l2_up"], n + 1))
            levels = LEVELS - 1 if nt == P else 2
            inv_pe(pe, RI, Q, n, levels, nt)
            for a_ in range(2):
                pe.wait_ge(RI["fup"], past(RI["fup"], inv_at(RI, n, levels, a_)[0] + 1))
            pe.wait_ge(R["l4_up"], past(R["l4_up"], n + 1))
            for s, tl, pr in heads():
                mm = pe.matmul(ps[0:nt, 6, tl * P:(tl + 1) * P][:, pr], Q["L2"][0:nt, s, 0:nt], Vt[0:nt, tl, pr], start=True, stop=True)
            mm.then_inc(R["gv_mm"], 1)
            for s, tl, pr in heads():
                mm = pe.matmul(ps[pr, 7, tl * P:tl * P + nt], Att[0:nt, tl, pr], Q["F"][0:nt, s, 0:nt], start=True, stop=True)
            mm.then_inc(R["wt_mm"], 1)
            pe.wait_ge(R["gv_cp"], past(R["gv_cp"], n + 1))
            for s, tl, pr in heads():
                mm = pe.matmul(ps[0:nt, 0, tl * P:(tl + 1) * P][:, pr], Q["F"][0:nt, s, 0:nt], GV[0:nt, tl, pr], start=True, stop=True)
            mm.then_inc(R["u_mm"], 1)
            pe.wait_ge(R["wt_cp"], past(R["wt_cp"], n + 1))
            if nt != P:
                return
            for cc in range(2):
                pp = slice(64 * cc, 64 * cc + 64)
                if cc:
                    pe.wait_ge(R["s_up"], past(R["s_up"], 2 * n + 2))
                for tl in range(4):
                    mm = pe.matmul(ps[pp, 5, tl * P:(tl + 1) * P], WT[:, tl, pp], RS[:, 4 * g + tl, :], start=True, stop=True)
                mm.then_inc(R["sa_mm"], 1)
                pe.wait_ge(R["sa_up"], past(R["sa_up"], 2 * n + cc + 1))
                for tl in range(4):
                    o = ps[:, 4, tl * P:(tl + 1) * P]
                    pe.matmul(o, Ktt[pp, tl, :], Vt[pp, tl, :], start=True, stop=False)
                    mm = pe.matmul(o, Btt[pp, tl, :], Uu[pp, tl, :], start=False, stop=True)
                mm.then_inc(R["ds_mm"], 1)
                for tl in range(4):
                    co = slice(tl * P + 64 * cc, tl * P + 64 * cc + 64)
                    pe.matmul(ps[:, 6, co], RS[:, 4 * g + tl, :], Rst[:, tl, pp], start=True, stop=False,
                              skip_group_check=True)
                    for par in range(2):
                        pr = slice(64 * par, 64 * par + 64)
                        s = par * 4 + tl
                        pe.matmul(ps[pr, 6, co], Uu[pp, tl, pr], Q["L3"][pp, s, pp], start=False, stop=False, skip_group_check=True)
                        mm = pe.matmul(ps[pr, 6, co], Vt[pp, tl, pr], Q["L4"][pp, s, pp], start=False, stop=True,
                                       skip_group_check=True)
                mm.then_inc(R["y_mm"], 1)

        def rst(i):
            return (RS if i % 2 == 0 else SB1)

        def rst_in(eng, i):
            eng.wait_ge((R["si0"], R["si1"])[i % 2], past((R["si0"], R["si1"])[i % 2], 32 * (i // 2 + 1)))

        def rsample_sp(sp):
            sp.wait_ge(R["s_up"], past(R["s_up"], 17))
            for par in range(2):
                hp = slice(64 * par, 64 * par + 64)
                sp.dma_start(a["rwkv_s_p"][hp], RS[hp, :, hp]).then_inc(R["s_out"], 16)
            sp.wait_ge(R["s_out"], past(R["s_out"], 32))
            for i in range(NM):
                g = i // 4
                if i % 4 == 0:
                    sp.wait_ge(R["sb_clr"], past(R["sb_clr"], g + 1))
                if i % 4 >= 2 or i >= 4:
                    sp.wait_ge(R["ss_up"], past(R["ss_up"], i - 1))
                for par in range(2):
                    hp = slice(64 * par, 64 * par + 64)
                    sp.dma_start(rst(i)[hp, :, hp], a["state_rwkv"][i, hp]).then_inc((R["si0"], R["si1"])[i % 2], 16)
                if i % 4 >= 1:
                    rout(sp, i - 1)
                if i % 4 == 3:
                    rout(sp, i)

        def rout(sp, i):
            sp.wait_ge(R["ss_up"], past(R["ss_up"], i + 1))
            sp.dma_start(a["rwkv_s_s"][i], SO[i % 2][:, :, :]).then_inc((R["so0"], R["so1"])[i % 2], 16)

        def rsample_pe(pe, g):
            for tl in range(4):
                i = 4 * g + tl
                rst_in(pe, i)
                pe.wait_ge(R["u_cp"], past(R["u_cp"], 8 + g + 1))
                if i > 0:
                    pe.wait_ge(R["ys_up"], past(R["ys_up"], i))
                b0 = ps[:, tl % 2, 0:2 * NS].rearrange("p (x t) -> p x t", x=2)
                for b in range(NB):
                    cols = slice(TS * b, TS * b + TS)
                    pe.matmul(b0[:, 0, cols], rst(i)[:, b, :], WT[:, tl, cols], start=True, stop=True)
                    mm = pe.matmul(b0[:, 1, cols], rst(i)[:, b, :], whole(r_)[:, i, TP:T][:, cols], start=True, stop=True)
                mm.then_inc(R["wq_mm"], 1)
                pe.wait_ge(R["wq_cp"], past(R["wq_cp"], i + 1))
                pe.transpose(ps[0:NS, 2, 0:P], wqr[i % 2][:, 0, :], M["ident"]).then_inc(R["wtr_mm"], 1)
                pe.wait_ge(R["sas_up"], past(R["sas_up"], i + 1))
                for par in range(2):
                    pr = slice(64 * par, 64 * par + 64)
                    s = par * 4 + tl
                    pe.matmul(ps[pr, 4, 0:NS], Uu[0:NS, tl, pr], Q["L3"][0:NS, s, 0:NS], start=True, stop=False)
                    mm = pe.matmul(ps[pr, 4, 0:NS], Vt[0:NS, tl, pr], Q["L4"][0:NS, s, 0:NS], start=False, stop=True)
                mm.then_inc(R["ys_mm"], 1)
                pe.wait_ge(R["vm_up"], past(R["vm_up"], i + 1))
                if i > 0:
                    pe.wait_ge(R["ss_add"], past(R["ss_add"], i))
                for q in range(2):
                    o = ps[:, 6 + q, :]
                    f4 = lambda t: t[0:NS, 4 * q:4 * q + 4, :].rearrange("p b t -> p (b t)")
                    pe.matmul(o, Btt[0:NS, tl, :], f4(VMa), start=True, stop=False)
                    mm = pe.matmul(o, Ktt[0:NS, tl, :], f4(VMb), start=False, stop=True)
                mm.then_inc(R["dss_mm"], 1)

        def rsample_act(act, g):
            for tl in range(4):
                i = 4 * g + tl
                act.wait_ge(R["wq_mm"], past(R["wq_mm"], i + 1))
                if i - 1 > 0:
                    act.wait_ge(R["ys_up"], past(R["ys_up"], i - 1))
                act.activation(wqr[i % 2][:, :, :], ps[:, tl % 2, 0:2 * NS].rearrange("p (x t) -> p x t", x=2),
                               ACT.Copy).then_inc(R["wq_cp"], 1)

        def rsample_dve(dve, g):
            dve.wait_ge(R["kt_mm"], past(R["kt_mm"], 8 + g + 1))
            dve.memset(SB1[:, :, :], 0.0).then_inc(R["sb_clr"], 1)
            for tl in range(4):
                i = 4 * g + tl
                dve.wait_ge(R["wtr_mm"], past(R["wtr_mm"], i + 1))
                dve.wait_ge(R["u_cp"], past(R["u_cp"], 8 + g + 1))
                dve.tensor_tensor(Uu[0:NS, tl, :], Uu[0:NS, tl, :], ps[0:NS, 2, 0:P], ALU.add).then_inc(R["sas_up"], 1)
                dve.wait_ge(R["ys_mm"], past(R["ys_mm"], i + 1))
                dve.tensor_tensor(whole(RA)[:, i, TP:T], wqr[i % 2][:, 1, :], ps[:, 4, 0:NS], ALU.add).then_inc(R["ys_up"], 1)
                dve.wait_ge(R["dss_mm"], past(R["dss_mm"], i + 1))
                st = rst(i)
                d = ps[:, 6:8, :].rearrange("p a (b t) -> p (a b) t", t=P)
                for par in range(2):
                    hp = slice(64 * par, 64 * par + 64)
                    q = dve.tensor_tensor(st[hp, :, hp], st[hp, :, hp], d[hp, :, hp], ALU.add)
                q.then_inc(R["ss_add"], 1)
                dve.wait_ge(R["ss_add"], past(R["ss_add"], i + 1))
                if 16 * (i // 2) > 0:
                    dve.wait_ge((R["so0"], R["so1"])[i % 2], past((R["so0"], R["so1"])[i % 2], 16 * (i // 2)))
                for par in range(2):
                    hp = slice(64 * par, 64 * par + 64)
                    q = dve.tensor_tensor(SO[i % 2][hp, :, :], st[hp, :, hp], over(ECE[hp, i, 8:16], 64), ALU.mult)
                q.then_inc(R["ss_up"], 1)

        def rsample_pool(pool, g):
            for tl in range(4):
                i = 4 * g + tl
                pool.wait_ge(R["sas_up"], past(R["sas_up"], i + 1))
                if i > 0:
                    pool.wait_ge(R["dss_mm"], past(R["dss_mm"], i))
                sq = over(mseq[0:NS, :], P)
                pool.tensor_tensor(VMa[0:NS, :, :], Uu[0:NS, tl, :].unsqueeze(1).broadcast_to([NS, NB, P]), sq, ALU.mult)
                pool.tensor_tensor(VMb[0:NS, :, :], Vt[0:NS, tl, :].unsqueeze(1).broadcast_to([NS, NB, P]), sq,
                                   ALU.mult).then_inc(R["vm_up"], 1)

        def rpost_pe(pe):
            pe.wait_ge(R["g2_in"], past(R["g2_in"], 16))
            for m in range(NM):
                if m == 0:
                    pe.wait_ge(R["ys_up"], past(R["ys_up"], NM))
                    pe.wait_ge(R["ss_add"], past(R["ss_add"], NM))
                if m > 0:
                    pe.wait_ge(R["yc"], past(R["yc"], m))
                for half in range(2):
                    mm = pe.matmul(pair(0)[:, half, :], M["headones"], wh(RA, m)[:, half, :], start=True, stop=True)
                mm.then_inc(R["mu_mm"], 1)
                if m - 1 > 0:
                    pe.wait_ge(R["gn3"], past(R["gn3"], m - 1))
                for half in range(2):
                    mm = pe.matmul(pair(2 + m % 2)[:, half, :], g2w[:, m * P:(m + 1) * P], lg[:, half, :], start=True, stop=True)
                mm.then_inc(R["g_mm"], 1)
                pe.wait_ge(R["ysq"], past(R["ysq"], m + 1))
                if m > 0:
                    pe.wait_ge(R["gn_rt"], past(R["gn_rt"], m))
                for half in range(2):
                    mm = pe.matmul(pair(1)[:, half, :], M["headones"], tb[m % 2][:, half, :], start=True, stop=True)
                mm.then_inc(R["var_mm"], 1)

        def rpost_act(act):
            for m in range(NM):
                act.wait_ge(R["yc"], past(R["yc"], m + 1))
                if m - 1 > 0:
                    act.wait_ge(R["var_mm"], past(R["var_mm"], m - 1))
                if m == 0:
                    act.wait_ge(R["ss_up"], past(R["ss_up"], NM))
                    act.wait_ge(R["ys_up"], past(R["ys_up"], NM))
                act.activation(tb[m % 2][:, :, :], wh(r_, m), ACT.Square).then_inc(R["ysq"], 1)
                act.wait_ge(R["var_mm"], past(R["var_mm"], m + 1))
                if m - 1 > 0:
                    act.wait_ge(R["gn1"], past(R["gn1"], m - 1))
                act.activation(tb[2 + m % 2][:, :, :], pair(1), ACT.Sqrt, bias=gneps[:, 0:1], scale=1.0 / 64).then_inc(R["gn_rt"], 1)
            for m in range(NM):
                act.wait_ge(R["gn3"], past(R["gn3"], m + 1))
                act.activation(wh(xh, m), wh(r_, m), ACT.Copy).then_inc(x_hi, 1)

        def rpost_dve(dve):
            for m in range(NM):
                y_ = wh(r_, m)
                dve.wait_ge(R["mu_mm"], past(R["mu_mm"], m + 1))
                dve.scalar_tensor_tensor(y_, pair(0), -1.0 / 64, wh(RA, m), ALU.mult, ALU.add).then_inc(R["yc"], 1)
                dve.wait_ge(R["gn_rt"], past(R["gn_rt"], m + 1))
                q = tb[2 + m % 2][:, :, :]
                dve.reciprocal(q, q).then_inc(R["gn_rs"], 1)
                dve.wait_ge(R["gn_rs"], past(R["gn_rs"], m + 1))
                dve.scalar_tensor_tensor(y_, y_, v(V_LNW + m), q, ALU.mult, ALU.mult).then_inc(R["gn1"], 1)
                dve.wait_ge(R["gn1"], past(R["gn1"], m + 1))
                dve.scalar_tensor_tensor(y_, y_, v(V_LNB + m), wh(BO, m), ALU.add, ALU.add).then_inc(R["gn2"], 1)
                dve.wait_ge(R["gn2"], past(R["gn2"], m + 1))
                dve.wait_ge(R["g_mm"], past(R["g_mm"], m + 1))
                dve.tensor_tensor(y_, y_, pair(2 + m % 2), ALU.mult).then_inc(R["gn3"], 1)
            for m in range(NM):
                dve.wait_ge(x_hi, 8 * SETS["wo"] + m + 1)
                dve.tensor_tensor(wh(xl, m), wh(r_, m), wh(xh, m).bitcast(F32), ALU.subtract).then_inc(x_lo, 1)

        def rwkv_pe(pe):
            norm_pe(pe, 8)
            for i, name in enumerate("rkv"):
                rkv_pe(pe, i, name)
            lora_pe(pe)
            prep_pe(pe)
            with pe.Fori(0, NCH) as c:
                for g in range(2):
                    rstep_pe(pe, 2 * c + g, c, g, P)
            for g in range(2):
                rstep_pe(pe, 8 + g, None, g, NS, smp=g)
                rsample_pe(pe, g)
            rpost_pe(pe)
            out_pe(pe, "wo", 9, 8 * SETS["wo"])
            norm_pe(pe, 9)

        def rwkv_act(act):
            norm_act(act, 8)
            for i, (name, dst) in enumerate((("r", r_), ("k", k_), ("v", v_))):
                if i == 0:
                    act.wait_ge(R["sh_out"], past(R["sh_out"], 16))
                rkv_act(act, i, name, dst)
            lora_act(act)
            prep_act(act)
            with act.Fori(0, NCH) as c:
                for g in range(2):
                    rstep_act(act, 2 * c + g, c, g, P)
            for g in range(2):
                rstep_act(act, 8 + g, None, g, NS, smp=g)
                rsample_act(act, g)
            rpost_act(act)
            out_act(act, "wo", 1, 9, y=y2)
            norm_act(act, 9)
            square_h(act, 10)

        def rwkv_dve(dve):
            shift_dve(dve)
            for i in range(6):
                mix_dve(dve, i)
            prep_dve(dve)
            dve.wait_ge(R["sg_cp"], past(R["sg_cp"], 2 * NM))
            dve.wait_ge(R["ece"], past(R["ece"], NM))
            dve.memset(RS[:, :, :], 0.0).then_inc(R["s_up"], 1)
            dve.memset(Ktt[:, :, :], 0.0).then_inc(R["y_cp"], 1)
            with dve.Fori(0, NCH) as c:
                for g in range(2):
                    rstep_dve(dve, 2 * c + g, c, g, P)
            for g in range(2):
                rstep_dve(dve, 8 + g, None, g, NS, smp=g)
                rsample_dve(dve, g)
            rpost_dve(dve)
            out_dve(dve, "wo", 1, 9)
            post_norm_dve(dve, 9, 1.0, y=y2)

        def rwkv_pool(pool):
            for name in "rkv":
                pool_units(pool, name)
            lora_pool(pool)
            prep_pool(pool)
            with pool.Fori(0, NCH) as c:
                for g in range(2):
                    rstep_pool(pool, 2 * c + g, c, g, P)
            for g in range(2):
                rstep_pool(pool, 8 + g, None, g, NS, smp=g)
                rsample_pool(pool, g)
            pool_units(pool, "wo")

        def rwkv_sp(sp):
            load_units(sp, "r", part=0)
            sp.wait_ge(acc, 2 * BASE["r"])
            sp.dma_start(shin[:, :, :], a["shift"]).then_inc(R["sh_in"], 16)
            sp.dma_start(wa2[:, :], a["wa2"]).then_inc(R["w2_in"], 16)
            sp.wait_ge(R["sh_cp"], past(R["sh_cp"], 1))
            sp.dma_start(a["shift_new"], shout[:, :, :]).then_inc(R["sh_out"], 16)
            load_units(sp, "r", part=1)
            load_units(sp, "k")
            load_units(sp, "v")
            load_units(sp, "lora")
            sp.wait_ge(R["mix"], past(R["mix"], 48))
            sp.wait_ge(x_lo, 8 * SETS["wo"])
            sp.dma_start(reset[:, :], a["reset"]).then_inc(R["rm_in"], 16)
            load_units(sp, "wo", part=0)
            rsample_sp(sp)
            sp.dma_start(g2w[:, :], a["g2"]).then_inc(R["g2_in"], 16)
            load_units(sp, "wo", part=1)

        block = es.enter_context(nc.Block())

        def consts(e):
            e.wait_ge(const_in, 16 * 7)

        @block.sync
        def _(sp):
            for t, n in ((vec, "vec"), (mf, "mf"), (mseq, "mseq"), (mg_f, "mg")):
                sp.dma_start(t[:], a[n]).then_inc(const_in, 16)
            sp.dma_start(h[:, :, :], a["xT"]).then_inc(const_in, 16)
            load_units(sp, "ffn0_in")
            load_units(sp, "ffn0_out")
            gdn_sp(sp)
            load_units(sp, "ffn1_in")
            load_units(sp, "ffn1_out")
            load_units(sp, "ffn2_in")
            load_units(sp, "ffn2_out")
            rwkv_sp(sp)
            load_units(sp, "ffn3_in")
            load_units(sp, "ffn3_out")
            sp.wait_ge(R["so0"], past(R["so0"], 64))
            sp.wait_ge(R["so1"], past(R["so1"], 64))
            sp.wait_ge(h_upd, 8 * 6)
            sp.dma_start(a["yT"], h[:, :, :]).then_inc(out_done, 16)
            sp.wait_ge(out_done, 16)
            sp.wait_ge(S["st_out0"], 64)
            sp.wait_ge(S["st_out1"], 64)

        @block.gpsimd
        def _(pool):
            pool.memset(gneps[:], GN_EPS)
            pool.memset(eps[:], EPS).then_inc(const_in, 16)
            pool.wait_ge(const_in, 96)
            pool.tensor_copy(mg[:], mg_f[:]).then_inc(const_in, 16)
            pool.wait_ge(const_in, 112)
            pool_units(pool, "ffn0_in")
            pool_units(pool, "ffn0_out")
            gdn_pool(pool)
            for f in (1, 2):
                pool_units(pool, f"ffn{f}_in")
                pool_units(pool, f"ffn{f}_out")
            rwkv_pool(pool)
            pool_units(pool, "ffn3_in")
            pool_units(pool, "ffn3_out")

        def pre_ffn_act(act, f):
            for j in range(2):
                split_hi(act, f"ffn{f}_in", 0, j)
            pre_norm_act(act, FFN_NORM[f], SETS[f"ffn{f}_in"], 8 * (FFN_NORM[f] // 2))

        @block.scalar
        def _(act):
            split_hi(act, "ffn0_in", 0, 0)
            split_hi(act, "ffn0_in", 0, 1)
            consts(act)
            square_h(act, 0)
            pre_norm_act(act, 0, SETS["ffn0_in"], 0)
            ffn_act(act, 0)
            norm_act(act, 1)
            square_h(act, 2)
            gdn_act(act)
            pre_ffn_act(act, 1)
            ffn_act(act, 1)
            norm_act(act, 5)
            square_h(act, 6)
            pre_ffn_act(act, 2)
            ffn_act(act, 2)
            norm_act(act, 7)
            square_h(act, 8)
            rwkv_act(act)
            pre_ffn_act(act, 3)
            ffn_act(act, 3)
            norm_act(act, 11)

        @block.vector
        def _(dve):
            consts(dve)
            clear_squares(dve, 0)
            pre_norm_dve(dve, 0, SETS["ffn0_in"])
            ffn_dve(dve, 0)
            post_norm_dve(dve, 1, 0.5)
            gdn_dve(dve)
            for f in (1, 2):
                pre_norm_dve(dve, FFN_NORM[f], SETS[f"ffn{f}_in"], squares=False)
                ffn_dve(dve, f)
                post_norm_dve(dve, FFN_NORM[f] + 1, 0.5)
            rwkv_dve(dve)
            pre_norm_dve(dve, 10, SETS["ffn3_in"], squares=False)
            ffn_dve(dve, 3)
            post_norm_dve(dve, 11, 0.5, last=True)

        @block.tensor
        def _(pe):
            norm_pe(pe, 0)
            ffn_pe(pe, 0)
            norm_pe(pe, 1)
            gdn_pe(pe)
            for f in (1, 2):
                norm_pe(pe, FFN_NORM[f])
                ffn_pe(pe, f)
                norm_pe(pe, FFN_NORM[f] + 1)
            rwkv_pe(pe)
            norm_pe(pe, 10)
            ffn_pe(pe, 3)
            norm_pe(pe, 11)


def lay_out(inp):
    f = lambda x: np.asarray(x)
    x = np.concatenate([f(inp["x_prompt"]).reshape(TP, D), f(inp["x_sample"]).reshape(NS, D)])
    o = {"xT": x.T.reshape(NM, P, 2, HALF).transpose(1, 0, 2, 3).reshape(P, 2 * NM, HALF)}

    def units(w):
        k, n = w.shape
        return w.reshape(k // P, P, n // P, P).transpose(2, 1, 0, 3).reshape(n // P, P, k // P * P)

    def tiles(vv):
        return f(vv).reshape(-1, P).T

    win, wout = f(inp["ffn_w_in"]), f(inp["ffn_w_out"])
    w8, w11 = [], []
    ffn_in, ffn_out = [], []
    for i in range(4):
        gu = units(win[i // 2, i % 2])
        ffn_in.append(np.stack([gu[:NF], gu[NF:]], 1).reshape(2 * NF, P, D))
        w = wout[i // 2, i % 2].reshape(2, KTO, P, NM, P).transpose(3, 0, 2, 1, 4)
        ffn_out.append(w.reshape(2 * NM, P, KTO * P))
    gin = f(inp["gdn_w_in"])[0]
    rkv = np.concatenate([units(f(inp["rwkv_w_rkv"])[0, i]) for i in range(3)])
    wa1 = np.concatenate([f(inp["rwkv_w1"])[0], f(inp["rwkv_a1"])[0]], 1)
    lora = np.concatenate([units(wa1), units(wa1), units(f(inp["rwkv_g1"])[0])])
    o["w8"] = np.concatenate([ffn_in[0], units(gin[:, :4096]), units(f(inp["gdn_w_out"])[0]), ffn_in[1],
                              ffn_in[2], rkv, lora, units(f(inp["rwkv_w_o"])[0]), ffn_in[3]])
    o["w11"] = np.concatenate(ffn_out)
    cw = f(inp["gdn_conv_w"])[0].reshape(4, NQKV, P).transpose(2, 1, 0).reshape(P, NQKV * 4)
    rows = [tiles(inp["norm_g"]), cw, f(inp["gdn_o_norm"])[0].reshape(P, 1), tiles(inp["rwkv_lerp"])]
    rows += [tiles(inp[n]) for n in ("rwkv_w0", "rwkv_a0", "rwkv_k_k", "rwkv_k_a", "rwkv_r_k", "rwkv_ln_w", "rwkv_ln_b")]
    rows += [np.repeat(f(inp["gdn_a_log"]).reshape(1, HG), P, 0), np.repeat(f(inp["gdn_dt_bias"]).reshape(1, HG), P, 0)]
    o["vec"] = np.concatenate(rows, 1)
    o["mf"], o["mg"] = MF, MG
    o["mseq"] = MSEQ
    o["wba"] = gin[:, 4096:].reshape(NM, P, 2 * HG).transpose(1, 0, 2)
    hist = f(inp["state_gdn_conv"])[0].reshape(NB, 3, NQKV, P).transpose(3, 2, 0, 1)
    o["conv_hist"] = hist.reshape(P, NQKV, NB * 3)
    w2a2 = np.concatenate([f(inp["rwkv_w2"])[0], f(inp["rwkv_a2"])[0]])
    o["wa2"], o["g2"] = w2a2, f(inp["rwkv_g2"])[0]
    o["shift"] = f(inp["state_rwkv_shift"])[0].reshape(NB, NM, P).transpose(2, 1, 0)
    o["state_rwkv"] = f(inp["state_rwkv"])[0].reshape(NB, NM, 2, 64, 64).transpose(1, 2, 4, 0, 3).reshape(NM, P, NB, 64)
    o["reset"] = RESET
    o["state_gdn"] = f(inp["state_gdn"])[0].transpose(1, 2, 0, 3)
    return o


_OUTS = {"yT": (P, 2 * NM, HALF), "gdn_s_p": (P, HG, P), "gdn_s_s": (HG, P, NB, P), "conv_new": (P, NQKV, 3 + NB * 3),
         "rwkv_s_p": (P, NM, 64), "rwkv_s_s": (NM, P, NB, 64), "shift_new": (P, NM, 1 + NB)}


def kernel(**inputs):
    import concourse.bacc as bacc
    from concourse.bass_utils import run_bass_kernel_spmd

    nc = bacc.Bacc("TRN2", target_bir_lowering=False, num_devices=1)
    arrays = {n: np.ascontiguousarray(x) for n, x in lay_out(inputs).items()}
    a = {n: nc.dram_tensor(n, x.shape, F32, kind="ExternalInput").ap() for n, x in arrays.items()}
    a.update({n: nc.dram_tensor(n, s, F32, kind="ExternalOutput").ap() for n, s in _OUTS.items()})
    trunk_kernel(nc, a)
    r = run_bass_kernel_spmd(nc, [arrays], core_ids=[0]).results[0]
    y = np.asarray(r["yT"]).reshape(P, NM, T).transpose(2, 1, 0).reshape(T, D)
    cn = np.asarray(r["conv_new"]).transpose(2, 1, 0).reshape(3 + NB * 3, NQKV * P)
    sh = np.asarray(r["shift_new"]).transpose(2, 1, 0).reshape(1 + NB, D)
    rp = np.asarray(r["rwkv_s_p"]).reshape(2, 64, NM, 64).transpose(2, 0, 3, 1).reshape(1, 1, 2 * NM, 64, 64)
    rsm = np.asarray(r["rwkv_s_s"]).reshape(NM, 2, 64, NB, 64).transpose(3, 0, 1, 4, 2).reshape(1, NB, 2 * NM, 64, 64)
    c = np.ascontiguousarray
    return (c(y[:TP].reshape(1, TP, D)), c(y[TP:].reshape(NB, TS, D)),
            c(np.asarray(r["gdn_s_p"]).transpose(1, 0, 2)[None, None]), c(cn[:3][None, None]), c(rp), c(sh[:1][None]),
            c(np.asarray(r["gdn_s_s"]).transpose(2, 0, 1, 3)[None]), c(cn[3:].reshape(1, NB, 3, NQKV * P)), c(rsm),
            c(sh[1:][None]))
```

```python
from contextlib import ExitStack

import numpy as np
import concourse.bass as bass
from concourse import mybir

F32 = mybir.dt.float32
F32R = mybir.dt.float32r
BF16 = mybir.dt.bfloat16
ALU = mybir.AluOpType
ACT = mybir.ActivationFunctionType
ds = bass.ds

P = 128
D = 1024
NM = D // P
TP = 512
NB, TS = 8, 4
NS = NB * TS
T = TP + NS
HALF = T // 2
DFF = 2816
NF = DFF // P
KTO = NF // 2
HG = 8
NCH = TP // P
NQKV = 3 * HG
EXT = TP + 3 + NB * (TS + 3)
EPS = 1e-6
GN_EPS = 64e-5
LEVELS = 7

V_NORM = 0
V_CONV = V_NORM + 12 * NM
V_ONORM = V_CONV + NQKV * 4
V_LERP = V_ONORM + 1
V_W0 = V_LERP + 6 * NM
V_A0 = V_W0 + NM
V_KK = V_A0 + NM
V_KA = V_KK + NM
V_RK = V_KA + NM
V_LNW = V_RK + NM
V_LNB = V_LNW + NM
V_ALOG = V_LNB + NM
V_DT = V_ALOG + HG
NVEC = V_DT + HG

PRODUCTS = [
    ("ffn0_in", 2 * NF, NM), ("ffn0_out", 2 * NM, KTO),
    ("gdn_in", 4 * HG, NM), ("ba", 1, NM), ("gdn_out", NM, NM),
    ("ffn1_in", 2 * NF, NM), ("ffn1_out", 2 * NM, KTO),
    ("ffn2_in", 2 * NF, NM), ("ffn2_out", 2 * NM, KTO),
    ("r", NM, NM), ("k", NM, NM), ("v", NM, NM), ("lora", 3, NM), ("wo", NM, NM),
    ("ffn3_in", 2 * NF, NM), ("ffn3_out", 2 * NM, KTO),
]
BASE, COUNT, KT, SRC = {}, {}, {}, {}
_n, _n8, _n11 = 0, 0, 0
for _name, _units, _kt in PRODUCTS:
    BASE[_name], COUNT[_name], KT[_name] = _n, _units, _kt
    _n += _units
    if _kt == KTO:
        SRC[_name] = _n11
        _n11 += _units
    else:
        SRC[_name] = _n8
        _n8 += _units
N8, N11 = _n8, _n11
SETS = {n: i for i, n in enumerate(
    ["ffn0_in", "gdn_in", "gdn_out", "ffn1_in", "ffn2_in", "x0", "x1", "x2", "x3", "x4", "x5", "wo", "ffn3_in"])}


def masks():
    i = np.arange(P)
    t, s = i[:, None], i[None, :]
    m = {}
    m["ones"] = np.ones((P, P))
    m["ident"] = np.eye(P)
    m["headones"] = (t // 64 == s // 64)
    m["cum128"] = (t <= s)
    m["cum4"] = (t <= s) & (t // 4 == s // 4)
    m["blk4"] = (t // 4 == s // 4)
    lev = [((t >> l) == (s >> l)) & (((t >> (l - 1)) & 1) == 1) & (((s >> (l - 1)) & 1) == 0)
           for l in range(1, LEVELS + 1)]
    lo = {"incl128": (t <= s), "incl64": (t <= s) & (t // 64 == s // 64), "strict64": (t < s) & (t // 64 == s // 64),
          "incl4": (t <= s) & (t // 4 == s // 4), "strict4": (t < s) & (t // 4 == s // 4)}
    one, two = np.zeros((P, 31)), np.zeros((P, 30))
    one[:, 15] = 1
    two[:64, 14] = two[64:, 15] = 1
    f = np.concatenate([np.asarray(v, np.float32) for v in list(m.values()) + [one, two]], 1)
    g = np.concatenate([np.asarray(v, np.float32) for v in lev + list(lo.values())], 1)
    seq = (t // 4 == np.arange(NB)[None, :]).astype(np.float32)
    return f, list(m), g, list(lo), seq


RESET = np.ones((P, T), np.float32)
RESET[:, 0:TP:64] = 0
RESET[:, TP:T:TS] = 0
MF, MF_NAMES, MG, MG_NAMES, MSEQ = masks()


def trunk_kernel(nc, a):
    es = ExitStack()
    with es:
        cursor = [(nc.sbuf_base + 63) // 64 * 64]
        es.enter_context(nc.sbuf_tensor("fence", [P, (nc.sbuf_usable_end - cursor[0] - 128) // 4], F32))
        end = nc.sbuf_usable_end

        def place(name, shape, dt=F32, at=None):
            n = int(np.prod(shape[1:])) * (2 if dt == BF16 else 4)
            n = (n + 31) // 32 * 32
            where = cursor[0] if at is None else at[0]
            assert where + n <= end, (name, where + n, end)
            t = nc.alloc_sbuf_tensor_at(name, list(shape), dt, offset=where)
            if at is None:
                cursor[0] += n
            else:
                at[0] += n
            return t

        vec = place("vec", [P, NVEC])
        mf = place("mf", [P, MF.shape[1]])
        mg = place("mg", [P, MG.shape[1]], BF16)
        mseq = place("mseq", [P, NB])
        eps, gneps = place("eps", [P, 1]), place("gneps", [P, 1])
        M = {n: mf[:, i * P:(i + 1) * P] for i, n in enumerate(MF_NAMES)}
        one_col = mf[:, len(MF_NAMES) * P:len(MF_NAMES) * P + 31]
        two_cols = mf[:, len(MF_NAMES) * P + 31:len(MF_NAMES) * P + 61]
        level_mask = [mg[:, l * P:(l + 1) * P] for l in range(LEVELS)]
        MB = {n: mg[:, (LEVELS + i) * P:(LEVELS + i + 1) * P] for i, n in enumerate(MG_NAMES)}
        h = place("h", [P, 2 * NM, HALF])
        raw = [place(f"raw{i}", [P, KTO * P]) for i in range(4)]
        ECE = place("ECE", [P, NM, 16], F32)
        small_at = cursor[0] - NM * 16 * 4
        tb_at = cursor[0]
        tb = [place(f"tb{i}", [P, 2, HALF]) for i in range(4)]
        rs = place("rs", [P, 2, HALF])
        region = cursor[0]
        at = [region]
        mg_f = place("mg_f", [P, MG.shape[1]], F32, [region + 57344 + 65536])
        whi = [place(f"whi{i}", [P, KTO * P], F32R, at) for i in range(2)]
        wlo = [place(f"wlo{i}", [P, KTO * P], F32R, at) for i in range(2)]
        xh = place("xh", [P, 2 * NM, HALF], F32R, at)
        x_at = at[0] - 2 * NM * HALF * 4
        xl = place("xl", [P, 2 * NM, HALF], F32R, at)
        y = place("y", [P, 2 * NM, HALF], F32, [x_at])
        after_x = at[0]
        mh = place("mh", [P, 2 * NF, HALF], F32R, at)
        ml = place("ml", [P, 2 * NF, HALF], F32R, at)
        ps = es.enter_context(nc.psum_tensor("ps", [P, 8, 512], F32))

        def pair(j):
            return ps[:, 2 * j:2 * j + 2, 0:HALF]

        def v(col):
            return vec[:, col:col + 1]

        def sem(name):
            return es.enter_context(nc.semaphore(name))

        const_in = sem("const_in")
        raw_in = [sem(f"raw_in{i}") for i in range(4)]
        w_hi, w_lo = sem("w_hi"), sem("w_lo")
        acc = sem("acc")
        x_hi, x_lo = sem("x_hi"), sem("x_lo")
        gate_scaled, up_scaled = sem("gate_scaled"), sem("up_scaled")
        silu_done, mult_done = sem("silu_done"), sem("mult_done")
        mid_hi, mid_lo = sem("mid_hi"), sem("mid_lo")
        sq_ready, sq_added = sem("sq_ready"), sem("sq_added")
        nrm_mm, rt_ready, rs_ready = sem("nrm_mm"), sem("rt_ready"), sem("rs_ready")
        h_upd, h_tmp = sem("h_upd"), sem("h_tmp")
        cleared = sem("cleared")
        out_done = sem("out_done")

        def above_zero(count):
            return not isinstance(count, int) or count > 0

        def groups(eng, name, body, peel_first=False, peel_last=False):
            n = COUNT[name] // 4
            lo, hi = (1 if peel_first else 0), (n - 1 if peel_last else n)
            if peel_first:
                body(0, n == 1)
            if hi > lo:
                with eng.Fori(lo, hi) as i:
                    body(i * 4, False)
            if peel_last and not (peel_first and n == 1):
                body(4 * (n - 1), True)

        def load_units(sp, name, part=None):
            base, kt = BASE[name], KT[name]
            src = a["w11"] if kt == KTO else a["w8"]

            def one(u, j):
                n = base + u + j
                slot = (base + j) % 4
                if above_zero(n - 3):
                    sp.wait_ge(w_lo, n - 3)
                sp.dma_start(raw[slot][:, 0:kt * P],
                             src[ds(SRC[name] + u + j, 1)].rearrange("o p c -> (o p) c")).then_inc(raw_in[slot], 16)

            def body(u, last):
                for j in range(4):
                    one(u, j)
            if COUNT[name] < 4:
                for j in range(COUNT[name]):
                    one(0, j)
            elif part is not None:
                body(4 * part, False)
            else:
                groups(sp, name, body, peel_first=(base == 0))

        def split_hi(act, name, u, j):
            base, kt = BASE[name], KT[name]
            n = base + u + j
            slot = (base + j) % 4
            two = (base + j) % 2
            turn = (base + j) // 4 + 1
            cnt = 16 * turn + u * 4
            act.wait_ge(raw_in[slot], cnt)
            if above_zero(2 * (n - 1)):
                act.wait_ge(acc, 2 * (n - 1))
            act.activation(whi[two][:, 0:kt * P], raw[slot][:, 0:kt * P], ACT.Copy).then_inc(w_hi, 1)

        def split_lo(pool, name, u, j):
            base, kt = BASE[name], KT[name]
            n = base + u + j
            slot = (base + j) % 4
            two = (base + j) % 2
            pool.wait_ge(w_hi, n + 1)
            pool.tensor_tensor(wlo[two][:, 0:kt * P], raw[slot][:, 0:kt * P],
                               whi[two][:, 0:kt * P].bitcast(F32), ALU.subtract).then_inc(w_lo, 1)

        def pool_units(pool, name, q=None):
            def body(u, last):
                for j in range(4):
                    split_lo(pool, name, u, j)
            if q is None:
                groups(pool, name, body)
                return
            split_lo(pool, name, 0, 0)
            split_lo(pool, name, 0, 1)
            add_squares_pool(pool, q)
            split_lo(pool, name, 0, 2)
            split_lo(pool, name, 0, 3)
            with pool.Fori(1, COUNT[name] // 4) as i:
                body(4 * i, False)

        def unit_mm(pe, name, u, j, out, hi, lo, k0=0, start=True, stop=True, ready=None):
            base, kt = BASE[name], KT[name]
            n = base + u + j
            two = (base + j) % 2
            pe.wait_ge(w_lo, n + 1)
            for half in range(2):
                for k in range(kt):
                    if ready is not None and half == 0:
                        pe.wait_ge(x_lo, ready + k + 1)
                    wh = whi[two][:, k * P:(k + 1) * P]
                    wl = wlo[two][:, k * P:(k + 1) * P]
                    r = 2 * (k0 + k) + half
                    o = out[:, half, :]
                    pe.matmul(o, wh, hi[:, r, :], start=(start and k == 0), stop=False)
                    pe.matmul(o, wh, lo[:, r, :], start=False, stop=False)
                    mm = pe.matmul(o, wl, hi[:, r, :], start=False, stop=(stop and k == kt - 1))
                mm.then_inc(acc, 1)

        def first_units_mm(pe, name, sett=None):
            base = BASE[name]
            pe.wait_ge(w_lo, base + 2)
            for k in range(NM):
                pe.wait_ge(x_lo, 8 * (SETS[name] if sett is None else sett) + k + 1)
                for j in range(2):
                    wh, wl = (t[(base + j) % 2][:, k * P:(k + 1) * P] for t in (whi, wlo))
                    for half in range(2):
                        o, r = pair(j)[:, half, :], 2 * k + half
                        pe.matmul(o, wh, xh[:, r, :], start=(k == 0), stop=False)
                        pe.matmul(o, wh, xl[:, r, :], start=False, stop=False)
                        mm = pe.matmul(o, wl, xh[:, r, :], start=False, stop=(k == NM - 1))
                        if k == NM - 1:
                            mm.then_inc(acc, 1)

        def norm_pe(pe, q):
            pe.wait_ge(sq_added, 8 * (q + 1))
            for half in range(2):
                mm = pe.matmul(pair(3)[:, half, :], M["ones"], tb[2][:, half, :], start=True, stop=True)
            mm.then_inc(nrm_mm, 1)

        def norm_act(act, q):
            act.wait_ge(nrm_mm, q + 1)
            act.activation(rs[:, :, :], pair(3), ACT.Sqrt, bias=eps[:, 0:1], scale=1.0 / D).then_inc(rt_ready, 1)

        def norm_dve(dve, q):
            dve.wait_ge(rt_ready, q + 1)
            dve.reciprocal(rs[:, :, :], rs[:, :, :]).then_inc(rs_ready, 1)
            dve.wait_ge(rs_ready, q + 1)

        def add_square(dve, q, m):
            dve.wait_ge(sq_ready, 8 * q + m + 1)
            dve.wait_ge(sq_added, 8 * q + m)
            dve.tensor_tensor(tb[2][:, :, :], tb[2][:, :, :], tb[m % 2][:, :, :], ALU.add).then_inc(sq_added, 1)

        def add_squares_pool(pool, q):
            for m in range(NM):
                pool.wait_ge(sq_ready, 8 * q + m + 1)
                if m == 0:
                    pool.tensor_copy(tb[2][:, :, :], tb[0][:, :, :]).then_inc(sq_added, 1)
                else:
                    pool.wait_ge(sq_added, 8 * q + m)
                    pool.tensor_tensor(tb[2][:, :, :], tb[2][:, :, :], tb[m % 2][:, :, :], ALU.add).then_inc(sq_added, 1)

        def clear_squares(dve, q):
            dve.wait_ge(nrm_mm, q)
            dve.memset(tb[2][:, :, :], 0.0).then_inc(cleared, 1)
            dve.wait_ge(cleared, (q + 1) // 2)

        def pre_norm_act(act, q, sett):
            for m in range(NM):
                if q:
                    act.wait_ge(h_upd, 8 * (q // 2 - 1) + m + 1)
                if sett is not None:
                    act.activation(xh[:, 2 * m:2 * m + 2, :], h[:, 2 * m:2 * m + 2, :], ACT.Copy,
                                   scale=v(V_NORM + q * NM + m)).then_inc(x_hi, 1)
                if 8 * q + m - 1 > 0:
                    act.wait_ge(sq_added, 8 * q + m - 1)
                act.activation(tb[m % 2][:, :, :], h[:, 2 * m:2 * m + 2, :], ACT.Square).then_inc(sq_ready, 1)
            norm_act(act, q)

        def pre_norm_low(dve, q, sett, m):
            dve.wait_ge(x_hi, 8 * sett + m + 1)
            dve.scalar_tensor_tensor(xl[:, 2 * m:2 * m + 2, :], h[:, 2 * m:2 * m + 2, :], v(V_NORM + q * NM + m),
                                     xh[:, 2 * m:2 * m + 2, :].bitcast(F32), ALU.mult, ALU.subtract).then_inc(x_lo, 1)

        def post_norm_dve(dve, q, step, sett=None, y=y):
            norm_dve(dve, q)
            base = 8 * (q // 2)
            for m in range(NM):
                if base + m > 0:
                    dve.wait_ge(h_upd, base + m)
                dve.tensor_tensor(tb[3][:, :, :], y[:, 2 * m:2 * m + 2, :], rs[:, :, :], ALU.mult).then_inc(h_tmp, 1)
                dve.wait_ge(h_tmp, base + m + 1)
                dve.scalar_tensor_tensor(h[:, 2 * m:2 * m + 2, :], tb[3][:, :, :], step,
                                         h[:, 2 * m:2 * m + 2, :], ALU.mult, ALU.add).then_inc(h_upd, 1)
                if sett is not None and m:
                    pre_norm_low(dve, q + 1, sett, m - 1)
            if sett is not None:
                pre_norm_low(dve, q + 1, sett, NM - 1)

        def ffn_pe(pe, f):
            name = f"ffn{f}_in"
            nb = NF * f

            first_units_mm(pe, name)
            norm_pe(pe, FFN_NORM[f])
            unit_mm(pe, name, 0, 2, pair(2), xh, xl)
            pe.wait_ge(rt_ready, FFN_NORM[f] + 1)
            unit_mm(pe, name, 0, 3, pair(3), xh, xl)
            with pe.Fori(1, COUNT[name] // 4) as i:
                for j in range(4):
                    pe.wait_ge(up_scaled if j % 2 else gate_scaled, nb + 2 * i + j // 2 - 1)
                    unit_mm(pe, name, 4 * i, j, pair(j), xh, xl)
            name = f"ffn{f}_out"
            q = FFN_NORM[f] + 1

            def out_body(i, first):
                for j in range(4):
                    m2 = j // 2
                    if j % 2 == 0 and not first:
                        pe.wait_ge(sq_ready, 8 * q + 2 * i + m2 - 1)
                    if first and j == 0:
                        pe.wait_ge(mid_lo, nb + KTO)
                    if first and j == 1:
                        pe.wait_ge(mid_lo, nb + NF)
                    unit_mm(pe, name, i * 4, j, pair(m2), mh, ml, k0=KTO * (j % 2), start=(j % 2 == 0), stop=(j % 2 == 1))
            out_body(0, True)
            with pe.Fori(1, 4) as i:
                out_body(i, False)

        FFN_NORM = [0, 4, 6, 10]

        def ffn_act(act, f):
            name = f"ffn{f}_in"
            nb, base = NF * f, BASE[name]

            def body(i, last):
                for j in range(4):
                    n = base + 4 * i + j
                    jj = 2 * i + j // 2
                    if not (last and j >= 2):
                        split_hi(act, name, 4 * i, j + 2)
                    if j % 2 == 0:
                        act.wait_ge(gate_scaled, nb + jj + 1)
                        act.activation(tb[j // 2][:, :, :], tb[j // 2][:, :, :], ACT.Silu).then_inc(silu_done, 1)
                    else:
                        act.wait_ge(mult_done, nb + jj + 1)
                        act.activation(mh[:, ds(2 * jj, 2), :], tb[2 + j // 2][:, :, :], ACT.Copy).then_inc(mid_hi, 1)
            n = COUNT[name] // 4
            body(0, False)
            with act.Fori(1, n - 1) as i:
                body(i, False)
            body(n - 1, True)
            out_act(act, f"ffn{f}_out", 2, FFN_NORM[f] + 1)

        def out_act(act, name, per_tile, q, y=y):
            base = BASE[name]
            for j in range(2):
                split_hi(act, name, 0, j)

            def body(i, last):
                for j in range(4):
                    n = base + 4 * i + j
                    if not (last and j >= 2):
                        split_hi(act, name, 4 * i, j + 2)
                    if j % per_tile == per_tile - 1:
                        mt = j // per_tile
                        m = (4 // per_tile) * i + mt
                        act.wait_ge(acc, 2 * (n + 1))
                        act.activation(y[:, ds(2 * m, 2), :], pair(mt), ACT.Copy, scale=vec[:, ds(V_NORM + q * NM + m, 1)])
                        if not isinstance(i, int) or i or mt >= 2:
                            act.wait_ge(sq_added, 8 * q + m - 1)
                        act.activation(tb[mt % 2][:, :, :], pair(mt), ACT.Square).then_inc(sq_ready, 1)
            n = COUNT[name] // 4
            with act.Fori(0, n - 1) as i:
                body(i, False)
            body(n - 1, True)

        def out_dve(dve, name, per_tile, q):
            clear_squares(dve, q)

            def body(i, last):
                for mt in range(4 // per_tile):
                    m = (4 // per_tile) * i + mt
                    dve.wait_ge(sq_ready, 8 * q + m + 1)
                    dve.wait_ge(sq_added, 8 * q + m)
                    dve.tensor_tensor(tb[2][:, :, :], tb[2][:, :, :], tb[mt % 2][:, :, :], ALU.add).then_inc(sq_added, 1)
            with dve.Fori(0, COUNT[name] // 4) as i:
                body(i, False)

        def ffn_dve(dve, f):
            name = f"ffn{f}_in"
            nb, base = NF * f, BASE[name]
            norm_dve(dve, FFN_NORM[f])
            with dve.Fori(0, NF // 2) as i:
                for two in range(2):
                    jj = 2 * i + two
                    n = base + 4 * i + 2 * two
                    dve.wait_ge(acc, 2 * (n + 1))
                    dve.tensor_tensor(tb[two][:, :, :], pair(2 * two), rs[:, :, :], ALU.mult).then_inc(gate_scaled, 1)
                    dve.wait_ge(acc, 2 * (n + 2))
                    dve.tensor_tensor(tb[2 + two][:, :, :], pair(2 * two + 1), rs[:, :, :], ALU.mult).then_inc(up_scaled, 1)
                    dve.wait_ge(silu_done, nb + jj + 1)
                    dve.wait_ge(up_scaled, nb + jj + 1)
                    dve.tensor_tensor(tb[2 + two][:, :, :], tb[two][:, :, :], tb[2 + two][:, :, :], ALU.mult).then_inc(mult_done, 1)
                    dve.wait_ge(mid_hi, nb + jj + 1)
                    dve.tensor_tensor(ml[:, ds(2 * jj, 2), :], tb[2 + two][:, :, :],
                                      mh[:, ds(2 * jj, 2), :].bitcast(F32), ALU.subtract).then_inc(mid_lo, 1)
            out_dve(dve, f"ffn{f}_out", 2, FFN_NORM[f] + 1)


        def out_pe(pe, name, q, ready):
            def body(i, first):
                for j in range(4):
                    if not first:
                        pe.wait_ge(sq_ready, 8 * q + 4 * i + j - 3)
                    unit_mm(pe, name, i * 4, j, pair(j), xh, xl, ready=ready if first and j == 0 else None)
            body(0, True)
            body(1, False)

        def flat(t):
            return t[:, :, :].rearrange("p a b -> p (a b)")

        def whole(t):
            return t[:, :, :].rearrange("p (m a) b -> p m (a b)", a=2)

        def sum_rows(pe, pr, window, rhs, first, last):
            for half in range(2):
                mm = pe.matmul(pr[0:16, half, :], window, rhs[:, half, :], start=first, stop=last)
            return mm

        def spread_row(pe, pr, rows, t):
            for half in range(2):
                mm = pe.matmul(pr[:, half, :], M["ident"][0:16, t:t + 1].broadcast_to([16, P]), rows[0:16, half, :],
                               start=True, stop=True)
            return mm

        def over(ap, n):
            return ap.unsqueeze(2).broadcast_to([ap.shape[0], ap.shape[1], n])

        def over_heads(ap, n):
            return ap.unsqueeze(1).broadcast_to([ap.shape[0], n, ap.shape[1]])

        def banks(b, n, parts, nt):
            return ps[:, b:b + n, :].rearrange("p a (c t) -> p (a c) t", t=P)[0:parts, :, 0:nt]

        INV = ("zl", "tmm", "tcp", "fmm", "gmm", "fup", "gup")

        def inv_at(I, it, l, a):
            L = I["L"]
            full = min(it, I["calls"]) if isinstance(it, int) else it
            small = it - full if isinstance(it, int) else 0
            return (I["past"][0] + full * (2 * L) + 4 * small + 2 * (l - 1) + a,
                    I["past"][1] + full * (2 * L - 2) + 2 * small + 2 * (l - 2) + a,
                    I["past"][2] + full * (2 * L - 4) + 2 * (l - 2) + a,
                    I["past"][3] + full * (2 * L - 2) + 2 * small + 2 * (l - 1) + a)

        def grp(b, a, nt):
            return b[0:nt, 4 * a:4 * a + 4, 0:nt]

        def bank(b, nt):
            return ps[0:nt, b, :].rearrange("p (c t) -> p c t", t=P)[:, :, 0:nt]

        def inv_pool(pool, I, B, it, levels, nt, first=1):
            for l in range(first, levels + 1):
                for a in range(2):
                    if l > 1:
                        pool.wait_ge(I["tmm"], inv_at(I, it, l - 1, a)[0] + 1)
                    if l == 2:
                        pool.wait_ge(I["gup"], inv_at(I, it, 1, a)[3] + 1)
                    pool.tensor_tensor(grp(B["ZL"], a, nt), grp(B["Z"], a, nt),
                                       over_heads(level_mask[l - 1][0:nt, 0:nt], 4), ALU.mult).then_inc(I["zl"], 1)

        def inv_pe(pe, I, B, it, levels, nt):
            for l in range(1, levels + 1):
                for a in range(2):
                    n, c, g, gu = inv_at(I, it, l, a)
                    pe.wait_ge(I["zl"], n + 1)
                    if l > 1:
                        pe.wait_ge(I["fup"], n - 2 + 1)
                        if l > 2:
                            pe.wait_ge(I["tcp"], c - 2 + 1)
                    for i in range(4):
                        r = M["ident"][0:nt, 0:nt] if l == 1 else B["F"][0:nt, 4 * a + i, 0:nt]
                        mm = pe.matmul(bank(a, nt)[:, i, :], B["ZL"][0:nt, 4 * a + i, 0:nt], r, start=True, stop=True)
                    mm.then_inc(I["tmm"], 1)
                if l == 1:
                    continue
                for a in range(2):
                    n, c, g, gu = inv_at(I, it, l, a)
                    pe.wait_ge(I["tcp"], c + 1)
                    pe.wait_ge(I["gup"], gu - 2 + 1)
                    for i in range(4):
                        mm = pe.matmul(bank(2 + 2 * a, nt)[:, i, :], B["G"][0:nt, 4 * a + i, 0:nt],
                                       B["T"][0:nt, 4 * a + i, 0:nt], start=True, stop=True)
                    mm.then_inc(I["fmm"], 1)
                    if l < levels:
                        for i in range(4):
                            mm = pe.matmul(bank(3 + 2 * a, nt)[:, i, :], B["T"][0:nt, 4 * a + i, 0:nt],
                                           B["G"][0:nt, 4 * a + i, 0:nt], start=True, stop=True)
                        mm.then_inc(I["gmm"], 1)

        def inv_act(act, I, B, it, levels, nt):
            for l in range(2, levels + 1):
                for a in range(2):
                    n, c, g, gu = inv_at(I, it, l, a)
                    act.wait_ge(I["tmm"], n + 1)
                    if l > 2:
                        act.wait_ge(I["gmm"], g - 2 + 1)
                    act.activation(grp(B["T"], a, nt), bank(a, nt), ACT.Copy).then_inc(I["tcp"], 1)

        def inv_dve(dve, I, B, it, levels, nt):
            ident = over_heads(M["ident"][0:nt, 0:nt], 4)
            for a in range(2):
                n, c, g, gu = inv_at(I, it, 1, a)
                dve.wait_ge(I["tmm"], n + 1)
                dve.tensor_tensor(grp(B["F"], a, nt), ident, bank(a, nt), ALU.subtract).then_inc(I["fup"], 1)
                dve.tensor_tensor(grp(B["G"], a, nt), ident, grp(B["ZL"], a, nt), ALU.subtract).then_inc(I["gup"], 1)
            for l in range(2, levels + 1):
                for a in range(2):
                    n, c, g, gu = inv_at(I, it, l, a)
                    dve.wait_ge(I["fmm"], c + 1)
                    dve.wait_ge(I["fup"], n - 2 + 1)
                    dve.tensor_tensor(grp(B["F"], a, nt), grp(B["F"], a, nt), bank(2 + 2 * a, nt), ALU.subtract).then_inc(I["fup"], 1)
                    if l < levels:
                        dve.wait_ge(I["gmm"], g + 1)
                        dve.wait_ge(I["gup"], gu - 2 + 1)
                        dve.tensor_tensor(grp(B["G"], a, nt), grp(B["G"], a, nt), bank(3 + 2 * a, nt), ALU.subtract).then_inc(I["gup"], 1)

        at = [after_x]
        qkv = place("qkv", [P, 2 * NQKV, HALF], F32, at)
        zg = place("zg", [P, 2 * HG, HALF], F32, at)
        tail = at[0]
        ext = [place(f"ext{i}", [P, 576], F32, at) for i in range(2)]
        cb = [place(f"cb{i}", [P, 576], F32, at) for i in range(2)]
        hist = place("hist", [P, NQKV, NB * 3], F32, at)
        cnew = place("cnew", [P, NQKV, 3 + NB * 3], F32, at)
        at = [region]
        KV = place("KV", [P, 2, HG, P], F32, at)
        B = dict(**{n: place("g" + n, [P, HG, P], F32, at)
                               for n in ("E", "AT", "Z", "ZL", "T", "F", "G", "BV", "BK", "KD", "U", "EG")})
        assert at[0] <= after_x
        at = [tail]
        ot = place("ot", [P, 2 * HG, HALF], F32, at)
        Sst = place("Sst", [P, HG, P], F32, at)
        SG = place("SG", [P, HG, P], F32, at)
        gs = {n: place("gs_" + n, [P, 5, HG], F32, at) for n in ("beta", "g", "gc", "bE", "egd", "tmp", "tmp2")}
        at = [small_at]
        ba = place("ba", [P, 5, 2 * HG], F32, at)
        gst = place("gst", [P, HG], F32, at)
        wqs = [tb[i][:, 0, 0:2 * NS].rearrange("p (x t) -> p x t", x=2) for i in range(2)]
        y2 = place("y2", [P, 2 * NM, HALF], F32, [after_x])
        counted = {
            NCH + 1: ("kst", "vst", "gst_r", "gcb_mm", "kk_mm", "vt_mm", "kt_mm", "e_sub", "e_min", "e_max", "eg_exp", "dt_exp",
                      "dn_exp", "z_mul", "at_mul", "bv_up", "bk_up", "kd_up", "z_beta", "at_mask", "qd_up", "wt_mm", "u_mm",
                      "wt_cp", "u_cp"),
            NCH: ("ws_mm", "vn_up", "o_mm", "kv_mm", "sg_up"),
            HG: ("wq_mm", "wq_cp", "wtr_mm", "vns_up", "oa_mm", "oa_up", "vm_up", "kvs_mm", "sgs_up", "sts_up",
                 "on_sq", "on_mm", "on_n", "on_f32", "z_scaled", "z_ready"),
            NQKV: ("ext_ready", "conv_done", "qkv_ready"),
        }
        others = ("hist_in", "cv", "l2_sq", "l2_mm", "l2_rt", "l2_rs", "l2_done", "l2_bc", "on_rt", "on_rs", "on_bc", "ba_mm",
                  "gdn_act", "gdn_dve", "gdn_pe", "o_cp", "s_up", "st_in0", "st_in1", "st_out0", "st_out1", "cn_out", "sp_out")
        S = {n: sem(n) for n in sum(counted.values(), ()) + others}
        GI = dict(L=LEVELS, calls=NCH, past=(0, 0, 0, 0), **{n: sem("inv_" + n) for n in INV})

        def conv_window(t, lo, n):
            return t[:, TP + 3:EXT].rearrange("p (b t) -> p b t", b=NB)[:, :, lo:lo + n]

        def gdn_in_act(act):
            base = BASE["gdn_in"]

            def silu_out(idx, e):
                act.wait_ge(S["cv"], 5 * (idx + 1))
                act.activation(whole(qkv)[:, ds(idx, 1), 0:TP].rearrange("p o t -> p (o t)"), cb[e][:, 0:TP], ACT.Silu)
                act.activation(whole(qkv)[:, ds(idx, 1), TP:T].rearrange("p o (b t) -> p (o b) t", b=NB),
                               conv_window(cb[e], 0, TS), ACT.Silu).then_inc(S["qkv_ready"], 1)

            def body(i, first):
                for j in range(4):
                    idx = 4 * i + j
                    e = j % 2
                    split_hi(act, "gdn_in", 4 * i, j + 2)
                    if not (first and j == 0):
                        silu_out(idx - 1, 1 - e)
            body(0, True)
            with act.Fori(1, NQKV // 4) as i:
                body(i, False)
            silu_out(NQKV - 1, 1)
            for i in range(2):
                for j in range(4):
                    idx = NQKV + 4 * i + j
                    if 4 * i + j < 6:
                        split_hi(act, "gdn_in", idx - j, j + 2)
                    if 4 * i + j == 6:
                        split_hi(act, "ba", 0, 0)
                    m = 4 * i + j
                    for t in (2 * m, 2 * m + 1):
                        act.wait_ge(S["qkv_ready"], t + 1)
                        if t > 1:
                            act.wait_ge(S["l2_mm"], t - 1)
                        act.activation(tb[t % 2][:, :, :], qkv[:, 2 * t:2 * t + 2, :], ACT.Square).then_inc(S["l2_sq"], 1)
                    act.wait_ge(S["z_scaled"], m + 1)
                    act.activation(zg[:, 2 * m:2 * m + 2, :], zg[:, 2 * m:2 * m + 2, :], ACT.Silu).then_inc(S["z_ready"], 1)

        def gdn_in_dve(dve):
            for e in range(2):
                dve.memset(ext[e][:, 0:3], 0.0)
            dve.wait_ge(S["hist_in"], 16)

            def body(i, first):
                for j in range(4):
                    idx = 4 * i + j
                    e = j % 2

                    def col(tap):
                        return vec[:, ds(V_CONV + 4 * idx + tap, 1)]
                    dve.wait_ge(acc, 2 * (BASE["gdn_in"] + idx + 1))
                    if above_zero(idx - 1):
                        dve.wait_ge(S["conv_done"], idx - 1)
                    dve.tensor_tensor(ext[e][:, 3:3 + HALF], pair(j)[:, 0, :], rs[:, 0, :], ALU.mult)
                    dve.tensor_tensor(ext[e][:, 3 + HALF:3 + TP], pair(j)[:, 1, 0:TP - HALF], rs[:, 1, 0:TP - HALF], ALU.mult)
                    dve.tensor_tensor(conv_window(ext[e], 3, TS),
                                      pair(j)[:, 1, TP - HALF:HALF].rearrange("p (b t) -> p b t", b=NB),
                                      rs[:, 1, TP - HALF:HALF].rearrange("p (b t) -> p b t", b=NB),
                                      ALU.mult).then_inc(S["ext_ready"], 1)
                    dve.wait_ge(S["ext_ready"], idx + 1)
                    dve.tensor_copy(conv_window(ext[e], 0, 3),
                                    hist[:, ds(idx, 1), :].rearrange("p o (b t) -> p (o b) t", b=NB)).then_inc(S["cv"], 1)
                    dve.wait_ge(S["cv"], 5 * idx + 1)
                    if above_zero(idx - 1):
                        dve.wait_ge(S["qkv_ready"], idx - 1)
                    n = EXT - 3
                    dve.tensor_scalar(cb[e][:, 0:n], ext[e][:, 0:n], col(0), None, ALU.mult).then_inc(S["cv"], 1)
                    for tap in range(1, 4):
                        dve.wait_ge(S["cv"], 5 * idx + 1 + tap)
                        dve.scalar_tensor_tensor(cb[e][:, 0:n], ext[e][:, tap:tap + n], col(tap), cb[e][:, 0:n],
                                                 ALU.mult, ALU.add).then_inc(S["cv"], 1)
                    cn = cnew[:, ds(idx, 1), :]
                    dve.tensor_copy(cn[:, :, 0:3].rearrange("p o t -> p (o t)"), ext[e][:, TP:TP + 3])
                    dve.tensor_copy(cn[:, :, 3:3 + NB * 3].rearrange("p o (b t) -> p (o b) t", b=NB),
                                    conv_window(ext[e], TS, 3)).then_inc(S["conv_done"], 1)
            body(0, True)
            with dve.Fori(1, NQKV // 4) as i:
                body(i, False)
            for m in range(HG):
                dve.wait_ge(acc, 2 * (BASE["gdn_in"] + NQKV + m + 1))
                dve.tensor_tensor(zg[:, 2 * m:2 * m + 2, :], pair(m % 3), rs[:, :, :], ALU.mult).then_inc(S["z_scaled"], 1)

        def gdn_in_pe(pe):
            first_units_mm(pe, "gdn_in")
            norm_pe(pe, 2)
            unit_mm(pe, "gdn_in", 0, 2, pair(2), xh, xl)
            pe.wait_ge(rt_ready, 3)
            unit_mm(pe, "gdn_in", 0, 3, pair(3), xh, xl)
            with pe.Fori(1, NQKV // 4) as i:
                for j in range(4):
                    pe.wait_ge(S["ext_ready"], 4 * i + j - 3)
                    unit_mm(pe, "gdn_in", i * 4, j, pair(j), xh, xl)
            for m in range(HG):
                if m < 3:
                    pe.wait_ge(S["ext_ready"], NQKV - 3 + m)
                else:
                    pe.wait_ge(S["z_scaled"], m - 2)
                unit_mm(pe, "gdn_in", NQKV + m - m % 4, m % 4, pair(m % 3), xh, xl)
                if m == 0:
                    pe.wait_ge(S["ext_ready"], NQKV)
                for t in (2 * m, 2 * m + 1):
                    pe.wait_ge(S["l2_sq"], t + 1)
                    sum_rows(pe, pair(3), one_col[:, 15 - t:31 - t], tb[t % 2], t == 0, t == 15).then_inc(S["l2_mm"], 1)

        def l2_act(act):
            act.wait_ge(S["l2_mm"], 2 * HG)
            act.activation(tb[2][0:16, :, :], pair(3)[0:16], ACT.Sqrt, bias=eps[0:16, 0:1]).then_inc(S["l2_rt"], 1)

        def l2_spread(pe, tiles):
            for t in tiles:
                if t == 0:
                    pe.wait_ge(S["z_scaled"], HG)
                    pe.wait_ge(S["l2_rs"], 1)
                if t > 1:
                    pe.wait_ge(S["l2_done"], t - 1)
                spread_row(pe, pair(t % 2), tb[2], t).then_inc(S["l2_bc"], 1)

        def l2_dve(dve, tiles):
            for t in tiles:
                dve.wait_ge(S["l2_bc"], t + 1)
                q = qkv[:, 2 * t:2 * t + 2, :]
                dve.scalar_tensor_tensor(q, q, P ** -0.5 if t < HG else 1.0, pair(t % 2), ALU.mult, ALU.mult).then_inc(S["l2_done"], 1)

        PIECES = [(P, slice(0, NCH), list(range(NCH))), (NS, slice(NCH, NCH + 1), [NCH])]

        def ba_pe_first(pe):
            unit_mm(pe, "ba", 0, 0, pair(2), xh, xl)

        def ba_pe_transpose(pe):
            pe.wait_ge(S["gdn_dve"], 2)
            for it in range(NCH + 1):
                nt = P if it < NCH else NS
                mm = pe.transpose(ps[0:nt, 4, 16 * it:16 * it + 16], flat(tb[3])[0:16, it * P:it * P + nt], M["ident"][0:16, 0:16])
            mm.then_inc(S["ba_mm"], 1)

        def ba_pe_second(pe):
            pe.wait_ge(S["gdn_dve"], 7)
            for nt, sl, its in PIECES:
                cum, blk = (M["cum128"], M["ones"]) if nt == P else (M["cum4"], M["blk4"])
                for it in its:
                    pe.matmul(ps[0:nt, 5, 8 * it:8 * it + 8], cum[0:nt, 0:nt], gs["g"][0:nt, it, :], start=True, stop=True)
                    mm = pe.matmul(ps[0:nt, 5, 64 + 8 * it:72 + 8 * it], blk[0:nt, 0:nt], gs["g"][0:nt, it, :],
                                   start=True, stop=True)
            mm.then_inc(S["gdn_pe"], 1)

        def ba_act2(act):
            act.wait_ge(S["gdn_dve"], 3)
            act.activation(gs["beta"][:, :, :], ba[:, :, 0:HG], ACT.Sigmoid).then_inc(S["gdn_act"], 1)
            act.activation(gs["tmp2"][:, :, :], gs["tmp"][:, :, :], ACT.Abs).then_inc(S["gdn_act"], 1)
            act.wait_ge(S["gdn_act"], 2)
            act.activation(gs["tmp2"][:, :, :], gs["tmp2"][:, :, :], ACT.Exp, scale=-1.0).then_inc(S["gdn_act"], 1)
            act.wait_ge(S["gdn_act"], 3)
            act.activation(gs["tmp2"][:, :, :], gs["tmp2"][:, :, :], ACT.Ln, bias=1.0).then_inc(S["gdn_act"], 1)
            act.activation(gs["gc"][:, 0, :], vec[:, V_ALOG:V_ALOG + HG], ACT.Exp).then_inc(S["gdn_act"], 1)
            act.wait_ge(S["gdn_dve"], 9)
            act.activation(gs["bE"][:, :, :], gs["gc"][:, :, :], ACT.Exp)
            act.activation(gs["egd"][:, :, :], gs["egd"][:, :, :], ACT.Exp).then_inc(S["gdn_act"], 1)

        def l2_ba_dve(dve):
            d = S["gdn_dve"]
            dve.memset(ba[:, :, :], 0.0).then_inc(d, 1)
            dve.wait_ge(acc, 2 * (BASE["ba"] + 1))
            dve.tensor_tensor(tb[3][0:16, :, :], pair(2)[0:16], rs[0:16, :, :], ALU.mult).then_inc(d, 1)
            dve.wait_ge(S["l2_rt"], 1)
            dve.reciprocal(tb[2][0:16, :, :], tb[2][0:16, :, :]).then_inc(S["l2_rs"], 1)
            dve.wait_ge(S["ba_mm"], 1)
            dve.wait_ge(d, 1)
            p4 = ps[:, 4, 0:16 * (NCH + 1)].rearrange("p (i c) -> p i c", c=16)
            dve.tensor_copy(ba[:, 0:NCH, :], p4[:, 0:NCH, :])
            dve.tensor_copy(ba[0:NS, NCH, :], p4[0:NS, NCH, :]).then_inc(S["l2_rs"], 1)
            dve.wait_ge(S["l2_rs"], 2)
            dt = vec[:, V_DT:V_DT + HG].unsqueeze(1).broadcast_to([P, NCH + 1, HG])
            dve.tensor_tensor(gs["tmp"][:, :, :], ba[:, :, HG:2 * HG], dt, ALU.add).then_inc(d, 1)
            l2_dve(dve, range(4))
            dve.wait_ge(S["gdn_act"], 5)
            dve.wait_ge(d, 3)
            dve.tensor_scalar(gs["tmp"][:, :, :], gs["tmp"][:, :, :], 0.0, None, ALU.max).then_inc(d, 1)
            dve.wait_ge(d, 4)
            dve.tensor_tensor(gs["g"][:, :, :], gs["tmp"][:, :, :], gs["tmp2"][:, :, :], ALU.add).then_inc(d, 1)
            dve.wait_ge(d, 5)
            ea = gs["gc"][:, 0, :].unsqueeze(1).broadcast_to([P, NCH + 1, HG])
            dve.tensor_tensor(gs["g"][:, :, :], gs["g"][:, :, :], ea, ALU.mult).then_inc(d, 1)
            dve.wait_ge(d, 6)
            dve.tensor_scalar(gs["g"][:, :, :], gs["g"][:, :, :], -1.0, None, ALU.mult).then_inc(d, 1)
            l2_dve(dve, range(4, 12))
            dve.wait_ge(S["gdn_pe"], 1)
            dve.memset(gs["gc"][:, :, :], 0.0)
            dve.memset(gs["egd"][:, :, :], 0.0).then_inc(d, 1)
            dve.wait_ge(d, 8)
            for n, (nt, sl, its) in enumerate(PIECES):
                c = ps[0:nt, 5, 0:40].rearrange("p (i c) -> p i c", c=HG)[:, sl, :]
                dve.tensor_copy(gs["gc"][0:nt, sl, :], c)
                i = dve.tensor_copy(gs["egd"][0:nt, sl, :], ps[0:nt, 5, 64:104].rearrange("p (i c) -> p i c", c=HG)[:, sl, :])
            i.then_inc(S["l2_rs"], 1)
            dve.wait_ge(S["l2_rs"], 3)
            dve.tensor_tensor(gs["egd"][:, :, :], gs["egd"][:, :, :], gs["gc"][:, :, :], ALU.subtract).then_inc(d, 1)
            dve.memset(Sst[:, :, :], 0.0).then_inc(S["s_up"], 1)
            dve.memset(SG[:, :, :], 0.0).then_inc(S["o_cp"], 1)
            l2_dve(dve, range(12, 2 * HG))
            dve.wait_ge(S["gdn_act"], 6)
            dve.tensor_tensor(gs["bE"][:, :, :], gs["bE"][:, :, :], gs["beta"][:, :, :], ALU.mult).then_inc(d, 1)

        def tok(t, it, nt, lo, hi):
            if nt == P:
                return whole(t)[:, lo:hi, ds(it * P, P)]
            return whole(t)[:, lo:hi, TP:T]

        def sc(n, it, nt):
            return gs[n][0:nt, ds(it, 1), :].rearrange("p o h -> p (o h)")

        def chunk_act(act, it, nt):
            act.wait_ge(S["l2_done"], 2 * HG)
            act.wait_ge(S["s_up"], it + 1)
            act.wait_ge(S["o_cp"], it + 1)
            act.activation(KV[:, 0, :, 0:nt], tok(qkv, it, nt, HG, 2 * HG), ACT.Copy).then_inc(S["kst"], 1)
            act.wait_ge(S["e_sub"], it + 1)
            act.activation(B["EG"][:, :, 0:nt], banks(0, 2, P, nt), ACT.Exp).then_inc(S["eg_exp"], 1)
            act.wait_ge(S["e_min"], it + 1)
            act.activation(B["AT"][0:nt, :, 0:nt], B["AT"][0:nt, :, 0:nt], ACT.Exp).then_inc(S["dt_exp"], 1)
            act.wait_ge(S["e_max"], it + 1)
            act.activation(B["E"][0:nt, :, 0:nt], B["E"][0:nt, :, 0:nt], ACT.Exp, scale=-1.0).then_inc(S["dn_exp"], 1)
            inv_act(act, GI, B, it, LEVELS if nt == P else 2, nt)
            act.wait_ge(S["wt_mm"], it + 1)
            act.activation(KV[:, 0, :, 0:nt], banks(6, 2, P, nt), ACT.Copy).then_inc(S["wt_cp"], 1)
            act.wait_ge(S["u_mm"], it + 1)
            act.activation(B["U"][0:nt, :, :], banks(0, 2, nt, P), ACT.Copy).then_inc(S["u_cp"], 1)
            if nt == P:
                act.wait_ge(S["o_mm"], it + 1)
                act.activation(tok(ot, it, nt, 0, HG), banks(4, 2, P, P), ACT.Copy).then_inc(S["o_cp"], 1)

        def chunk_pool(pool, it, nt):
            pool.wait_ge(S["l2_done"], 2 * HG)
            pool.wait_ge(S["gdn_dve"], 10)
            pool.wait_ge(S["s_up"], it + 1)
            pool.wait_ge(S["o_cp"], it + 1)
            pool.tensor_copy(gst[0:nt, :], sc("g", it, nt)).then_inc(S["gst_r"], 1)
            pool.tensor_copy(KV[:, 1, :, 0:nt], tok(qkv, it, nt, 2 * HG, 3 * HG)).then_inc(S["vst"], 1)
            pool.wait_ge(S["z_mul"], it + 1)
            pool.tensor_tensor(B["Z"][0:nt, :, 0:nt], B["Z"][0:nt, :, 0:nt], over(sc("beta", it, nt), nt), ALU.mult).then_inc(S["z_beta"], 1)
            pool.wait_ge(S["z_beta"], it + 1)
            inv_pool(pool, GI, B, it, 1, nt)
            pool.wait_ge(S["at_mul"], it + 1)
            pool.tensor_tensor(B["AT"][0:nt, :, 0:nt], B["AT"][0:nt, :, 0:nt],
                               over_heads(MB["incl128" if nt == P else "incl4"][0:nt, 0:nt], HG), ALU.mult).then_inc(S["at_mask"], 1)
            pool.wait_ge(S["vt_mm"], it + 1)
            pool.wait_ge(S["eg_exp"], it + 1)
            pool.tensor_tensor(KV[:, 1, :, 0:nt], tok(qkv, it, nt, 0, HG), B["EG"][:, :, 0:nt], ALU.mult).then_inc(S["qd_up"], 1)
            inv_pool(pool, GI, B, it, LEVELS if nt == P else 2, nt, first=2)
            if nt == P:
                pool.tensor_tensor(SG[:, :, :], Sst[:, :, :], B["EG"][:, :, P - 1:P].broadcast_to([P, HG, P]),
                                   ALU.mult).then_inc(S["sg_up"], 1)

        KQ = ps[:, 2:6, :].rearrange("p b (h x t) -> p (b h) x t", h=2, x=2)

        def chunk_dve(dve, it, nt):
            dve.wait_ge(S["gcb_mm"], it + 1)
            dve.wait_ge(S["s_up"], it + 1)
            dve.wait_ge(S["o_cp"], it + 1)
            e, at_ = B["E"][0:nt, :, 0:nt], B["AT"][0:nt, :, 0:nt]
            dve.tensor_tensor(e, banks(0, 2, nt, nt), over(sc("gc", it, nt), nt), ALU.subtract).then_inc(S["e_sub"], 1)
            dve.wait_ge(S["e_sub"], it + 1)
            dve.tensor_scalar(at_, e, 0.0, None, ALU.min).then_inc(S["e_min"], 1)
            dve.wait_ge(S["e_min"], it + 1)
            dve.tensor_scalar(e, e, 0.0, None, ALU.max).then_inc(S["e_max"], 1)
            dve.wait_ge(S["kk_mm"], it + 1)
            dve.wait_ge(S["dn_exp"], it + 1)
            dve.tensor_tensor(B["Z"][0:nt, :, 0:nt], KQ[0:nt, :, 1, 0:nt], e, ALU.mult).then_inc(S["z_mul"], 1)
            dve.tensor_tensor(at_, KQ[0:nt, :, 0, 0:nt], at_, ALU.mult).then_inc(S["at_mul"], 1)
            dve.wait_ge(S["vt_mm"], it + 1)
            dve.tensor_tensor(B["BV"][0:nt, :, :], banks(6, 2, nt, P), over(sc("beta", it, nt), P), ALU.mult).then_inc(S["bv_up"], 1)
            dve.wait_ge(S["kt_mm"], it + 1)
            dve.tensor_tensor(B["BK"][0:nt, :, :], banks(0, 2, nt, P), over(sc("bE", it, nt), P), ALU.mult).then_inc(S["bk_up"], 1)
            dve.tensor_tensor(B["KD"][0:nt, :, :], banks(0, 2, nt, P), over(sc("egd", it, nt), P), ALU.mult).then_inc(S["kd_up"], 1)
            inv_dve(dve, GI, B, it, LEVELS if nt == P else 2, nt)
            if nt == P:
                dve.wait_ge(S["ws_mm"], it + 1)
                dve.wait_ge(S["u_cp"], it + 1)
                dve.tensor_tensor(B["U"][:, :, :], B["U"][:, :, :], banks(2, 2, P, P), ALU.subtract).then_inc(S["vn_up"], 1)
                dve.wait_ge(S["o_mm"], it + 1)
                dve.wait_ge(S["sg_up"], it + 1)
                dve.tensor_tensor(Sst[:, :, :], banks(6, 2, P, P), SG[:, :, :], ALU.add).then_inc(S["s_up"], 1)

        def chunk_pe(pe, it, nt):
            pe.wait_ge(S["gst_r"], it + 1)
            pe.wait_ge(S["s_up"], it + 1)
            pe.wait_ge(S["o_cp"], it + 1)
            cum = M["cum128" if nt == P else "cum4"]
            for hh in range(HG):
                mm = pe.matmul(ps[:, hh // 4, (hh % 4) * P:(hh % 4) * P + nt],
                               gst[0:nt, hh:hh + 1].broadcast_to([nt, P]), cum[0:nt, 0:nt], start=True, stop=True)
            mm.then_inc(S["gcb_mm"], 1)
            pe.wait_ge(S["kst"], it + 1)
            for hh in range(HG):
                rhs = tok(qkv, it, nt, 0, 2 * HG).rearrange("p (x h) t -> p x h t", x=2)[:, :, hh, :]
                mm = pe.matmul(KQ[0:nt, hh, :, 0:nt], KV[:, 0, hh, 0:nt], rhs, start=True, stop=True)
            mm.then_inc(S["kk_mm"], 1)
            pe.wait_ge(S["vst"], it + 1)
            for hh in range(HG):
                mm = pe.transpose(ps[0:nt, 6 + hh // 4, (hh % 4) * P:(hh % 4 + 1) * P], KV[:, 1, hh, 0:nt], M["ident"])
            mm.then_inc(S["vt_mm"], 1)
            pe.wait_ge(S["eg_exp"], it + 1)
            for hh in range(HG):
                mm = pe.transpose(ps[0:nt, hh // 4, (hh % 4) * P:(hh % 4 + 1) * P], KV[:, 0, hh, 0:nt], M["ident"])
            mm.then_inc(S["kt_mm"], 1)
            pe.wait_ge(S["kd_up"], it + 1)
            pe.wait_ge(S["at_mul"], it + 1)
            levels = LEVELS if nt == P else 2
            inv_pe(pe, GI, B, it, levels, nt)
            for a in range(2):
                pe.wait_ge(GI["fup"], inv_at(GI, it, levels, a)[0] + 1)
            for hh in range(HG):
                mm = pe.matmul(ps[:, 6 + hh // 4, (hh % 4) * P:(hh % 4) * P + nt], B["BK"][0:nt, hh, :],
                               B["F"][0:nt, hh, 0:nt], start=True, stop=True)
            mm.then_inc(S["wt_mm"], 1)
            for hh in range(HG):
                mm = pe.matmul(ps[0:nt, hh // 4, (hh % 4) * P:(hh % 4 + 1) * P], B["F"][0:nt, hh, 0:nt],
                               B["BV"][0:nt, hh, :], start=True, stop=True)
            mm.then_inc(S["u_mm"], 1)
            pe.wait_ge(S["wt_cp"], it + 1)
            pe.wait_ge(S["qd_up"], it + 1)
            pe.wait_ge(S["at_mask"], it + 1)
            if nt == P:
                for hh in range(HG):
                    mm = pe.matmul(ps[:, 2 + hh // 4, (hh % 4) * P:(hh % 4 + 1) * P], KV[:, 0, hh, :], Sst[:, hh, :],
                                   start=True, stop=True)
                mm.then_inc(S["ws_mm"], 1)
                pe.wait_ge(S["vn_up"], it + 1)
                for hh in range(HG):
                    mm = pe.matmul(ps[:, 6 + hh // 4, (hh % 4) * P:(hh % 4 + 1) * P], B["KD"][:, hh, :], B["U"][:, hh, :],
                                   start=True, stop=True)
                mm.then_inc(S["kv_mm"], 1)
                for hh in range(HG):
                    o = ps[:, 4 + hh // 4, (hh % 4) * P:(hh % 4 + 1) * P]
                    pe.matmul(o, Sst[:, hh, :], KV[:, 1, hh, :], start=True, stop=False)
                    mm = pe.matmul(o, B["U"][:, hh, :], B["AT"][:, hh, :], start=False, stop=True)
                mm.then_inc(S["o_mm"], 1)

        STB = [Sst, SG]
        STN = [B["G"], B["T"]]

        def seqs(e):
            return ps[:, 6:8, :].rearrange("p a (b t) -> p (a b) t", t=P)

        def sstep_sp(sp):
            sin, sout = [S["st_in0"], S["st_in1"]], [S["st_out0"], S["st_out1"]]
            sp.wait_ge(S["s_up"], NCH + 1)
            sp.dma_start(a["gdn_s_p"], Sst[:, :, :]).then_inc(S["sp_out"], 16)
            sp.wait_ge(S["sp_out"], 16)
            for hh in range(2):
                sp.dma_start(STB[hh][:, :, :], a["state_gdn"][hh]).then_inc(sin[hh], 16)
            for hh in range(HG):
                if hh + 2 < HG:
                    sp.wait_ge(S["wq_mm"], hh + 1)
                    sp.wait_ge(S["sgs_up"], hh + 1)
                    sp.dma_start(STB[hh % 2][:, :, :], a["state_gdn"][hh + 2]).then_inc(sin[hh % 2], 16)
                sp.wait_ge(S["sts_up"], hh + 1)
                sp.dma_start(a["gdn_s_s"][hh], STN[hh % 2][:, :, :]).then_inc(sout[hh % 2], 16)

        def st_arrived(eng, hh):
            eng.wait_ge([S["st_in0"], S["st_in1"]][hh % 2], 16 * (hh // 2 + 1))

        def sstep_pe(pe):
            def read(hh):
                st_arrived(pe, hh)
                pe.wait_ge(S["u_cp"], NCH + 1)
                if hh > 1:
                    pe.wait_ge(S["oa_up"], hh - 1)
                wq = ps[:, hh % 2, 0:2 * NS].rearrange("p (x t) -> p x t", x=2)
                for b in range(NB):
                    mm = pe.matmul(wq[:, :, TS * b:TS * b + TS], STB[hh % 2][:, b, :], KV[:, :, hh, TS * b:TS * b + TS],
                                   start=True, stop=True)
                mm.then_inc(S["wq_mm"], 1)
                pe.wait_ge(S["wq_cp"], hh + 1)
                pe.transpose(ps[0:NS, 2 + hh % 2, 0:P], wqs[hh % 2][:, 0, :], M["ident"]).then_inc(S["wtr_mm"], 1)
            read(0)
            for hh in range(HG):
                pe.wait_ge(S["vns_up"], hh + 1)
                pe.matmul(ps[:, 4 + hh % 2, 0:NS], B["U"][0:NS, hh, :], B["AT"][0:NS, hh, 0:NS],
                          start=True, stop=True).then_inc(S["oa_mm"], 1)
                if hh + 1 < HG:
                    read(hh + 1)
                pe.wait_ge(S["vm_up"], hh + 1)
                if hh:
                    pe.wait_ge(S["sts_up"], hh)
                for g in range(2):
                    mm = pe.matmul(ps[:, 6 + g, :], B["KD"][0:NS, hh, :],
                                   B["E"][0:NS, 4 * g:4 * g + 4, :].rearrange("p b t -> p (b t)"), start=True, stop=True)
                mm.then_inc(S["kvs_mm"], 1)

        def sstep_act(act):
            for hh in range(HG):
                act.wait_ge(S["wq_mm"], hh + 1)
                if hh - 1 > 0:
                    act.wait_ge(S["oa_up"], hh - 1)
                act.activation(wqs[hh % 2][:, :, :], ps[:, hh % 2, 0:2 * NS].rearrange("p (x t) -> p x t", x=2),
                               ACT.Copy).then_inc(S["wq_cp"], 1)

        def sstep_dve(dve):
            def correct(hh):
                dve.wait_ge(S["wtr_mm"], hh + 1)
                dve.wait_ge(S["u_cp"], NCH + 1)
                dve.tensor_tensor(B["U"][0:NS, hh, :], B["U"][0:NS, hh, :], ps[0:NS, 2 + hh % 2, 0:P],
                                  ALU.subtract).then_inc(S["vns_up"], 1)
            correct(0)
            for hh in range(HG):
                dve.wait_ge(S["oa_mm"], hh + 1)
                dve.tensor_tensor(whole(ot)[:, hh, TP:T], wqs[hh % 2][:, 1, :], ps[:, 4 + hh % 2, 0:NS], ALU.add).then_inc(S["oa_up"], 1)
                st_arrived(dve, hh)
                if hh:
                    dve.wait_ge(S["sts_up"], hh)
                gt = B["EG"][:, hh, 0:NS].rearrange("p (b t) -> p b t", t=TS)[:, :, TS - 1]
                dve.tensor_tensor(B["Z"][:, :, :], STB[hh % 2][:, :, :], over(gt, P), ALU.mult).then_inc(S["sgs_up"], 1)
                if hh + 1 < HG:
                    correct(hh + 1)
                dve.wait_ge(S["kvs_mm"], hh + 1)
                dve.wait_ge(S["sgs_up"], hh + 1)
                if hh > 1:
                    dve.wait_ge([S["st_out0"], S["st_out1"]][hh % 2], 16 * (hh // 2))
                dve.tensor_tensor(STN[hh % 2][:, :, :], seqs(0), B["Z"][:, :, :], ALU.add).then_inc(S["sts_up"], 1)

        def sstep_pool(pool):
            for hh in range(HG):
                pool.wait_ge(S["vns_up"], hh + 1)
                if hh:
                    pool.wait_ge(S["kvs_mm"], hh)
                pool.tensor_tensor(B["E"][0:NS, :, :], B["U"][0:NS, hh, :].unsqueeze(1).broadcast_to([NS, NB, P]),
                                   over(mseq[0:NS, :], P), ALU.mult).then_inc(S["vm_up"], 1)

        def onorm_act(act):
            for t in range(HG):
                if t == 0:
                    act.wait_ge(S["oa_up"], HG)
                if t > 1:
                    act.wait_ge(S["on_mm"], t - 1)
                act.activation(tb[t % 2][:, :, :], ot[:, 2 * t:2 * t + 2, :], ACT.Square).then_inc(S["on_sq"], 1)
            act.wait_ge(S["on_mm"], HG)
            act.activation(tb[2][0:16, :, :], pair(2)[0:16], ACT.Sqrt, bias=eps[0:16, 0:1], scale=1.0 / P).then_inc(S["on_rt"], 1)
            act.wait_ge(S["sts_up"], HG)
            act.wait_ge(S["st_out0"], 64)
            act.wait_ge(S["st_out1"], 64)
            for t in range(HG):
                act.wait_ge(S["on_f32"], t + 1)
                act.activation(xh[:, 2 * t:2 * t + 2, :], ot[:, 2 * t:2 * t + 2, :], ACT.Copy).then_inc(x_hi, 1)

        def onorm_pe(pe):
            for t in range(HG):
                pe.wait_ge(S["on_sq"], t + 1)
                sum_rows(pe, pair(2), one_col[:, 15 - t:31 - t], tb[t % 2], t == 0, t == HG - 1).then_inc(S["on_mm"], 1)
            pe.wait_ge(S["on_rs"], 1)
            for t in range(HG):
                if t > 1:
                    pe.wait_ge(S["on_n"], t - 1)
                spread_row(pe, pair(t % 2), tb[2], t).then_inc(S["on_bc"], 1)

        def onorm_dve(dve):
            dve.wait_ge(S["on_rt"], 1)
            dve.reciprocal(tb[2][0:16, :, :], tb[2][0:16, :, :]).then_inc(S["on_rs"], 1)
            for t in range(HG):
                dve.wait_ge(S["on_bc"], t + 1)
                o = ot[:, 2 * t:2 * t + 2, :]
                dve.scalar_tensor_tensor(o, o, v(V_ONORM), pair(t % 2), ALU.mult, ALU.mult).then_inc(S["on_n"], 1)
                dve.wait_ge(S["on_n"], t + 1)
                dve.tensor_tensor(o, o, zg[:, 2 * t:2 * t + 2, :], ALU.mult).then_inc(S["on_f32"], 1)
                if t:
                    gdn_out_low(dve, t - 1)
            gdn_out_low(dve, HG - 1)

        def gdn_out_low(dve, t):
            dve.wait_ge(x_hi, 8 * SETS["gdn_out"] + t + 1)
            dve.tensor_tensor(xl[:, 2 * t:2 * t + 2, :], ot[:, 2 * t:2 * t + 2, :],
                              xh[:, 2 * t:2 * t + 2, :].bitcast(F32), ALU.subtract).then_inc(x_lo, 1)

        def gdn_pe(pe):
            gdn_in_pe(pe)
            ba_pe_first(pe)
            ba_pe_transpose(pe)
            l2_spread(pe, range(6))
            ba_pe_second(pe)
            l2_spread(pe, range(6, 2 * HG))
            with pe.Fori(0, NCH) as it:
                chunk_pe(pe, it, P)
            chunk_pe(pe, NCH, NS)
            sstep_pe(pe)
            onorm_pe(pe)
            out_pe(pe, "gdn_out", 3, 8 * SETS["gdn_out"])
            norm_pe(pe, 3)

        def gdn_act(act):
            for j in range(2):
                split_hi(act, "gdn_in", 0, j)
            pre_norm_act(act, 2, SETS["gdn_in"])
            gdn_in_act(act)
            l2_act(act)
            ba_act2(act)
            act.wait_ge(S["cn_out"], 16)
            with act.Fori(0, NCH) as it:
                chunk_act(act, it, P)
            chunk_act(act, NCH, NS)
            sstep_act(act)
            onorm_act(act)
            out_act(act, "gdn_out", 1, 3, y=y2)
            norm_act(act, 3)

        def gdn_dve(dve):
            norm_dve(dve, 2)
            gdn_in_dve(dve)
            l2_ba_dve(dve)
            with dve.Fori(0, NCH) as it:
                chunk_dve(dve, it, P)
            chunk_dve(dve, NCH, NS)
            sstep_dve(dve)
            onorm_dve(dve)
            out_dve(dve, "gdn_out", 1, 3)
            post_norm_dve(dve, 3, 1.0, SETS["ffn1_in"], y=y2)

        def gdn_pool(pool):
            pool_units(pool, "gdn_in", 2)
            split_lo(pool, "ba", 0, 0)
            with pool.Fori(0, NCH) as it:
                chunk_pool(pool, it, P)
            chunk_pool(pool, NCH, NS)
            sstep_pool(pool)
            pool_units(pool, "gdn_out")

        def gdn_sp(sp):
            sp.wait_ge(mid_lo, NF)
            sp.wait_ge(acc, 2 * BASE["gdn_in"])
            sp.dma_start(hist[:, :, :], a["conv_hist"]).then_inc(S["hist_in"], 16)
            load_units(sp, "gdn_in")
            load_units(sp, "ba")
            sp.wait_ge(S["conv_done"], NQKV)
            sp.dma_start(a["conv_new"], cnew[:, :, :]).then_inc(S["cn_out"], 16)
            sp.wait_ge(S["cn_out"], 16)
            load_units(sp, "gdn_out", part=0)
            sstep_sp(sp)
            load_units(sp, "gdn_out", part=1)

        at = [after_x]
        xn = place("xn", [P, 2 * NM, HALF], F32, at)
        dd = place("dd", [P, 2 * NM, HALF], F32, at)
        r_, k_, v_ = (place(n, [P, 2 * NM, HALF], F32, at) for n in ("rr", "rk", "rv"))
        wa2_at = at[0]
        wa2 = place("wa2", [P, D], F32, at)
        lt1 = place("lt1", [P, 2, HALF], F32, at)
        lg = place("lg", [P, 2, HALF], F32, at)
        at = [region]
        RA, RB, BO = (place(n, [P, 2 * NM, HALF], F32, at) for n in ("RA", "RB", "BO"))
        gap = at[0]
        at = [after_x]
        tmp = [[place(f"pt{e}{i}", [P, 2, HALF], F32, at) for i in range(4)] for e in range(2)]
        reset = place("reset", [P, T], F32, at)
        shin = place("shin", [P, NM, NB], F32, [after_x + 2 * NM * HALF * 4 * 2])
        shout = place("shout", [P, NM, 1 + NB], F32, [after_x + 2 * NM * HALF * 4 * 2 + 512])
        at = [after_x]
        Q = dict(**{n: place("r" + n, [P, 8, P], F32, at) for n in ("Z", "ZL", "T", "F", "G", "L2", "L3", "L4")})
        Vt = place("Vt", [P, 4, P], F32, at)
        assert at[0] <= after_x + 2 * 2 * NM * HALF * 4
        Uu = place("Uu", [P, 4, P], F32, [after_x])
        WT = place("WT", [P, 4, P], F32, [after_x + 4096])
        GV = place("GV", [P, 4, P], F32, [after_x + 2 * 4096])
        VMa = place("VMa", [P, NB, P], F32, [after_x + 3 * 4096])
        SO = [place(f"SO{i}", [P, NB, 64], F32, [after_x + 4 * 4096 + 2048 * i]) for i in range(2)]
        VMb = place("VMb", [P, NB, P], F32, [after_x + 5 * 4096])
        at = [gap]
        Att = place("Att", [P, 4, P], F32, at)
        Btt = place("Btt", [P, 4, P], F32, at)
        assert at[0] <= after_x
        at = [wa2_at]
        Ktt = place("Ktt", [P, 4, P], F32, at)
        RS = place("RS", [P, NM, P], F32, at)
        assert at[0] <= wa2_at + 4096 + 2176
        at = [tb_at]
        Ast, Bst, Kst, Vst, Rst = (place(n, [P, 4, P], F32, at) for n in ("Ast", "Bst", "Kst", "Vst", "Rst"))
        assert at[0] <= region
        SB1 = place("SB1", [P, NB, P], F32, [tb_at])
        wqr = [place(f"wqr{i}", [P, 2, NS], F32, [tb_at + 4096 + 256 * i]) for i in range(2)]
        g2w = place("g2w", [P, D], F32, [after_x + 3 * 2 * NM * HALF * 4])
        gdn_last = {}
        spare = [(n, last) for last, names in counted.items() for n in names]

        def take_over(old, last):
            gdn_last[id(old)] = last
            return old

        def past(s, count):
            return count + gdn_last.get(id(s), 0)
        steps = (
            "xn_up", "sh_in", "w2_in", "rm_in", "dd_up", "sh_cp", "sh_out", "mix", "r_cp", "lora_cp", "sg_mm", "sg_cp",
            "kq_sq", "kq_mm", "kq_rt", "kq_rs", "kq_bc", "halves", "kk_up", "d0", "scan", "cprev", "ex", "a_up", "ka", "b1", "b2", "kp",
            "rkk", "bo_mm", "bo_up", "r_up", "k_up", "ece", "ast", "bst", "rst", "kst", "vst", "l1_mm", "l3_mm", "l2_mm",
            "l4_mm", "z_cp", "l3_up", "l2_up", "l4_up", "vt_mm", "at_mm", "bt_mm", "kt_mm", "vt_cp", "at_cp",
            "bt_cp", "kt_cp", "gv_mm", "gv_cp", "u_mm", "u_cp", "wt_mm", "wt_cp", "sa_mm", "sa_up", "ds_mm", "y_mm",
            "s_add", "s_up", "y_cp", "s_out", "si0", "si1", "so0", "so1", "so_cp", "sb_clr", "wq_mm", "wq_cp", "wtr_mm",
            "sas_up", "ys_mm", "ys_up", "vm_up", "vmb_up", "dss_mm", "ss_add", "ss_up", "g2_in", "mu_mm", "yc", "ysq",
            "var_mm", "gn_rt", "gn_rs", "gn_bc", "gn1", "gn2", "gn3", "g_mm")
        own = len(steps) - len(spare)
        R = dict(**{n: sem("r_" + n) for n in steps[:own]},
                            **{n: take_over(S[old], last) for n, (old, last) in zip(steps[own:], spare)})
        after = inv_at(GI, NCH + 1, 1, 0), inv_at(GI, NCH + 1, 2, 0)
        halves = place("halves", [16, NM, P], F32, [tb_at + 3 * T * 4])
        assert tb_at + 3 * T * 4 + NM * P * 4 <= region

        def make_halves(pool):
            pool.tensor_copy(halves[:, :, :].rearrange("p m (h t) -> p (m h) t", t=64),
                             M["ident"][0:16, 0:16].unsqueeze(2).broadcast_to([16, 16, 64])).then_inc(R["halves"], 1)

        def spread_two_rows(pe, pr, rows, m):
            for half in range(2):
                mm = pe.matmul(pr[:, half, :], halves[:, m, :], rows[0:16, half, :], start=True, stop=True)
            return mm
        RI = dict(L=LEVELS - 1, calls=2 * NCH, past=(after[0][0], after[1][1], after[1][2], after[0][3]),
                   zl=GI["zl"], tmm=GI["tmm"], fup=GI["fup"], tcp=GI["tcp"], fmm=GI["fmm"], gmm=GI["gmm"], gup=GI["gup"])


        def wh(t, m):
            return t[:, 2 * m:2 * m + 2, :]

        def mix_dve(dve, i):
            def low(m):
                dve.wait_ge(x_hi, 8 * SETS[f"x{i}"] + m + 1)
                dve.tensor_tensor(wh(xl, m), tb[m % 2][:, :, :], wh(xh, m).bitcast(F32), ALU.subtract).then_inc(x_lo, 1)
            for m in range(NM):
                dve.wait_ge(x_lo, 8 * SETS[f"x{i}"] + m - 1)
                dve.scalar_tensor_tensor(tb[m % 2][:, :, :], wh(dd, m), v(V_LERP + i * NM + m), wh(xn, m),
                                         ALU.mult, ALU.add).then_inc(R["mix"], 1)
                if m:
                    low(m - 1)
            low(NM - 1)

        def mix_act(act, i):
            for m in range(NM):
                act.wait_ge(R["mix"], past(R["mix"], 8 * i + m + 1))
                act.activation(wh(xh, m), tb[m % 2][:, :, :], ACT.Copy).then_inc(x_hi, 1)

        def rkv_act(act, i, name, dst):
            for j in range(2):
                split_hi(act, name, 0, j)
            act.wait_ge(acc, 2 * BASE[name])
            mix_act(act, i)
            for u in (0, 4):
                for j in range(4):
                    if u + j + 2 < NM:
                        split_hi(act, name, u, j + 2)
                    act.wait_ge(acc, 2 * (BASE[name] + u + j + 1))
                    act.activation(wh(dst, u + j), pair(j), ACT.Copy).then_inc(R["r_cp"], 1)

        def rkv_pe(pe, i, name):
            if i:
                pe.wait_ge(R["r_cp"], past(R["r_cp"], 8 * i - 2))
            first_units_mm(pe, name, SETS[f"x{i}"])
            for m in range(2, NM):
                if 8 * i + m - 3 > 0:
                    pe.wait_ge(R["r_cp"], past(R["r_cp"], 8 * i + m - 3))
                unit_mm(pe, name, m - m % 4, m % 4, pair(m % 4), xh, xl)

        def shift_dve(dve):
            norm_dve(dve, 8)
            for m in range(NM):
                dve.scalar_tensor_tensor(wh(xn, m), wh(h, m), v(V_NORM + 8 * NM + m), rs[:, :, :],
                                         ALU.mult, ALU.mult).then_inc(R["xn_up"], 1)
            dve.wait_ge(R["xn_up"], past(R["xn_up"], NM))
            dve.wait_ge(R["sh_in"], past(R["sh_in"], 16))
            x, d = whole(xn), whole(dd)
            xs = x[:, :, TP:T].rearrange("p m (b t) -> p m b t", b=NB)
            dsn = d[:, :, TP:T].rearrange("p m (b t) -> p m b t", b=NB)
            dve.tensor_tensor(d[:, :, 1:TP], x[:, :, 0:TP - 1], x[:, :, 1:TP], ALU.subtract)
            dve.tensor_scalar(d[:, :, 0:1], x[:, :, 0:1], -1.0, None, ALU.mult)
            dve.tensor_tensor(dsn[:, :, :, 1:TS], xs[:, :, :, 0:TS - 1], xs[:, :, :, 1:TS], ALU.subtract)
            dve.tensor_tensor(dsn[:, :, :, 0], shin[:, :, :], xs[:, :, :, 0], ALU.subtract).then_inc(R["dd_up"], 1)
            dve.tensor_copy(shout[:, :, 0:1], x[:, :, TP - 1:TP])
            dve.tensor_copy(shout[:, :, 1:1 + NB], xs[:, :, :, TS - 1]).then_inc(R["sh_cp"], 1)
            dve.wait_ge(R["dd_up"], past(R["dd_up"], 1))

        def lora_act(act):
            for j in range(2):
                split_hi(act, "lora", 0, j)
            for j in range(3):
                n = BASE["lora"] + j
                act.wait_ge(acc, 2 * n)
                mix_act(act, 3 + j)
                if j == 0:
                    split_hi(act, "lora", 0, 2)
                act.wait_ge(acc, 2 * (n + 1))
                if j == 0:
                    act.activation(lt1[0:64, :, :], ps[0:64, 0:2, 0:HALF], ACT.Tanh).then_inc(R["lora_cp"], 1)
                elif j == 1:
                    act.activation(lt1[64:P, :, :], ps[64:P, 2:4, 0:HALF], ACT.Copy).then_inc(R["lora_cp"], 1)
                else:
                    act.activation(lg[:, :, :], pair(2), ACT.Sigmoid).then_inc(R["lora_cp"], 1)

        def lora_pe(pe):
            for j in range(3):
                pe.wait_ge(R["r_cp"], past(R["r_cp"], 24))
                unit_mm(pe, "lora", 0, j, pair(j), xh, xl, ready=8 * SETS[f"x{3 + j}"])

        def lora_pool(pool):
            for j in range(3):
                split_lo(pool, "lora", 0, j)

        def prep_pe(pe):
            pe.wait_ge(R["w2_in"], past(R["w2_in"], 16))
            pe.wait_ge(R["lora_cp"], past(R["lora_cp"], 3))
            for m in range(NM):
                if 2 * (m - 1) > 0:
                    pe.wait_ge(R["sg_cp"], past(R["sg_cp"], 2 * (m - 1)))
                for par in range(2):
                    lo = 64 * par
                    for half in range(2):
                        mm = pe.matmul(pair(2 * (m % 2) + par)[:, half, :], wa2[lo:lo + 64, m * P:(m + 1) * P],
                                       lt1[lo:lo + 64, half, :], start=True, stop=True)
                    mm.then_inc(R["sg_mm"], 1)
            for m in range(NM):
                pe.wait_ge(R["kq_sq"], past(R["kq_sq"], m + 1))
                if m < 2:
                    pe.wait_ge(R["sg_cp"], past(R["sg_cp"], 2 * NM))
                sum_rows(pe, pair(0), two_cols[:, 14 - 2 * m:30 - 2 * m], tb[m % 2], m == 0, m == NM - 1).then_inc(R["kq_mm"], 1)
            pe.wait_ge(R["halves"], past(R["halves"], 1))
            pe.wait_ge(R["kq_rs"], past(R["kq_rs"], 1))
            for m in range(NM):
                if m > 1:
                    pe.wait_ge(R["kk_up"], past(R["kk_up"], m - 1))
                spread_two_rows(pe, pair(m % 2), tb[2], m).then_inc(R["kq_bc"], 1)
            for m in range(NM):
                pe.wait_ge(R["rkk"], past(R["rkk"], m + 1))
                if m - 1 > 0:
                    pe.wait_ge(R["bo_up"], past(R["bo_up"], m - 1))
                for half in range(2):
                    mm = pe.matmul(pair(2 + m % 2)[:, half, :], M["headones"], tmp[m % 2][3][:, half, :], start=True, stop=True)
                mm.then_inc(R["bo_mm"], 1)

        def prep_act(act):
            for m in range(NM):
                for par, (dst, bias) in enumerate(((RA, V_W0), (RB, V_A0))):
                    act.wait_ge(R["sg_mm"], past(R["sg_mm"], 2 * m + par + 1))
                    act.activation(wh(dst, m), pair(2 * (m % 2) + par), ACT.Sigmoid, bias=v(bias + m)).then_inc(R["sg_cp"], 1)
            for m in range(NM):
                if m - 1 > 0:
                    act.wait_ge(R["kq_mm"], past(R["kq_mm"], m - 1))
                act.activation(tb[m % 2][:, :, :], wh(k_, m), ACT.Square, scale=v(V_KK + m)).then_inc(R["kq_sq"], 1)
            act.wait_ge(R["kq_mm"], past(R["kq_mm"], NM))
            act.activation(tb[2][0:16, :, :], pair(0)[0:16], ACT.Sqrt, bias=eps[0:16, 0:1]).then_inc(R["kq_rt"], 1)
            for m in range(NM):
                u0, u2, u3, u6 = (t[:, :, :] for t in tmp[m % 2])
                act.wait_ge(R["cprev"], past(R["cprev"], m + 1))
                if m - 1 > 0:
                    act.wait_ge(R["k_up"], past(R["k_up"], m - 1))
                if m - 1 > 0:
                    act.wait_ge(R["b2"], past(R["b2"], m - 1))
                act.activation(u3, u2, ACT.Exp, scale=-1.0)
                act.activation(u0, u0, ACT.Exp).then_inc(R["ex"], 1)
                act.wait_ge(R["ex"], past(R["ex"], 2 * m + 1))
                act.activation(u2, u2, ACT.Exp).then_inc(R["ex"], 1)

        def prep_dve(dve):
            dve.wait_ge(R["kq_rt"], past(R["kq_rt"], 1))
            dve.reciprocal(tb[2][0:16, :, :], tb[2][0:16, :, :]).then_inc(R["kq_rs"], 1)
            for m in range(NM):
                dve.wait_ge(R["kq_bc"], past(R["kq_bc"], m + 1))
                dve.scalar_tensor_tensor(wh(BO, m), wh(k_, m), v(V_KK + m), pair(m % 2), ALU.mult, ALU.mult).then_inc(R["kk_up"], 1)
            dve.wait_ge(R["kk_up"], past(R["kk_up"], NM))
            dve.wait_ge(R["rm_in"], past(R["rm_in"], 16))
            for m in range(NM):
                t0, t2, t3, t6 = tmp[m % 2]
                u0, u2, u3, u6 = (t[:, :, :] for t in tmp[m % 2])
                if m - 1 > 0:
                    dve.wait_ge(R["a_up"], past(R["a_up"], m - 1))
                if m - 1 > 0:
                    dve.wait_ge(R["ece"], past(R["ece"], m - 1))
                if m - 1 > 0:
                    dve.wait_ge(R["r_up"], past(R["r_up"], m - 1))
                dve.tensor_scalar(u0, wh(RA, m), -float(np.exp(-0.5)), None, ALU.mult).then_inc(R["d0"], 1)
                dve.wait_ge(R["d0"], past(R["d0"], m + 1))
                dve.tensor_tensor_scan(flat(t2), reset[:, :], flat(t0), 0.0, ALU.mult, ALU.add).then_inc(R["scan"], 1)
                dve.wait_ge(R["scan"], past(R["scan"], m + 1))
                dve.tensor_tensor(u0, u2, u0, ALU.subtract).then_inc(R["cprev"], 1)
                if m - 1 > 0:
                    dve.wait_ge(R["bo_mm"], past(R["bo_mm"], m - 1))
                dve.tensor_scalar(u6, wh(RB, m), -1.0, v(V_KA + m), ALU.add, ALU.mult).then_inc(R["ka"], 1)
                dve.wait_ge(R["ka"], past(R["ka"], m + 1))
                dve.scalar_tensor_tensor(wh(k_, m), u6, 1.0, wh(k_, m), ALU.add, ALU.mult).then_inc(R["kp"], 1)
                dve.wait_ge(R["kp"], past(R["kp"], m + 1))
                dve.scalar_tensor_tensor(u6, wh(r_, m), v(V_RK + m), wh(k_, m), ALU.mult, ALU.mult).then_inc(R["rkk"], 1)
                dve.wait_ge(R["ex"], past(R["ex"], 2 * m + 1))
                dve.scalar_tensor_tensor(wh(RA, m), wh(BO, m), -1.0, u0, ALU.mult, ALU.mult).then_inc(R["a_up"], 1)
                dve.wait_ge(R["bo_mm"], past(R["bo_mm"], m + 1))
                dve.wait_ge(R["b1"], past(R["b1"], m + 1))
                dve.wait_ge(R["a_up"], past(R["a_up"], m + 1))
                dve.tensor_tensor(wh(BO, m), wh(v_, m), pair(2 + m % 2), ALU.mult).then_inc(R["bo_up"], 1)

        def prep_pool(pool):
            pool.wait_ge(x_lo, 8 * SETS["wo"])
            make_halves(pool)
            for m in range(NM):
                u0, u2, u3, u6 = (t[:, :, :] for t in tmp[m % 2])
                pool.wait_ge(R["ka"], past(R["ka"], m + 1))
                pool.tensor_tensor(wh(RB, m), wh(BO, m), wh(RB, m), ALU.mult).then_inc(R["b1"], 1)
                pool.wait_ge(R["ex"], past(R["ex"], 2 * m + 1))
                pool.wait_ge(R["b1"], past(R["b1"], m + 1))
                pool.tensor_tensor(wh(RB, m), wh(RB, m), u3, ALU.mult).then_inc(R["b2"], 1)
                pool.wait_ge(R["rkk"], past(R["rkk"], m + 1))
                pool.tensor_tensor(wh(k_, m), wh(k_, m), u3, ALU.mult).then_inc(R["k_up"], 1)
                pool.wait_ge(R["ex"], past(R["ex"], 2 * m + 2))
                pool.tensor_tensor(wh(r_, m), wh(r_, m), u2, ALU.mult).then_inc(R["r_up"], 1)
                ec = flat(tmp[m % 2][1])
                pool.tensor_copy(ECE[:, m, 0:8], ec[:, 0:TP].rearrange("p (c t) -> p c t", t=64)[:, :, 63])
                pool.tensor_copy(ECE[:, m, 8:16], ec[:, TP:T].rearrange("p (c t) -> p c t", t=TS)[:, :, TS - 1]).then_inc(R["ece"], 1)

        def rt(t, c, g, nt):
            if nt == P:
                return whole(t)[:, 4 * g:4 * g + 4, ds(c * P, P)]
            return whole(t)[:, 4 * g:4 * g + 4, TP:T]

        def start_waits(e, n, smp):
            e.wait_ge(R["s_up"], past(R["s_up"], 2 * n + 1 if smp is None else 17))
            e.wait_ge(R["y_cp"], past(R["y_cp"], n + 1 if smp is None else 9))
            if smp:
                e.wait_ge(R["ss_up"], past(R["ss_up"], 4 * smp))
                e.wait_ge(R["so0"], past(R["so0"], 32 * smp))
                e.wait_ge(R["so1"], past(R["so1"], 32 * smp))
                e.wait_ge(R["vm_up"], past(R["vm_up"], 4 * smp))
                e.wait_ge(R["ys_up"], past(R["ys_up"], 4 * smp))

        def rstep_pool(pool, n, c, g, nt, smp=None):
            if smp is not None:
                start_waits(pool, n, smp)
            else:
                pool.wait_ge(R["kt_mm"], past(R["kt_mm"], n + 1))
            pool.tensor_copy(Ast[:, :, 0:nt], rt(RA, c, g, nt)).then_inc(R["ast"], 1)
            pool.tensor_copy(Bst[:, :, 0:nt], rt(RB, c, g, nt)).then_inc(R["bst"], 1)
            pool.tensor_copy(Rst[:, :, 0:nt], rt(r_, c, g, nt)).then_inc(R["rst"], 1)
            pool.tensor_copy(Kst[:, :, 0:nt], rt(k_, c, g, nt)).then_inc(R["kst"], 1)
            pool.tensor_copy(Vst[:, :, 0:nt], rt(v_, c, g, nt)).then_inc(R["vst"], 1)
            pool.wait_ge(R["z_cp"], past(R["z_cp"], n + 1))
            inv_pool(pool, RI, Q, n, LEVELS - 1 if nt == P else 2, nt)

        def rstep_act(act, n, c, g, nt, smp=None):
            start_waits(act, n, smp)
            act.wait_ge(R["l1_mm"], past(R["l1_mm"], n + 1))
            act.activation(Q["Z"][0:nt, :, 0:nt], banks(0, 2, nt, nt), ACT.Copy, scale=-1.0).then_inc(R["z_cp"], 1)
            for mm, cp, dst, b in ((R["vt_mm"], R["vt_cp"], Vt, 0), (R["at_mm"], R["at_cp"], Att, 1), (R["bt_mm"], R["bt_cp"], Btt, 2),
                                   (R["kt_mm"], R["kt_cp"], Ktt, 3)):
                act.wait_ge(mm, past(mm, n + 1 + (mm is R["kt_mm"])))
                act.activation(dst[0:nt, :, :], banks(b, 1, nt, P), ACT.Copy).then_inc(cp, 1)
            inv_act(act, RI, Q, n, LEVELS - 1 if nt == P else 2, nt)
            act.wait_ge(R["gv_mm"], past(R["gv_mm"], n + 1))
            act.activation(GV[0:nt, :, :], banks(6, 1, nt, P), ACT.Copy).then_inc(R["gv_cp"], 1)
            act.wait_ge(R["wt_mm"], past(R["wt_mm"], n + 1))
            act.activation(WT[:, :, 0:nt], banks(7, 1, P, nt), ACT.Copy).then_inc(R["wt_cp"], 1)
            act.wait_ge(R["u_mm"], past(R["u_mm"], n + 1))
            act.activation(Uu[0:nt, :, :], banks(0, 1, nt, P), ACT.Copy).then_inc(R["u_cp"], 1)
            if nt == P:
                act.wait_ge(R["y_mm"], past(R["y_mm"], 2 * n + 2))
                act.activation(rt(RA, c, g, nt), banks(6, 1, P, P), ACT.Copy).then_inc(R["y_cp"], 1)

        def rstep_dve(dve, n, c, g, nt, smp=None):
            start_waits(dve, n, smp)
            cs = "64" if nt == P else "4"
            for mm, up, dst, b, mask in ((R["l3_mm"], R["l3_up"], Q["L3"], 2, "incl"), (R["l2_mm"], R["l2_up"], Q["L2"], 4, "strict"),
                                         (R["l4_mm"], R["l4_up"], Q["L4"], 6, "incl")):
                dve.wait_ge(mm, past(mm, n + 1))
                dve.tensor_tensor(dst[0:nt, :, 0:nt], banks(b, 2, nt, nt), over_heads(MB[mask + cs][0:nt, 0:nt], 8),
                                  ALU.mult).then_inc(up, 1)
            inv_dve(dve, RI, Q, n, LEVELS - 1 if nt == P else 2, nt)
            if nt != P:
                return
            for cc in range(2):
                pp = slice(64 * cc, 64 * cc + 64)
                if cc == 0:
                    dve.wait_ge(R["u_cp"], past(R["u_cp"], n + 1))
                dve.wait_ge(R["sa_mm"], past(R["sa_mm"], 2 * n + cc + 1))
                dve.tensor_tensor(Uu[pp, :, :], Uu[pp, :, :], banks(5, 1, P, P)[pp], ALU.add).then_inc(R["sa_up"], 1)
                dve.wait_ge(R["ds_mm"], past(R["ds_mm"], 2 * n + cc + 1))
                dve.wait_ge(R["y_mm"], past(R["y_mm"], 2 * n + cc + 1))
                d = banks(4, 1, P, P)
                for par in range(2):
                    hp = slice(64 * par, 64 * par + 64)
                    i = dve.tensor_tensor(RS[hp, 4 * g:4 * g + 4, hp], RS[hp, 4 * g:4 * g + 4, hp], d[hp, :, hp], ALU.add)
                i.then_inc(R["s_add"], 1)
                dve.wait_ge(R["s_add"], past(R["s_add"], 2 * n + cc + 1))
                e = ECE[:, 4 * g:4 * g + 4, ds(2 * c + cc, 1)].broadcast_to([P, 4, P])
                dve.tensor_tensor(RS[:, 4 * g:4 * g + 4, :], RS[:, 4 * g:4 * g + 4, :], e, ALU.mult).then_inc(R["s_up"], 1)

        def rstep_pe(pe, n, c, g, nt, smp=None):
            if smp is not None:
                start_waits(pe, n, smp)

            def heads():
                for tl in range(4):
                    for par in range(2):
                        yield par * 4 + tl, tl, slice(64 * par, 64 * par + 64)

            def prod(ready, st, rhs, b, done):
                for s_ in ready:
                    pe.wait_ge(s_, past(s_, n + 1))
                for s, tl, pr in heads():
                    mm = pe.matmul(ps[0:nt, b + s // 4, (s % 4) * P:(s % 4) * P + nt], st[pr, tl, 0:nt], rhs[pr, tl, 0:nt],
                                   start=True, stop=True)
                mm.then_inc(done, 1)
            prod((R["ast"], R["bst"]), Ast, Bst, 0, R["l1_mm"])
            prod((R["rst"],), Bst, Rst, 2, R["l3_mm"])
            if smp is None:
                pe.wait_ge(R["s_up"], past(R["s_up"], 2 * n + 1))
                pe.wait_ge(R["y_cp"], past(R["y_cp"], n + 1))
            prod((R["kst"],), Kst, Ast, 4, R["l2_mm"])
            prod((), Kst, Rst, 6, R["l4_mm"])
            for st, b, wait, done in ((Vst, 0, R["z_cp"], R["vt_mm"]), (Ast, 1, R["z_cp"], R["at_mm"]), (Bst, 2, R["l3_up"], R["bt_mm"]),
                                      (Kst, 3, R["l3_up"], R["kt_mm"])):
                pe.wait_ge(wait, past(wait, n + 1))
                if st is Vst:
                    pe.wait_ge(R["vst"], past(R["vst"], n + 1))
                for tl in range(4):
                    mm = pe.transpose(ps[0:nt, b, tl * P:(tl + 1) * P], st[:, tl, 0:nt], M["ident"])
                mm.then_inc(done, 1)
            for cp in (R["vt_cp"], R["at_cp"], R["bt_cp"], R["kt_cp"]):
                pe.wait_ge(cp, past(cp, n + 1))
            pe.wait_ge(R["l2_up"], past(R["l2_up"], n + 1))
            levels = LEVELS - 1 if nt == P else 2
            inv_pe(pe, RI, Q, n, levels, nt)
            for a_ in range(2):
                pe.wait_ge(RI["fup"], past(RI["fup"], inv_at(RI, n, levels, a_)[0] + 1))
            pe.wait_ge(R["l4_up"], past(R["l4_up"], n + 1))
            for s, tl, pr in heads():
                mm = pe.matmul(ps[0:nt, 6, tl * P:(tl + 1) * P][:, pr], Q["L2"][0:nt, s, 0:nt], Vt[0:nt, tl, pr], start=True, stop=True)
            mm.then_inc(R["gv_mm"], 1)
            for s, tl, pr in heads():
                mm = pe.matmul(ps[pr, 7, tl * P:tl * P + nt], Att[0:nt, tl, pr], Q["F"][0:nt, s, 0:nt], start=True, stop=True)
            mm.then_inc(R["wt_mm"], 1)
            pe.wait_ge(R["gv_cp"], past(R["gv_cp"], n + 1))
            for s, tl, pr in heads():
                mm = pe.matmul(ps[0:nt, 0, tl * P:(tl + 1) * P][:, pr], Q["F"][0:nt, s, 0:nt], GV[0:nt, tl, pr], start=True, stop=True)
            mm.then_inc(R["u_mm"], 1)
            pe.wait_ge(R["wt_cp"], past(R["wt_cp"], n + 1))
            if nt != P:
                return
            for cc in range(2):
                pp = slice(64 * cc, 64 * cc + 64)
                if cc:
                    pe.wait_ge(R["s_up"], past(R["s_up"], 2 * n + 2))
                for tl in range(4):
                    mm = pe.matmul(ps[pp, 5, tl * P:(tl + 1) * P], WT[:, tl, pp], RS[:, 4 * g + tl, :], start=True, stop=True)
                mm.then_inc(R["sa_mm"], 1)
                pe.wait_ge(R["sa_up"], past(R["sa_up"], 2 * n + cc + 1))
                for tl in range(4):
                    o = ps[:, 4, tl * P:(tl + 1) * P]
                    pe.matmul(o, Ktt[pp, tl, :], Vt[pp, tl, :], start=True, stop=False)
                    mm = pe.matmul(o, Btt[pp, tl, :], Uu[pp, tl, :], start=False, stop=True)
                mm.then_inc(R["ds_mm"], 1)
                for tl in range(4):
                    co = slice(tl * P + 64 * cc, tl * P + 64 * cc + 64)
                    pe.matmul(ps[:, 6, co], RS[:, 4 * g + tl, :], rt(r_, c, g, nt)[:, tl, pp], start=True, stop=False,
                              skip_group_check=True)
                    for par in range(2):
                        pr = slice(64 * par, 64 * par + 64)
                        s = par * 4 + tl
                        pe.matmul(ps[pr, 6, co], Uu[pp, tl, pr], Q["L3"][pp, s, pp], start=False, stop=False, skip_group_check=True)
                        mm = pe.matmul(ps[pr, 6, co], Vt[pp, tl, pr], Q["L4"][pp, s, pp], start=False, stop=True,
                                       skip_group_check=True)
                mm.then_inc(R["y_mm"], 1)

        def rst(i):
            return (RS if i % 2 == 0 else SB1)

        def rst_in(eng, i):
            eng.wait_ge((R["si0"], R["si1"])[i % 2], past((R["si0"], R["si1"])[i % 2], 32 * (i // 2 + 1)))

        def rsample_sp(sp):
            sp.wait_ge(R["s_up"], past(R["s_up"], 17))
            for par in range(2):
                hp = slice(64 * par, 64 * par + 64)
                sp.dma_start(a["rwkv_s_p"][hp], RS[hp, :, hp]).then_inc(R["s_out"], 16)
            sp.wait_ge(R["s_out"], past(R["s_out"], 32))
            for i in range(NM):
                if i % 4 == 0:
                    sp.wait_ge(R["sb_clr"], past(R["sb_clr"], i // 4 + 1))
                if i > 1:
                    sp.wait_ge(R["wq_mm"], past(R["wq_mm"], i - 1))
                    sp.wait_ge(R["so_cp"], past(R["so_cp"], i - 1))
                for par in range(2):
                    hp = slice(64 * par, 64 * par + 64)
                    sp.dma_start(rst(i)[hp, :, hp], a["state_rwkv"][i, hp]).then_inc((R["si0"], R["si1"])[i % 2], 16)
                if i % 4 >= 1:
                    rout(sp, i - 1)
                if i % 4 == 3:
                    rout(sp, i)

        def rout(sp, i):
            sp.wait_ge(R["ss_up"], past(R["ss_up"], i + 1))
            sp.dma_start(a["rwkv_s_s"][i], SO[i % 2][:, :, :]).then_inc((R["so0"], R["so1"])[i % 2], 16)

        def rsample_pe(pe, g):
            def read(tl):
                i = 4 * g + tl
                rst_in(pe, i)
                pe.wait_ge(R["u_cp"], past(R["u_cp"], 8 + g + 1))
                if i > 1:
                    pe.wait_ge(R["ys_up"], past(R["ys_up"], i - 1))
                b0 = ps[:, tl % 2, 0:2 * NS].rearrange("p (x t) -> p x t", x=2)
                for b in range(NB):
                    cols = slice(TS * b, TS * b + TS)
                    pe.matmul(b0[:, 0, cols], rst(i)[:, b, :], WT[:, tl, cols], start=True, stop=True)
                    mm = pe.matmul(b0[:, 1, cols], rst(i)[:, b, :], whole(r_)[:, i, TP:T][:, cols], start=True, stop=True)
                mm.then_inc(R["wq_mm"], 1)
                pe.wait_ge(R["wq_cp"], past(R["wq_cp"], i + 1))
                pe.transpose(ps[0:NS, 2 + tl % 2, 0:P], wqr[i % 2][:, 0, :], M["ident"]).then_inc(R["wtr_mm"], 1)
            read(0)
            for tl in range(4):
                i = 4 * g + tl
                pe.wait_ge(R["sas_up"], past(R["sas_up"], i + 1))
                if i:
                    pe.wait_ge(R["ys_up"], past(R["ys_up"], i))
                for par in range(2):
                    pr = slice(64 * par, 64 * par + 64)
                    s = par * 4 + tl
                    pe.matmul(ps[pr, 4, 0:NS], Uu[0:NS, tl, pr], Q["L3"][0:NS, s, 0:NS], start=True, stop=False)
                    mm = pe.matmul(ps[pr, 4, 0:NS], Vt[0:NS, tl, pr], Q["L4"][0:NS, s, 0:NS], start=False, stop=True)
                mm.then_inc(R["ys_mm"], 1)
                if tl < 3:
                    read(tl + 1)
                pe.wait_ge(R["vm_up"], past(R["vm_up"], i + 1))
                pe.wait_ge(R["vmb_up"], past(R["vmb_up"], i + 1))
                if i:
                    pe.wait_ge(R["ss_add"], past(R["ss_add"], i))
                for q in range(2):
                    o = ps[:, 6 + q, :]
                    va, vb = (t[0:NS, 4 * q:4 * q + 4, :].rearrange("p b t -> p (b t)") for t in (VMa, VMb))
                    pe.matmul(o, Btt[0:NS, tl, :], va, start=True, stop=False)
                    mm = pe.matmul(o, Ktt[0:NS, tl, :], vb, start=False, stop=True)
                mm.then_inc(R["dss_mm"], 1)

        def rsample_act(act, g):
            for tl in range(4):
                i = 4 * g + tl
                rst_in(act, i)
                if i > 1:
                    act.wait_ge((R["so0"], R["so1"])[i % 2], past((R["so0"], R["so1"])[i % 2], 16 * (i // 2)))
                for par in range(2):
                    hp = slice(64 * par, 64 * par + 64)
                    cp = act.activation(SO[i % 2][hp, :, :], rst(i)[hp, :, hp], ACT.Copy)
                cp.then_inc(R["so_cp"], 1)
                act.wait_ge(R["wq_mm"], past(R["wq_mm"], i + 1))
                if i > 1:
                    act.wait_ge(R["ys_up"], past(R["ys_up"], i - 1))
                act.activation(wqr[i % 2][:, :, :], ps[:, tl % 2, 0:2 * NS].rearrange("p (x t) -> p x t", x=2),
                               ACT.Copy).then_inc(R["wq_cp"], 1)

        def rsample_dve(dve, g):
            dve.wait_ge(R["kt_mm"], past(R["kt_mm"], 8 + g + 2))
            dve.memset(SB1[:, :, :], 0.0).then_inc(R["sb_clr"], 1)
            def correct(tl):
                i = 4 * g + tl
                dve.wait_ge(R["wtr_mm"], past(R["wtr_mm"], i + 1))
                dve.wait_ge(R["u_cp"], past(R["u_cp"], 8 + g + 1))
                dve.tensor_tensor(Uu[0:NS, tl, :], Uu[0:NS, tl, :], ps[0:NS, 2 + tl % 2, 0:P], ALU.add).then_inc(R["sas_up"], 1)
            correct(0)
            for tl in range(4):
                i = 4 * g + tl
                dve.wait_ge(R["ys_mm"], past(R["ys_mm"], i + 1))
                dve.tensor_tensor(whole(RA)[:, i, TP:T], wqr[i % 2][:, 1, :], ps[:, 4, 0:NS], ALU.add).then_inc(R["ys_up"], 1)
                if i:
                    dve.wait_ge(R["dss_mm"], past(R["dss_mm"], i))
                dve.tensor_tensor(VMb[0:NS, :, :], Vt[0:NS, tl, :].unsqueeze(1).broadcast_to([NS, NB, P]),
                                  over(mseq[0:NS, :], P), ALU.mult).then_inc(R["vmb_up"], 1)
                if tl < 3:
                    correct(tl + 1)
                dve.wait_ge(R["dss_mm"], past(R["dss_mm"], i + 1))
                dve.wait_ge(R["so_cp"], past(R["so_cp"], i + 1))
                new = SO[i % 2]
                d = ps[:, 6:8, :].rearrange("p a (b t) -> p (a b) t", t=P)
                for par in range(2):
                    hp = slice(64 * par, 64 * par + 64)
                    q = dve.tensor_tensor(new[hp, :, :], new[hp, :, :], d[hp, :, hp], ALU.add)
                q.then_inc(R["ss_add"], 1)
                dve.wait_ge(R["ss_add"], past(R["ss_add"], i + 1))
                dve.tensor_tensor(new[:, :, :], new[:, :, :], over(ECE[:, i, 8:16], 64), ALU.mult).then_inc(R["ss_up"], 1)

        def rsample_pool(pool, g):
            for tl in range(4):
                i = 4 * g + tl
                pool.wait_ge(R["sas_up"], past(R["sas_up"], i + 1))
                if i:
                    pool.wait_ge(R["dss_mm"], past(R["dss_mm"], i))
                pool.tensor_tensor(VMa[0:NS, :, :], Uu[0:NS, tl, :].unsqueeze(1).broadcast_to([NS, NB, P]),
                                   over(mseq[0:NS, :], P), ALU.mult).then_inc(R["vm_up"], 1)

        def rpost_pe(pe):
            pe.wait_ge(R["ys_up"], past(R["ys_up"], NM))
            pe.wait_ge(R["ss_add"], past(R["ss_add"], NM))

            def mean(m):
                if m > 1:
                    pe.wait_ge(R["yc"], past(R["yc"], m - 1))
                for half in range(2):
                    mm = pe.matmul(pair(2 * (m % 2))[:, half, :], M["headones"], wh(RA, m)[:, half, :], start=True, stop=True)
                mm.then_inc(R["mu_mm"], 1)
            mean(0)
            for m in range(NM):
                if m + 1 < NM:
                    mean(m + 1)
                pe.wait_ge(R["ysq"], past(R["ysq"], m + 1))
                sum_rows(pe, pair(1), two_cols[:, 14 - 2 * m:30 - 2 * m], tb[m % 2], m == 0, m == NM - 1).then_inc(R["var_mm"], 1)
            pe.wait_ge(R["g2_in"], past(R["g2_in"], 16))
            pe.wait_ge(R["yc"], past(R["yc"], NM))
            for m in range(NM):
                if m > 1:
                    pe.wait_ge(R["gn3"], past(R["gn3"], m - 1))
                for half in range(2):
                    mm = pe.matmul(pair(2 + m % 2)[:, half, :], g2w[:, m * P:(m + 1) * P], lg[:, half, :], start=True, stop=True)
                mm.then_inc(R["g_mm"], 1)
                if m == 0:
                    pe.wait_ge(R["halves"], past(R["halves"], 2))
                    pe.wait_ge(R["gn_rs"], past(R["gn_rs"], 1))
                if m > 1:
                    pe.wait_ge(R["gn1"], past(R["gn1"], m - 1))
                spread_two_rows(pe, pair(m % 2), tb[2], m).then_inc(R["gn_bc"], 1)

        def rpost_act(act):
            for m in range(NM):
                act.wait_ge(R["yc"], past(R["yc"], m + 1))
                if m > 1:
                    act.wait_ge(R["var_mm"], past(R["var_mm"], m - 1))
                if m == 0:
                    act.wait_ge(R["ss_up"], past(R["ss_up"], NM))
                    act.wait_ge(R["ys_up"], past(R["ys_up"], NM))
                act.activation(tb[m % 2][:, :, :], wh(r_, m), ACT.Square).then_inc(R["ysq"], 1)
            act.wait_ge(R["var_mm"], past(R["var_mm"], NM))
            act.activation(tb[2][0:16, :, :], pair(1)[0:16], ACT.Sqrt, bias=gneps[0:16, 0:1], scale=1.0 / 64).then_inc(R["gn_rt"], 1)
            for m in range(NM):
                act.wait_ge(R["gn3"], past(R["gn3"], m + 1))
                act.activation(wh(xh, m), wh(r_, m), ACT.Copy).then_inc(x_hi, 1)

        def rpost_dve(dve):
            for m in range(NM):
                dve.wait_ge(R["mu_mm"], past(R["mu_mm"], m + 1))
                dve.scalar_tensor_tensor(wh(r_, m), pair(2 * (m % 2)), -1.0 / 64, wh(RA, m), ALU.mult, ALU.add).then_inc(R["yc"], 1)
            dve.wait_ge(R["gn_rt"], past(R["gn_rt"], 1))
            dve.reciprocal(tb[2][0:16, :, :], tb[2][0:16, :, :]).then_inc(R["gn_rs"], 1)
            for m in range(NM):
                y_ = wh(r_, m)
                dve.wait_ge(R["gn_bc"], past(R["gn_bc"], m + 1))
                dve.scalar_tensor_tensor(y_, y_, v(V_LNW + m), pair(m % 2), ALU.mult, ALU.mult).then_inc(R["gn1"], 1)
                dve.wait_ge(R["gn1"], past(R["gn1"], m + 1))
                dve.scalar_tensor_tensor(y_, y_, v(V_LNB + m), wh(BO, m), ALU.add, ALU.add).then_inc(R["gn2"], 1)
                dve.wait_ge(R["gn2"], past(R["gn2"], m + 1))
                dve.wait_ge(R["g_mm"], past(R["g_mm"], m + 1))
                dve.tensor_tensor(y_, y_, pair(2 + m % 2), ALU.mult).then_inc(R["gn3"], 1)
                if m >= 3:
                    wo_low(dve, m - 3)
            for m in range(NM - 3, NM):
                wo_low(dve, m)

        def wo_low(dve, m):
            dve.wait_ge(x_hi, 8 * SETS["wo"] + m + 1)
            dve.tensor_tensor(wh(xl, m), wh(r_, m), wh(xh, m).bitcast(F32), ALU.subtract).then_inc(x_lo, 1)

        def rwkv_pe(pe):
            norm_pe(pe, 8)
            for i, name in enumerate("rkv"):
                rkv_pe(pe, i, name)
            lora_pe(pe)
            prep_pe(pe)
            with pe.Fori(0, NCH) as c:
                for g in range(2):
                    rstep_pe(pe, 2 * c + g, c, g, P)
            for g in range(2):
                rstep_pe(pe, 8 + g, None, g, NS, smp=g)
                rsample_pe(pe, g)
            rpost_pe(pe)
            out_pe(pe, "wo", 9, 8 * SETS["wo"])
            norm_pe(pe, 9)

        def rwkv_act(act):
            pre_norm_act(act, 8, None)
            for i, (name, dst) in enumerate((("r", r_), ("k", k_), ("v", v_))):
                if i == 0:
                    act.wait_ge(R["sh_out"], past(R["sh_out"], 16))
                rkv_act(act, i, name, dst)
            lora_act(act)
            prep_act(act)
            with act.Fori(0, NCH) as c:
                for g in range(2):
                    rstep_act(act, 2 * c + g, c, g, P)
            for g in range(2):
                rstep_act(act, 8 + g, None, g, NS, smp=g)
                rsample_act(act, g)
            rpost_act(act)
            out_act(act, "wo", 1, 9, y=y2)
            norm_act(act, 9)

        def rwkv_dve(dve):
            shift_dve(dve)
            for i in range(6):
                mix_dve(dve, i)
            prep_dve(dve)
            dve.wait_ge(R["sg_cp"], past(R["sg_cp"], 2 * NM))
            dve.wait_ge(R["ece"], past(R["ece"], NM))
            dve.memset(RS[:, :, :], 0.0).then_inc(R["s_up"], 1)
            dve.memset(Ktt[:, :, :], 0.0).then_inc(R["y_cp"], 1)
            dve.memset(Btt[:, :, :], 0.0).then_inc(R["kt_mm"], 1)
            with dve.Fori(0, NCH) as c:
                for g in range(2):
                    rstep_dve(dve, 2 * c + g, c, g, P)
            for g in range(2):
                rstep_dve(dve, 8 + g, None, g, NS, smp=g)
                rsample_dve(dve, g)
            rpost_dve(dve)
            out_dve(dve, "wo", 1, 9)
            post_norm_dve(dve, 9, 1.0, SETS["ffn3_in"], y=y2)

        def rwkv_pool(pool):
            add_squares_pool(pool, 8)
            pool_units(pool, "r")
            pool_units(pool, "k")
            pool_units(pool, "v")
            lora_pool(pool)
            prep_pool(pool)
            with pool.Fori(0, NCH) as c:
                for g in range(2):
                    rstep_pool(pool, 2 * c + g, c, g, P)
            for g in range(2):
                rstep_pool(pool, 8 + g, None, g, NS, smp=g)
                rsample_pool(pool, g)
            pool.wait_ge(R["ss_up"], past(R["ss_up"], NM))
            pool.wait_ge(R["ys_up"], past(R["ys_up"], NM))
            make_halves(pool)
            pool_units(pool, "wo")

        def rwkv_sp(sp):
            load_units(sp, "r", part=0)
            sp.wait_ge(acc, 2 * BASE["r"])
            sp.dma_start(shin[:, :, :], a["shift"]).then_inc(R["sh_in"], 16)
            sp.dma_start(wa2[:, :], a["wa2"]).then_inc(R["w2_in"], 16)
            sp.wait_ge(R["sh_cp"], past(R["sh_cp"], 1))
            sp.dma_start(a["shift_new"], shout[:, :, :]).then_inc(R["sh_out"], 16)
            load_units(sp, "r", part=1)
            load_units(sp, "k")
            load_units(sp, "v")
            load_units(sp, "lora")
            sp.wait_ge(R["mix"], past(R["mix"], 48))
            sp.wait_ge(x_lo, 8 * SETS["wo"])
            sp.dma_start(reset[:, :], a["reset"]).then_inc(R["rm_in"], 16)
            load_units(sp, "wo", part=0)
            rsample_sp(sp)
            sp.dma_start(g2w[:, :], a["g2"]).then_inc(R["g2_in"], 16)
            load_units(sp, "wo", part=1)

        block = es.enter_context(nc.Block())

        def consts(e):
            e.wait_ge(const_in, 16 * 7)

        @block.sync
        def _(sp):
            for t, n in ((vec, "vec"), (mf, "mf"), (mseq, "mseq"), (mg_f, "mg")):
                sp.dma_start(t[:], a[n]).then_inc(const_in, 16)
            sp.dma_start(h[:, :, :], a["xT"]).then_inc(const_in, 16)
            load_units(sp, "ffn0_in")
            load_units(sp, "ffn0_out")
            gdn_sp(sp)
            load_units(sp, "ffn1_in")
            load_units(sp, "ffn1_out")
            load_units(sp, "ffn2_in")
            load_units(sp, "ffn2_out")
            rwkv_sp(sp)
            load_units(sp, "ffn3_in")
            load_units(sp, "ffn3_out")
            sp.wait_ge(R["so0"], past(R["so0"], 64))
            sp.wait_ge(R["so1"], past(R["so1"], 64))
            sp.wait_ge(h_upd, 8 * 6)
            sp.dma_start(a["yT"], h[:, :, :]).then_inc(out_done, 16)
            sp.wait_ge(out_done, 16)
            sp.wait_ge(S["st_out0"], 64)
            sp.wait_ge(S["st_out1"], 64)

        @block.gpsimd
        def _(pool):
            pool.memset(gneps[:], GN_EPS)
            pool.memset(eps[:], EPS).then_inc(const_in, 16)
            pool.wait_ge(const_in, 96)
            pool.tensor_copy(mg[:], mg_f[:]).then_inc(const_in, 16)
            pool.wait_ge(const_in, 112)
            pool_units(pool, "ffn0_in", 0)
            pool_units(pool, "ffn0_out")
            gdn_pool(pool)
            for f in (1, 2):
                pool_units(pool, f"ffn{f}_in", FFN_NORM[f])
                pool_units(pool, f"ffn{f}_out")
            rwkv_pool(pool)
            pool_units(pool, "ffn3_in", 10)
            pool_units(pool, "ffn3_out")

        def pre_ffn_act(act, f):
            for j in range(2):
                split_hi(act, f"ffn{f}_in", 0, j)
            pre_norm_act(act, FFN_NORM[f], SETS[f"ffn{f}_in"])

        @block.scalar
        def _(act):
            split_hi(act, "ffn0_in", 0, 0)
            split_hi(act, "ffn0_in", 0, 1)
            consts(act)
            pre_norm_act(act, 0, SETS["ffn0_in"])
            ffn_act(act, 0)
            norm_act(act, 1)
            gdn_act(act)
            pre_ffn_act(act, 1)
            ffn_act(act, 1)
            norm_act(act, 5)
            pre_ffn_act(act, 2)
            ffn_act(act, 2)
            norm_act(act, 7)
            rwkv_act(act)
            pre_ffn_act(act, 3)
            ffn_act(act, 3)
            norm_act(act, 11)

        @block.vector
        def _(dve):
            consts(dve)
            for m in range(NM):
                pre_norm_low(dve, 0, SETS["ffn0_in"], m)
            ffn_dve(dve, 0)
            post_norm_dve(dve, 1, 0.5, SETS["gdn_in"])
            gdn_dve(dve)
            ffn_dve(dve, 1)
            post_norm_dve(dve, 5, 0.5, SETS["ffn2_in"])
            ffn_dve(dve, 2)
            post_norm_dve(dve, 7, 0.5)
            rwkv_dve(dve)
            ffn_dve(dve, 3)
            post_norm_dve(dve, 11, 0.5)

        @block.tensor
        def _(pe):
            ffn_pe(pe, 0)
            norm_pe(pe, 1)
            gdn_pe(pe)
            for f in (1, 2):
                ffn_pe(pe, f)
                norm_pe(pe, FFN_NORM[f] + 1)
            rwkv_pe(pe)
            ffn_pe(pe, 3)
            norm_pe(pe, 11)


def lay_out(inp):
    f = lambda x: np.asarray(x)
    x = np.concatenate([f(inp["x_prompt"]).reshape(TP, D), f(inp["x_sample"]).reshape(NS, D)])
    o = {"xT": x.T.reshape(NM, P, 2, HALF).transpose(1, 0, 2, 3).reshape(P, 2 * NM, HALF)}

    def units(w):
        k, n = w.shape
        return w.reshape(k // P, P, n // P, P).transpose(2, 1, 0, 3).reshape(n // P, P, k // P * P)

    def tiles(vv):
        return f(vv).reshape(-1, P).T

    win, wout = f(inp["ffn_w_in"]), f(inp["ffn_w_out"])
    w8, w11 = [], []
    ffn_in, ffn_out = [], []
    for i in range(4):
        gu = units(win[i // 2, i % 2])
        ffn_in.append(np.stack([gu[:NF], gu[NF:]], 1).reshape(2 * NF, P, D))
        w = wout[i // 2, i % 2].reshape(2, KTO, P, NM, P).transpose(3, 0, 2, 1, 4)
        ffn_out.append(w.reshape(2 * NM, P, KTO * P))
    gin = f(inp["gdn_w_in"])[0]
    rkv = np.concatenate([units(f(inp["rwkv_w_rkv"])[0, i]) for i in range(3)])
    wa1 = np.concatenate([f(inp["rwkv_w1"])[0], f(inp["rwkv_a1"])[0]], 1)
    lora = np.concatenate([units(wa1), units(wa1), units(f(inp["rwkv_g1"])[0])])
    ba = np.concatenate([gin[:, 4096:], np.zeros((D, P - 2 * HG), np.float32)], 1)
    o["w8"] = np.concatenate([ffn_in[0], units(gin[:, :4096]), units(ba), units(f(inp["gdn_w_out"])[0]), ffn_in[1],
                              ffn_in[2], rkv, lora, units(f(inp["rwkv_w_o"])[0]), ffn_in[3]])
    o["w11"] = np.concatenate(ffn_out)
    cw = f(inp["gdn_conv_w"])[0].reshape(4, NQKV, P).transpose(2, 1, 0).reshape(P, NQKV * 4)
    rows = [tiles(inp["norm_g"]), cw, f(inp["gdn_o_norm"])[0].reshape(P, 1), tiles(inp["rwkv_lerp"])]
    rows += [tiles(inp[n]) for n in ("rwkv_w0", "rwkv_a0", "rwkv_k_k", "rwkv_k_a", "rwkv_r_k", "rwkv_ln_w", "rwkv_ln_b")]
    rows += [np.repeat(f(inp["gdn_a_log"]).reshape(1, HG), P, 0), np.repeat(f(inp["gdn_dt_bias"]).reshape(1, HG), P, 0)]
    o["vec"] = np.concatenate(rows, 1)
    o["mf"], o["mg"] = MF, MG
    o["mseq"] = MSEQ
    hist = f(inp["state_gdn_conv"])[0].reshape(NB, 3, NQKV, P).transpose(3, 2, 0, 1)
    o["conv_hist"] = hist.reshape(P, NQKV, NB * 3)
    w2a2 = np.concatenate([f(inp["rwkv_w2"])[0], f(inp["rwkv_a2"])[0]])
    o["wa2"], o["g2"] = w2a2, f(inp["rwkv_g2"])[0]
    o["shift"] = f(inp["state_rwkv_shift"])[0].reshape(NB, NM, P).transpose(2, 1, 0)
    o["state_rwkv"] = f(inp["state_rwkv"])[0].reshape(NB, NM, 2, 64, 64).transpose(1, 2, 4, 0, 3).reshape(NM, P, NB, 64)
    o["reset"] = RESET
    o["state_gdn"] = f(inp["state_gdn"])[0].transpose(1, 2, 0, 3)
    return o


_OUTS = {"yT": (P, 2 * NM, HALF), "gdn_s_p": (P, HG, P), "gdn_s_s": (HG, P, NB, P), "conv_new": (P, NQKV, 3 + NB * 3),
         "rwkv_s_p": (P, NM, 64), "rwkv_s_s": (NM, P, NB, 64), "shift_new": (P, NM, 1 + NB)}


def kernel(**inputs):
    import concourse.bacc as bacc
    from concourse.bass_utils import run_bass_kernel_spmd

    nc = bacc.Bacc("TRN2", target_bir_lowering=False, num_devices=1)
    arrays = {n: np.ascontiguousarray(x) for n, x in lay_out(inputs).items()}
    a = {n: nc.dram_tensor(n, x.shape, F32, kind="ExternalInput").ap() for n, x in arrays.items()}
    a.update({n: nc.dram_tensor(n, s, F32, kind="ExternalOutput").ap() for n, s in _OUTS.items()})
    trunk_kernel(nc, a)
    r = run_bass_kernel_spmd(nc, [arrays], core_ids=[0]).results[0]
    y = np.asarray(r["yT"]).reshape(P, NM, T).transpose(2, 1, 0).reshape(T, D)
    cn = np.asarray(r["conv_new"]).transpose(2, 1, 0).reshape(3 + NB * 3, NQKV * P)
    sh = np.asarray(r["shift_new"]).transpose(2, 1, 0).reshape(1 + NB, D)
    rp = np.asarray(r["rwkv_s_p"]).reshape(2, 64, NM, 64).transpose(2, 0, 3, 1).reshape(1, 1, 2 * NM, 64, 64)
    rsm = np.asarray(r["rwkv_s_s"]).reshape(NM, 2, 64, NB, 64).transpose(3, 0, 1, 4, 2).reshape(1, NB, 2 * NM, 64, 64)
    c = np.ascontiguousarray
    return (c(y[:TP].reshape(1, TP, D)), c(y[TP:].reshape(NB, TS, D)),
            c(np.asarray(r["gdn_s_p"]).transpose(1, 0, 2)[None, None]), c(cn[:3][None, None]), c(rp), c(sh[:1][None]),
            c(np.asarray(r["gdn_s_s"]).transpose(2, 0, 1, 3)[None]), c(cn[3:].reshape(1, NB, 3, NQKV * P)), c(rsm),
            c(sh[1:][None]))
```
